# Optimizing a Trainium2 kernel written in Bass

```python
import jax, jax.numpy as jnp
from jax import lax
import numpy as np

D_MODEL = 1024
BATCH = 1
SEQ = 256
DEPTH = 1

GRID_W = 64
CTX_LEN = 256
N_Q_HEADS = 8
N_KV_HEADS = 2
HEAD_DIM = 64
GROUP = N_Q_HEADS // N_KV_HEADS
ATTN_DIM = N_Q_HEADS * HEAD_DIM
KV_DIM = N_KV_HEADS * HEAD_DIM
CONV_DIM = D_MODEL - ATTN_DIM
MIX_DIM = ATTN_DIM + CONV_DIM
CONV_K = 3
OFF_K = ATTN_DIM
OFF_V = OFF_K + KV_DIM
OFF_B = OFF_V + KV_DIM
OFF_C = OFF_B + CONV_DIM
OFF_U = OFF_C + CONV_DIM
MIX_IN_DIM = OFF_U + CONV_DIM
D_FF = 2816
N_MOD = 9
ROPE_THETA = 10000.0
Q_BLOCK = 128
ATTN_SCALE = HEAD_DIM ** -0.5
EPS = 1e-6


def rmsnorm(x, g):
    x32 = x.astype(jnp.float32)
    y = x32 * lax.rsqrt(jnp.mean(x32 * x32, axis=-1, keepdims=True) + EPS)
    return (y * g.astype(jnp.float32)).astype(x.dtype)

def modulate(h, shift, scale):
    return h * (1 + scale) + shift

def swiglu(h, w_in, w_out):
    gate, up = jnp.split(h @ w_in, 2, axis=-1)
    return (jax.nn.silu(gate) * up) @ w_out

def axial_rope_tables(n_tokens):
    rows = n_tokens // GRID_W
    row = jnp.repeat(jnp.arange(rows, dtype=jnp.float32), GRID_W)
    col = jnp.tile(jnp.arange(GRID_W, dtype=jnp.float32), rows)
    n_freq = HEAD_DIM // 4
    inv = ROPE_THETA ** (-jnp.arange(n_freq, dtype=jnp.float32) / n_freq)
    ang = jnp.concatenate([row[:, None] * inv, col[:, None] * inv], axis=-1)
    return jnp.cos(ang)[:, None, :], jnp.sin(ang)[:, None, :]

def apply_rope(x, cos, sin):
    xr = x.astype(jnp.float32).reshape(x.shape[:-1] + (HEAD_DIM // 2, 2))
    x0, x1 = xr[..., 0], xr[..., 1]
    out = jnp.stack([x0 * cos - x1 * sin, x0 * sin + x1 * cos], axis=-1)
    return out.reshape(x.shape).astype(x.dtype)

def gqa_softmax(q, k, v):
    s = jnp.einsum('bqkgd,bskd->bkgqs', q, k, preferred_element_type=jnp.float32) * ATTN_SCALE
    p = jax.nn.softmax(s, axis=-1).astype(v.dtype)
    return jnp.einsum('bkgqs,bskd->bqkgd', p, v)

def latent_attention(q, k, v, kc, vc):
    b, s = q.shape[:2]
    nb = s // Q_BLOCK
    k_all = jnp.concatenate([kc, k], axis=1)
    v_all = jnp.concatenate([vc, v], axis=1)
    qb = q.reshape(b, nb, Q_BLOCK, N_KV_HEADS, GROUP, HEAD_DIM).transpose(1, 0, 2, 3, 4, 5)
    o = lax.map(lambda qi: gqa_softmax(qi, k_all, v_all), qb)
    return o.transpose(1, 0, 2, 3, 4, 5).reshape(b, s, ATTN_DIM)

def context_attention(q, kc, vc):
    b, l = q.shape[:2]
    o = gqa_softmax(q.reshape(b, l, N_KV_HEADS, GROUP, HEAD_DIM), kc, vc)
    return o.reshape(b, l, ATTN_DIM)

def short_conv3(u, w):
    up = jnp.pad(u, ((0, 0), (1, 1), (0, 0)))
    return up[:, :-2] * w[0] + up[:, 1:-1] * w[1] + up[:, 2:] * w[2]

def split_heads(p, q_norm, k_norm):
    b, l = p.shape[:2]
    q = rmsnorm(p[..., :OFF_K].reshape(b, l, N_Q_HEADS, HEAD_DIM), q_norm)
    k = rmsnorm(p[..., OFF_K:OFF_V].reshape(b, l, N_KV_HEADS, HEAD_DIM), k_norm)
    v = p[..., OFF_V:OFF_B].reshape(b, l, N_KV_HEADS, HEAD_DIM)
    gb, gc, u = p[..., OFF_B:OFF_C], p[..., OFF_C:OFF_U], p[..., OFF_U:]
    return q, k, v, gb, gc, u

def first_inputs(seed: int = 0) -> dict:
    key = jax.random.key(seed)
    ks = jax.random.split(key, 24)
    f32 = jnp.float32
    nrm = lambda k, shape, s: jax.random.normal(k, shape, f32) * s
    gain = lambda k, shape: 1.0 + 0.05 * jax.random.normal(k, shape, f32)
    return {
        "x": nrm(ks[0], (BATCH, SEQ, D_MODEL), 1.0),
        "c": nrm(ks[1], (BATCH, D_MODEL), 1.0),
        "ctx": nrm(ks[2], (BATCH, CTX_LEN, D_MODEL), 1.0),
        "c_ctx": nrm(ks[3], (D_MODEL,), 1.0),
        "w_ada": nrm(ks[4], (DEPTH, D_MODEL, N_MOD * D_MODEL), 0.5 * D_MODEL ** -0.5),
        "b_ada": nrm(ks[5], (DEPTH, N_MOD * D_MODEL), 0.02),
        "norm_ffn1": gain(ks[6], (DEPTH, D_MODEL)),
        "w_ffn1_in": nrm(ks[7], (DEPTH, D_MODEL, 2 * D_FF), D_MODEL ** -0.5),
        "w_ffn1_out": nrm(ks[8], (DEPTH, D_FF, D_MODEL), D_FF ** -0.5),
        "norm_mix": gain(ks[9], (DEPTH, D_MODEL)),
        "w_mix_in": nrm(ks[10], (DEPTH, D_MODEL, MIX_IN_DIM), D_MODEL ** -0.5),
        "q_norm": gain(ks[11], (DEPTH, HEAD_DIM)),
        "k_norm": gain(ks[12], (DEPTH, HEAD_DIM)),
        "conv_w": nrm(ks[13], (DEPTH, CONV_K, CONV_DIM), CONV_K ** -0.5),
        "attn_out_norm": gain(ks[14], (DEPTH, ATTN_DIM)),
        "conv_out_norm": gain(ks[15], (DEPTH, CONV_DIM)),
        "w_mix_out": nrm(ks[16], (DEPTH, MIX_DIM, D_MODEL), MIX_DIM ** -0.5),
        "norm_ffn2": gain(ks[17], (DEPTH, D_MODEL)),
        "w_ffn2_in": nrm(ks[18], (DEPTH, D_MODEL, 2 * D_FF), D_MODEL ** -0.5),
        "w_ffn2_out": nrm(ks[19], (DEPTH, D_FF, D_MODEL), D_FF ** -0.5),
        "final_norm": gain(ks[20], (D_MODEL,)),
    }

def first_block(x, c, ctx, c_ctx, w_ada, b_ada, norm_ffn1, w_ffn1_in, w_ffn1_out,
              norm_mix, w_mix_in, q_norm, k_norm, conv_w, attn_out_norm, conv_out_norm,
              w_mix_out, norm_ffn2, w_ffn2_in, w_ffn2_out, final_norm):
    b, s, d = x.shape
    cos, sin = axial_rope_tables(s)

    for l in range(DEPTH):
        update_ctx = l < DEPTH - 1
        m = (jax.nn.silu(c) @ w_ada[l] + b_ada[l]).reshape(b, 1, N_MOD, d)
        mc = (jax.nn.silu(c_ctx) @ w_ada[l] + b_ada[l]).reshape(1, 1, N_MOD, d)

        x = x + 0.5 * m[:, :, 2] * swiglu(modulate(rmsnorm(x, norm_ffn1[l]), m[:, :, 0], m[:, :, 1]),
                                          w_ffn1_in[l], w_ffn1_out[l])
        ctx = ctx + 0.5 * mc[:, :, 2] * swiglu(modulate(rmsnorm(ctx, norm_ffn1[l]), mc[:, :, 0], mc[:, :, 1]),
                                               w_ffn1_in[l], w_ffn1_out[l])

        px = modulate(rmsnorm(x, norm_mix[l]), m[:, :, 3], m[:, :, 4]) @ w_mix_in[l]
        pc = modulate(rmsnorm(ctx, norm_mix[l]), mc[:, :, 3], mc[:, :, 4]) @ w_mix_in[l]
        q, k, v, gb, gc, u = split_heads(px, q_norm[l], k_norm[l])
        qc, kc, vc, gbc, gcc, uc = split_heads(pc, q_norm[l], k_norm[l])

        a = latent_attention(apply_rope(q, cos, sin), apply_rope(k, cos, sin), v, kc, vc)
        sc = gb * short_conv3(gc * u, conv_w[l])
        mix = jnp.concatenate([rmsnorm(a, attn_out_norm[l]), rmsnorm(sc, conv_out_norm[l])], axis=-1)
        x = x + m[:, :, 5] * (mix @ w_mix_out[l])

        if update_ctx:
            ac = context_attention(qc, kc, vc)
            scc = gbc * short_conv3(gcc * uc, conv_w[l])
            mixc = jnp.concatenate([rmsnorm(ac, attn_out_norm[l]), rmsnorm(scc, conv_out_norm[l])], axis=-1)
            ctx = ctx + mc[:, :, 5] * (mixc @ w_mix_out[l])
            ctx = ctx + 0.5 * mc[:, :, 8] * swiglu(modulate(rmsnorm(ctx, norm_ffn2[l]), mc[:, :, 6], mc[:, :, 7]),
                                                   w_ffn2_in[l], w_ffn2_out[l])

        x = x + 0.5 * m[:, :, 8] * swiglu(modulate(rmsnorm(x, norm_ffn2[l]), m[:, :, 6], m[:, :, 7]),
                                          w_ffn2_in[l], w_ffn2_out[l])

    return rmsnorm(x, final_norm)


A_GROUPS = 4
A_GROUP_DIM = 128
A_WIDTH = A_GROUPS * A_GROUP_DIM
CHUNK = 128
N_HEADS = 4
HEAD_DIM_2 = 128
B_WIDTH = N_HEADS * HEAD_DIM_2
KV_LATENT = 256
ROT_DIM = HEAD_DIM_2 // 4
IDX_HEADS = 4
IDX_DIM = 64
IDX_ROT = IDX_DIM // 4
TOPK_MAX = 256
ROPE_THETA_2 = 500000.0
N_BRANCHES = 2
PEER_HEADS = 8
PEER_KEY_DIM = 256
PEER_HALF = PEER_KEY_DIM // 2
N_KEYS = 128
N_EXPERTS = N_KEYS * N_KEYS
PEER_TOPK = 16
PEER_BLOCK = 128

SPLITS = (A_WIDTH, A_WIDTH, B_WIDTH, KV_LATENT, IDX_HEADS * IDX_DIM, IDX_DIM, IDX_HEADS, N_BRANCHES * D_MODEL)
IN_WIDTH = sum(SPLITS)
SPLIT_OFFSETS = tuple(int(o) for o in np.cumsum(SPLITS)[:-1])


def rms_norm(x, g):
    xf = x.astype(jnp.float32)
    y = xf * lax.rsqrt(jnp.mean(xf * xf, axis=-1, keepdims=True) + EPS)
    return (y * g.astype(jnp.float32)).astype(x.dtype)

def layer_norm(x, g, b):
    xf = x.astype(jnp.float32)
    mu = jnp.mean(xf, axis=-1, keepdims=True)
    xc = xf - mu
    y = xc * lax.rsqrt(jnp.mean(xc * xc, axis=-1, keepdims=True) + EPS)
    return (y * g.astype(jnp.float32) + b.astype(jnp.float32)).astype(x.dtype)

def partial_rope(x, pos, rot_dim):
    half = rot_dim // 2
    inv = jnp.power(jnp.float32(ROPE_THETA_2), -jnp.arange(half, dtype=jnp.float32) * 2.0 / rot_dim)
    ang = pos.astype(jnp.float32)[..., None] * inv
    cos = jnp.cos(ang)[:, :, None, :]
    sin = jnp.sin(ang)[:, :, None, :]
    xr = x[..., :rot_dim].astype(jnp.float32)
    x1, x2 = xr[..., :half], xr[..., half:]
    rot = jnp.concatenate([x1 * cos - x2 * sin, x2 * cos + x1 * sin], axis=-1)
    return jnp.concatenate([rot.astype(x.dtype), x[..., rot_dim:]], axis=-1)

def chunked_spatial_gating(u, v, v_g, v_b, w_s, b_s):
    bsz, s, _ = u.shape
    u = jax.nn.gelu(u)
    v = layer_norm(jax.nn.gelu(v), v_g, v_b)
    v = v.reshape(bsz, s // CHUNK, CHUNK, A_GROUPS, A_GROUP_DIM)
    causal = jnp.tril(jnp.ones((CHUNK, CHUNK), dtype=bool))
    w = jnp.where(causal[None], w_s, jnp.zeros_like(w_s))
    z = jnp.einsum('gts,bcsgd->bctgd', w, v) + b_s.T[None, None, :, :, None]
    return u * z.reshape(bsz, s, A_WIDTH)

def dsa_attention(q, k, v, q_idx, k_idx, w_idx):
    bsz, s = q.shape[:2]
    n_sel = min(TOPK_MAX, s // 4)
    nblk = s // Q_BLOCK
    key_pos = jnp.arange(s)

    def to_blocks(a):
        return a.reshape(bsz, nblk, Q_BLOCK, *a.shape[2:]).swapaxes(0, 1)

    def gather_rows(table, idx):
        return table[idx]

    def block_fn(args):
        blk, qb, qib, wib = args
        q_pos = blk * Q_BLOCK + jnp.arange(Q_BLOCK)
        causal = key_pos[None, :] <= q_pos[:, None]
        logits = jnp.einsum('bqhd,bsd->bqhs', qib, k_idx, preferred_element_type=jnp.float32) * (IDX_DIM ** -0.5)
        scores = jnp.einsum('bqh,bqhs->bqs', wib.astype(jnp.float32), jax.nn.relu(logits))
        scores = jnp.where(causal[None], scores, -jnp.inf)
        _, idx = lax.top_k(scores, n_sel)
        valid = idx <= q_pos[None, :, None]
        k_sel = jax.vmap(gather_rows)(k, idx)
        v_sel = jax.vmap(gather_rows)(v, idx)
        att = jnp.einsum('bqhd,bqnd->bqhn', qb, k_sel, preferred_element_type=jnp.float32) * (HEAD_DIM_2 ** -0.5)
        att = jnp.where(valid[:, :, None, :], att, jnp.float32(-1e30))
        p = jax.nn.softmax(att, axis=-1).astype(v.dtype)
        return jnp.einsum('bqhn,bqnd->bqhd', p, v_sel)

    out = lax.map(block_fn, (jnp.arange(nblk), to_blocks(q), to_blocks(q_idx), to_blocks(w_idx)))
    return out.swapaxes(0, 1).reshape(bsz, s, B_WIDTH)

def peer(xn, wq, subkeys, u_tab, v_tab):
    bsz, s, d = xn.shape
    q = (xn @ wq).reshape(bsz, s, PEER_HEADS, 2, PEER_HALF)
    sub = jnp.einsum('bshpd,hpnd->bshpn', q, subkeys, preferred_element_type=jnp.float32)
    s_top, i_top = lax.top_k(sub, PEER_TOPK)
    cand = (s_top[..., 0, :, None] + s_top[..., 1, None, :]).reshape(bsz, s, PEER_HEADS, PEER_TOPK * PEER_TOPK)
    cand_idx = (i_top[..., 0, :, None] * N_KEYS + i_top[..., 1, None, :]).reshape(bsz, s, PEER_HEADS, PEER_TOPK * PEER_TOPK)
    best, pos = lax.top_k(cand, PEER_TOPK)
    expert = jnp.take_along_axis(cand_idx, pos, axis=-1)
    gate = jax.nn.softmax(best, axis=-1)
    nb = (bsz * s) // PEER_BLOCK
    hk = PEER_HEADS * PEER_TOPK
    xt = xn.reshape(nb, PEER_BLOCK, d)
    et = expert.reshape(nb, PEER_BLOCK, hk)
    gt = gate.reshape(nb, PEER_BLOCK, hk)

    def blk(args):
        xb, eb, gb = args
        ub = u_tab[eb]
        vb = v_tab[eb]
        a = jax.nn.gelu(jnp.einsum('td,ted->te', xb, ub, preferred_element_type=jnp.float32))
        return jnp.einsum('te,ted->td', (gb * a).astype(vb.dtype), vb)

    y = lax.map(blk, (xt, et, gt))
    return y.reshape(bsz, s, d)

def second_inputs(seed: int = 0) -> dict:
    key = jax.random.key(seed)
    ks = jax.random.split(key, 24)
    f32 = jnp.float32
    L = DEPTH
    nrm = lambda k, shape, scale: jax.random.normal(k, shape, f32) * scale
    x = jax.random.normal(ks[0], (BATCH, SEQ, D_MODEL), f32)
    positions = jnp.broadcast_to(jnp.arange(SEQ, dtype=jnp.int32)[None, :], (BATCH, SEQ))
    return {
        "x": x,
        "positions": positions,
        "norm1_g": 1.0 + nrm(ks[1], (L, D_MODEL), 0.02),
        "w_in": nrm(ks[2], (L, D_MODEL, IN_WIDTH), D_MODEL ** -0.5),
        "v_norm_g": 1.0 + nrm(ks[3], (L, A_WIDTH), 0.02),
        "v_norm_b": nrm(ks[4], (L, A_WIDTH), 0.02),
        "spatial_w": nrm(ks[5], (L, A_GROUPS, CHUNK, CHUNK), CHUNK ** -0.5),
        "spatial_b": 1.0 + nrm(ks[6], (L, A_GROUPS, CHUNK), 0.1),
        "kv_norm_g": 1.0 + nrm(ks[7], (L, KV_LATENT), 0.02),
        "w_uk": nrm(ks[8], (L, KV_LATENT, HEAD_DIM_2), KV_LATENT ** -0.5),
        "w_uv": nrm(ks[9], (L, KV_LATENT, HEAD_DIM_2), KV_LATENT ** -0.5),
        "q_norm_g": 1.0 + nrm(ks[10], (L, HEAD_DIM_2), 0.02),
        "k_norm_g": 1.0 + nrm(ks[11], (L, HEAD_DIM_2), 0.02),
        "w_a_out": nrm(ks[12], (L, A_WIDTH, D_MODEL), A_WIDTH ** -0.5),
        "w_b_out": nrm(ks[13], (L, B_WIDTH, D_MODEL), B_WIDTH ** -0.5),
        "w_o": nrm(ks[14], (L, D_MODEL, D_MODEL), D_MODEL ** -0.5),
        "norm2_g": 1.0 + nrm(ks[15], (L, D_MODEL), 0.02),
        "peer_wq": nrm(ks[16], (L, D_MODEL, PEER_HEADS * PEER_KEY_DIM), D_MODEL ** -0.5),
        "peer_subkeys": nrm(ks[17], (L, PEER_HEADS, 2, N_KEYS, PEER_HALF), PEER_HALF ** -0.5),
        "peer_u": nrm(ks[18], (L, N_EXPERTS, D_MODEL), D_MODEL ** -0.5),
        "peer_v": nrm(ks[19], (L, N_EXPERTS, D_MODEL), 0.5 * PEER_HEADS ** -0.5),
    }

def second_block(x, positions, norm1_g, w_in, v_norm_g, v_norm_b, spatial_w, spatial_b, kv_norm_g, w_uk, w_uv,
              q_norm_g, k_norm_g, w_a_out, w_b_out, w_o, norm2_g, peer_wq, peer_subkeys, peer_u, peer_v):
    bsz, s, d = x.shape
    h = x
    for l in range(DEPTH):
        xn = rms_norm(h, norm1_g[l])
        proj = xn @ w_in[l]
        u, v, q, c_kv, q_idx, k_idx, w_idx, gates = jnp.split(proj, SPLIT_OFFSETS, axis=-1)

        y_a = chunked_spatial_gating(u, v, v_norm_g[l], v_norm_b[l], spatial_w[l], spatial_b[l])

        c_n = rms_norm(c_kv, kv_norm_g[l])
        k = rms_norm(c_n @ w_uk[l], k_norm_g[l])
        vv = c_n @ w_uv[l]
        qh = rms_norm(q.reshape(bsz, s, N_HEADS, HEAD_DIM_2), q_norm_g[l])
        qh = partial_rope(qh, positions, ROT_DIM)
        k = partial_rope(k[:, :, None, :], positions, ROT_DIM)[:, :, 0, :]
        qi = partial_rope(q_idx.reshape(bsz, s, IDX_HEADS, IDX_DIM), positions, IDX_ROT)
        ki = partial_rope(k_idx[:, :, None, :], positions, IDX_ROT)[:, :, 0, :]
        wi = w_idx * (IDX_HEADS ** -0.5)
        y_b = dsa_attention(qh, k, vv, qi, ki, wi)

        g = jax.nn.sigmoid(gates.reshape(bsz, s, N_BRANCHES, d))
        merged = g[:, :, 0, :] * (y_a @ w_a_out[l]) + g[:, :, 1, :] * (y_b @ w_b_out[l])
        h = h + merged @ w_o[l]

        hn = rms_norm(h, norm2_g[l])
        h = h + peer(hn, peer_wq[l], peer_subkeys[l], peer_u[l], peer_v[l])
    return h


def setup_inputs(seed=0):
    out = dict(first_inputs(seed))
    for name, value in second_inputs(seed + 1).items():
        if name != "x":
            out[name + "_2"] = value
    return out


def reference(
    x, c, ctx, c_ctx, w_ada, b_ada, norm_ffn1, w_ffn1_in, w_ffn1_out, norm_mix, w_mix_in,
    q_norm, k_norm, conv_w, attn_out_norm, conv_out_norm, w_mix_out, norm_ffn2, w_ffn2_in,
    w_ffn2_out, final_norm, positions_2, norm1_g_2, w_in_2, v_norm_g_2, v_norm_b_2, spatial_w_2,
    spatial_b_2, kv_norm_g_2, w_uk_2, w_uv_2, q_norm_g_2, k_norm_g_2, w_a_out_2, w_b_out_2,
    w_o_2, norm2_g_2, peer_wq_2, peer_subkeys_2, peer_u_2, peer_v_2,
):
    x = first_block(
        x, c, ctx, c_ctx, w_ada, b_ada, norm_ffn1, w_ffn1_in, w_ffn1_out, norm_mix, w_mix_in,
        q_norm, k_norm, conv_w, attn_out_norm, conv_out_norm, w_mix_out, norm_ffn2, w_ffn2_in,
        w_ffn2_out, final_norm,
    )
    return second_block(
        x, positions_2, norm1_g_2, w_in_2, v_norm_g_2, v_norm_b_2, spatial_w_2, spatial_b_2,
        kv_norm_g_2, w_uk_2, w_uv_2, q_norm_g_2, k_norm_g_2, w_a_out_2, w_b_out_2, w_o_2,
        norm2_g_2, peer_wq_2, peer_subkeys_2, peer_u_2, peer_v_2,
    )


_drawn_inputs = setup_inputs


def setup_inputs(seed=0):
    import zlib

    import numpy as np

    out = dict(_drawn_inputs(seed))
    spreads = {}
    factors = {'norm_ffn1': 3.909,
     'q_norm': 5.591,
     'k_norm': 5.942,
     'attn_out_norm': 3.184,
     'conv_out_norm': 3.26,
     'norm_ffn2': 3.898,
     'norm1_g_2': 2.845,
     'v_norm_g_2': 26.821,
     'v_norm_b_2': 25.757,
     'kv_norm_g_2': 8.0,
     'q_norm_g_2': 8.0,
     'k_norm_g_2': 8.0,
     'norm2_g_2': 37.784,
     'spatial_b_2': 3.754}
    for name, (base, spread) in spreads.items():
        noise = np.random.default_rng([zlib.crc32(name.encode()), seed]).standard_normal(out[name].shape)
        drawn = base * np.exp(spread * noise) if base else spread * noise
        out[name] = __import__('jax').numpy.asarray(drawn.astype(out[name].dtype))
    for name, factor in factors.items():
        out[name] = (out[name] * factor).astype(out[name].dtype)
    return out
```

```python
from contextlib import ExitStack

import numpy as np

import concourse.bass as bass
from concourse import mybir

F32 = mybir.dt.float32
U32 = mybir.dt.uint32
I32 = mybir.dt.int32
ALU = mybir.AluOpType
ACT = mybir.ActivationFunctionType
AX = mybir.AxisListType.X
EPS = 1e-6
BIG = 1e30
NS = 16

CV = {}
CVN = 0
for _n, _w in [("c2", 16), ("b_ada", 72), ("g_ffn1", 8), ("g_mix", 8), ("g_ffn2", 8), ("g_fin", 8),
               ("g_n1", 8), ("g_n2", 8), ("qn", 1), ("kn", 1), ("conv", 12), ("aon", 4), ("con", 4),
               ("kvn", 2), ("qn2", 1), ("kn2", 1)]:
    CV[_n] = (CVN, CVN + _w)
    CVN += _w

KC = {}
KCN = 0
for _n, _w in [("ident", 128), ("ones", 128), ("blk", 128), ("perm1", 128), ("perm2", 128), ("perm3", 128),
               ("cos1", 256), ("sin1", 256), ("cap", 512), ("iota", 16), ("inv2", 1), ("inv3", 1)]:
    KC[_n] = (KCN, KCN + _w)
    KCN += _w


class Queue:

    def __init__(self, sem):
        self.sem, self.count, self.items, self.seen = sem, 0, [], {}

    def wait(self, *tokens):
        for t in tokens:
            if t is None:
                continue
            if isinstance(t, list):
                self.wait(*t)
                continue
            sem, value = t
            if self.seen.get(sem.name, 0) >= value:
                continue
            self.seen[sem.name] = value
            self.items.append(lambda e, s=sem, v=value: e.wait_ge(s, v))

    def do(self, fn, *tokens):
        self.wait(*tokens)
        self.count += 1
        self.items.append(lambda e: fn(e).then_inc(self.sem, 1))
        return (self.sem, self.count)

    def quiet(self, fn, *tokens):
        self.wait(*tokens)
        self.items.append(fn)

    def dma(self, dst, src, sem, *tokens):
        self.wait(*tokens)
        self.items.append(lambda e: e.dma_start(dst, src).then_inc(sem, 16))

    def run(self, eng):
        for f in self.items:
            f(eng)


def program(nc, T, out, dbg=None):
    ctx = ExitStack()
    with ctx:
        def sb(name, shape, dt=F32):
            return ctx.enter_context(nc.sbuf_tensor(name, shape, dt))

        def sem(name):
            return ctx.enter_context(nc.semaphore(name))

        pe, dv, ac, po, sp = (Queue(sem("q_" + n)) for n in ("pe", "dve", "act", "pool", "sp"))
        psum = [ctx.enter_context(nc.psum_tensor(f"ps{i}", [128, 512], F32)) for i in range(8)]

        ring = sb("ring", [128, NS, 1024])
        XT = sb("XT", [128, 8, 512])
        HT = sb("HT", [128, 8, 512])
        AA = sb("AA", [128, 11264])
        AB = sb("AB", [128, 7168])
        ACTT = AA[:, :].rearrange("p (k t) -> p k t", k=22)
        cv = sb("cv", [128, CVN])
        kc = sb("kc", [128, KCN])
        sq = sb("sq", [128, 2, 512])
        R = sb("R", [128, 2, 512])
        M = sb("M", [128, 72, 2])
        co = sb("co", [128, 8, 2])
        sc2 = sb("sc2", [128, 16])
        m2h = sb("m2h", [128, 8, 2])
        sg = sb("sg", [128, 2, 512])
        small = sb("small", [128, 64])

        def C(n):
            return cv[:, CV[n][0]:CV[n][1]]

        def K(n):
            return kc[:, KC[n][0]:KC[n][1]]

        free = {i: None for i in range(8)}
        turn = [0, [0, 1, 2, 3, 4, 5]]

        def bank():
            b = turn[1][turn[0] % len(turn[1])]
            turn[0] += 1
            return b

        s_w = [sem(f"w{i}") for i in range(NS)]
        used = []

        def load(src, nk, nc_):
            n = len(used)
            slot = n % NS
            dst = ring[:, slot, 0:nk * nc_]
            sp.dma(dst, src, s_w[slot], used[n - NS] if n >= NS else None)
            used.append(None)
            return dst.rearrange("p (k c) -> p k c", k=nk), (s_w[slot], 16 * (n // NS + 1)), n

        def group(o, pairs, *tokens):
            n = len(pairs)
            for i, (l, r) in enumerate(pairs):
                f = (lambda e, l=l, r=r, i=i: e.matmul(o, l, r, start=(i == 0), stop=(i == n - 1)))
                if i == n - 1:
                    t = pe.do(f, *tokens)
                else:
                    pe.quiet(f, *tokens)
            return t

        s_c = sem("s_c")
        ncst = [0]

        def const(dst, src):
            sp.dma(dst, src, s_c)
            ncst[0] += 16

        const(cv[:, :], T["cvec"])
        const(kc[:, :], T["kcst"])
        c_in = (s_c, 32)
        s_c2 = sem("s_c2")
        bc = sb("bc", [128, 3, 512])
        for i, n in enumerate(("vg", "vb", "bs")):
            sp.dma(bc[:, i, :], T[n].partition_broadcast(128), s_c2)
        wsp = sb("wsp", [128, 512])
        sp.dma(wsp[:, :], T["wsp"], s_c2)
        posi = sb("posi", [128, 256], I32)
        sp.dma(posi[:, :], T["pos"].partition_broadcast(128), s_c2)
        c2_in = (s_c2, 80)

        t_sc = ac.do(lambda e: e.activation(sc2[:, :], C("c2"), ACT.Silu), c_in)
        scv = sc2[:, :].rearrange("p (k s) -> p k s", k=8)
        m_tok = {}
        ada = [0]

        def ada_tiles(n):
            for _ in range(n):
                i = ada[0]
                if i == 72:
                    return
                ada[0] += 1
                idx, j = divmod(i, 8)
                b = 6 + idx % 2
                w, tw, s = load(T["w_ada"][i], 8, 128)
                t = group(psum[b][:, 2 * j:2 * j + 2], [(w[:, k, :], scv[:, k, :]) for k in range(8)],
                          tw, t_sc, free[b])
                used[s] = t
                if j == 7:
                    bb = C("b_ada")[:, 8 * idx:8 * idx + 8].unsqueeze(2).broadcast_to([128, 8, 2])
                    m_tok[idx] = free[b] = dv.do(lambda e, b=b, idx=idx, bb=bb: e.tensor_tensor(
                        M[:, 8 * idx:8 * idx + 8, :], psum[b][:, 0:16].rearrange("p (k s) -> p k s", s=2),
                        bb, ALU.add), t, c_in)

        sqt = [None, None]
        nsq = [0]
        nR = [0]

        def rms(srcs, N, inv, toks, lhs="ones"):
            b = bank()
            for i, (s, t) in enumerate(zip(srcs, toks)):
                q = nsq[0] % 2
                nsq[0] += 1
                ta = ac.do(lambda e, s=s, q=q: e.activation(sq[:, q, 0:N], s, ACT.Square), t, sqt[q])
                f = (lambda e, q=q, i=i: e.matmul(psum[b][:, 0:N], K(lhs), sq[:, q, 0:N], start=(i == 0),
                                                  stop=(i == len(srcs) - 1)))
                tp = sqt[q] = pe.do(f, ta, free[b], c_in)
            r = R[:, nR[0] % 2, 0:N]
            nR[0] += 1
            t1 = dv.do(lambda e: e.tensor_scalar(r, psum[b][:, 0:N], inv, EPS, ALU.mult, ALU.add), tp)
            free[b] = t1
            t2 = dv.do(lambda e: e.reciprocal(r, r), t1)
            t3 = ac.do(lambda e: e.activation(r, r, ACT.Sqrt), t2)
            return r, t3

        def modulated(gain, ishift, N, toks, *ht_free):
            for i in (ishift, ishift + 1):
                while i not in m_tok:
                    ada_tiles(1)
            sh, scl = M[:, 8 * ishift:8 * ishift + 8, :], M[:, 8 * ishift + 8:8 * ishift + 16, :]
            tc = dv.do(lambda e: e.scalar_tensor_tensor(
                out=co[:, :, :], in0=scl, scalar=1.0,
                in1=C(gain).unsqueeze(2).broadcast_to([128, 8, 2]), op0=ALU.add, op1=ALU.mult),
                m_tok[ishift + 1], m_tok[ishift], c_in)
            r, tr = rms([XT[:, k, 0:N] for k in range(8)], N, 1.0 / 1024, toks)
            done = []
            for k in range(8):
                for s in range(N // 256):
                    a = slice(256 * s, 256 * s + 256)
                    td = dv.do(lambda e, k=k, s=s, a=a: e.scalar_tensor_tensor(
                        out=HT[:, k, a], in0=XT[:, k, a], scalar=co[:, k, s:s + 1], in1=r[:, a],
                        op0=ALU.mult, op1=ALU.mult), tc, tr, toks[k], *ht_free)
                    td = ac.do(lambda e, k=k, s=s, a=a: e.activation(
                        HT[:, k, a], HT[:, k, a], ACT.Identity, bias=sh[:, k, s:s + 1]), td)
                done.append(td)
            return done

        def plain(gain, srcs, N, toks, inv, dst, *ws, lhs="ones"):
            r, tr = rms(srcs, N, inv, toks, lhs)
            return [dv.do(lambda e, k=k: e.scalar_tensor_tensor(
                out=dst(k), in0=srcs[k], scalar=C(gain)[:, k:k + 1], in1=r, op0=ALU.mult, op1=ALU.mult),
                tr, toks[k], *ws) for k in range(len(srcs))]

        def project(wsrc, rhs, N, toks, *ws):
            b = bank()
            nk = len(rhs)
            pairs, at = [], 0
            while at < nk:
                n = min(8, nk - at)
                w, tw, s = load(wsrc[:, at * 128:(at + n) * 128], n, 128)
                for k in range(n):
                    i = at + k
                    f = (lambda e, w=w, k=k, i=i: e.matmul(psum[b][:, 0:N], w[:, k, :], rhs[i],
                                                           start=(i == 0), stop=(i == nk - 1)))
                    if k == n - 1:
                        t = used[s] = pe.do(f, tw, free[b], toks[i], *ws)
                    else:
                        pe.quiet(f, tw, free[b], toks[i], *ws)
                at += n
            return b, t

        sgt = [None, None]

        def ffn(win, wout, N, gain, im, toks, act_free, *ht_free, more=(0, 0)):
            h = modulated(gain, im, N, toks, *ht_free)
            at = []
            for j in range(22):
                b1, t1 = project(T[win][j], [HT[:, k, 0:N] for k in range(8)], N, h)
                b2, t2 = project(T[win][22 + j], [HT[:, k, 0:N] for k in range(8)], N, h)
                ta = ac.do(lambda e, j=j, b1=b1: e.activation(sg[:, j % 2, 0:N], psum[b1][:, 0:N], ACT.Silu),
                           t1, sgt[j % 2])
                free[b1] = ta
                td = dv.do(lambda e, j=j, b2=b2: e.tensor_tensor(
                    ACTT[:, j, 0:N], sg[:, j % 2, 0:N], psum[b2][:, 0:N], ALU.mult), ta, t2, act_free)
                free[b2] = sgt[j % 2] = td
                at.append(td)
                ada_tiles(more[0])
            while im + 2 not in m_tok:
                ada_tiles(1)
            tm = dv.do(lambda e: e.tensor_scalar(m2h[:, :, :], M[:, 8 * im + 16:8 * im + 24, :], 0.5, None,
                                                 ALU.mult), m_tok[im + 2])
            new = []
            for d in range(8):
                b, t = project(T[wout][d], [ACTT[:, k, 0:N] for k in range(22)], N, at)
                for s in range(N // 256):
                    a = slice(256 * s, 256 * s + 256)
                    td = dv.do(lambda e, d=d, s=s, a=a, b=b: e.scalar_tensor_tensor(
                        out=XT[:, d, a], in0=psum[b][:, a], scalar=m2h[:, d, s:s + 1], in1=XT[:, d, a],
                        op0=ALU.mult, op1=ALU.add), t, tm)
                free[b] = td
                new.append(td)
                ada_tiles(more[1])
            return new, t

        def copy_out(eng, dst, b, src, *tokens):
            if eng is ac:
                t = ac.do(lambda e: e.copy(dst, src), *tokens)
            else:
                t = dv.do(lambda e: e.tensor_copy(dst, src), *tokens)
            free[b] = t
            return t

        dumps = []

        def dump(name, ap, *toks):
            if dbg is not None and name in dbg:
                dumps.append((dbg[name], ap))
                s = sem("dbg_" + name)
                sp.dma(dbg[name], ap, s, *toks)
                dumps[-1] = (s, 16)

        s_x = sem("s_x")
        sp.dma(XT[:, :, :], T["xT"], s_x)
        x_in = (s_x, 16)
        x, t_pe = ffn("f1i", "f1o", 512, "g_ffn1", 0, [x_in] * 8, None, more=(1, 1))
        dump("x1", XT[:, :, :], x)
        h = modulated("g_mix", 3, 512, x, t_pe)

        qT = AA[:, 0:1024].rearrange("p (j t) -> p j t", j=4)
        kT = AA[:, 1024:2048].rearrange("p (j t) -> p j t", j=2)
        vN = AA[:, 2048:2560].rearrange("p (j d) -> p j d", j=4)
        gb = AA[:, 2560:3584].rearrange("p (j t) -> p j t", j=4)
        gc = AA[:, 3584:4608].rearrange("p (j t) -> p j t", j=4)
        pz = AA[:, 4608:4608 + 4 * 258].rearrange("p (j t) -> p j t", j=4)
        cs = AA[:, 5640:6664].rearrange("p (j t) -> p j t", j=4)
        aT = AA[:, 6664:7688].rearrange("p (j t) -> p j t", j=4)
        MX = AA[:, 7688:9736].rearrange("p (j t) -> p j t", j=8)
        tmp = AA[:, 9736:10248].rearrange("p (j t) -> p j t", j=2)
        Pb = AB[:, 0:1024].rearrange("p (j s) -> p j s", j=2)
        PT = AB[:, 1024:3072].rearrange("p (j k q) -> p j k q", j=2, k=4)
        aa_free = t_pe

        tok = {}
        for j in range(4):
            b, t = project(T["mi"][j], [HT[:, k, 0:256] for k in range(8)], 256, h)
            tok["q", j] = copy_out(ac, qT[:, j, :], b, psum[b][:, 0:256], t, aa_free)
        for j in range(2):
            b, t = project(T["mi"][4 + j], [HT[:, k, :] for k in range(8)], 512, h)
            tok["k", j] = copy_out(ac, kT[:, j, :], b, psum[b][:, :], t, aa_free)
        w, tw, s = load(T["mi"][6], 8, 128)
        b = bank()
        for i in range(4):
            t = group(psum[b][:, 128 * i:128 * i + 128],
                      [(HT[:, k, 128 * i:128 * i + 128], w[:, k, :]) for k in range(8)], tw, free[b], h)
        used[s] = t
        tok["v"] = copy_out(ac, vN.rearrange("p j d -> p (j d)"), b, psum[b][:, :], t, aa_free)
        tz = po.do(lambda e: e.memset(AA[:, 4608:4608 + 4 * 258], 0.0), aa_free)
        for j in range(4):
            b, t = project(T["mi"][7 + j], [HT[:, k, 0:256] for k in range(8)], 256, h)
            tok["gb", j] = copy_out(ac, gb[:, j, :], b, psum[b][:, 0:256], t, aa_free)
        for j in range(4):
            b, t = project(T["mi"][11 + j], [HT[:, k, 0:256] for k in range(8)], 256, h)
            tok["gc", j] = copy_out(ac, gc[:, j, :], b, psum[b][:, 0:256], t, aa_free)
        for j in range(4):
            b, t = project(T["mi"][15 + j], [HT[:, k, 0:256] for k in range(8)], 256, h)
            free[b] = tok["p", j] = dv.do(lambda e, j=j, b=b: e.tensor_tensor(
                pz[:, j, 1:257], gc[:, j, :], psum[b][:, 0:256], ALU.mult), t, tok["gc", j], tz)
        ht_used = t

        def rope(dst, src, tin, perm, cos, sin, ti, *ws):
            b = bank()
            tp = pe.do(lambda e: e.matmul(psum[b][:, 0:256], K(perm), src, start=True, stop=True), tin, free[b])
            t1 = dv.do(lambda e: e.tensor_tensor(tmp[:, ti, :], psum[b][:, 0:256], sin, ALU.mult), tp, *ws)
            free[b] = t1
            t2 = dv.do(lambda e: e.tensor_tensor(dst, src, cos, ALU.mult), tp, t1)
            return dv.do(lambda e: e.tensor_tensor(dst, dst, tmp[:, ti, :], ALU.add), t2)

        for j in range(4):
            (t,) = plain("qn", [qT[:, j, :]], 256, [tok["q", j]], 1.0 / 64, lambda k, j=j: qT[:, j, :], lhs="blk")
            tok["q", j] = rope(qT[:, j, :], qT[:, j, :], t, "perm1", K("cos1"), K("sin1"), j % 2)
        for j in range(2):
            (t,) = plain("kn", [kT[:, j, :]], 512, [tok["k", j]], 1.0 / 64, lambda k, j=j: kT[:, j, :], lhs="blk")
            tok["k", j] = rope(kT[:, j, 0:256], kT[:, j, 0:256], t, "perm1", K("cos1"), K("sin1"), j % 2)
        dump("qT", qT, tok["q", 0], tok["q", 1], tok["q", 2], tok["q", 3])
        dump("kT", kT, tok["k", 0], tok["k", 1])

        def softmax_rows(Sap, Pap, n, scale, *toks):
            c = 4 * (n % 8)
            m, nm, su, ri = (small[:, c + i:c + i + 1] for i in range(4))
            t1 = dv.do(lambda e: e.reduce_max(m, Sap, AX), *toks)
            t2 = dv.do(lambda e: e.tensor_scalar(nm, m, -scale, None, ALU.mult), t1)
            t3 = ac.do(lambda e: e.activation(Pap, Sap, ACT.Exp, bias=nm, scale=scale, accum_out=su), t2, *toks)
            t4 = dv.do(lambda e: e.reciprocal(ri, su), t3)
            t5 = dv.do(lambda e: e.tensor_scalar(Pap, Pap, ri, None, ALU.mult), t4)
            return t5, t3

        n_sm = 0
        pt_use = [None, None]
        p_use = [None, None]
        for hd in range(8):
            o = 64 * (hd % 2)
            j, kv = hd // 2, hd // 4
            ts = []
            for i in range(2):
                b = bank()
                t = pe.do(lambda e, b=b, i=i, o=o, j=j, kv=kv: e.matmul(
                    psum[b][:, :], qT[o:o + 64, j, 128 * i:128 * i + 128], kT[o:o + 64, kv, :],
                    start=True, stop=True), tok["q", j], tok["k", kv], free[b])
                tp, rd = softmax_rows(psum[b][:, :], Pb[:, i, :], n_sm, 0.125, t, p_use[i], aa_free)
                free[b] = rd
                n_sm += 1
                b = bank()
                for k in range(4):
                    t = pe.do(lambda e, b=b, i=i, k=k: e.transpose(
                        psum[b][:, 128 * k:128 * k + 128], Pb[:, i, 128 * k:128 * k + 128], K("ident")),
                        tp, free[b])
                p_use[i] = t
                ts.append(copy_out(dv, PT[:, hd % 2, :, 128 * i:128 * i + 128], b,
                                   psum[b][:, :].rearrange("p (k q) -> p k q", k=4), t, pt_use[hd % 2]))
            if hd % 2 == 0:
                bo = bank()
            pt_use[hd % 2] = t = group(
                psum[bo][o:o + 64, 0:256],
                [(vN[:, k, 64 * kv:64 * kv + 64], PT[:, hd % 2, k, :]) for k in range(4)],
                ts, tok["v"], free[bo])
            if hd % 2:
                tok["a", j] = copy_out(ac, aT[:, j, :], bo, psum[bo][:, 0:256], t)
        dump("aT", aT, tok["a", 3])
        ca = plain("aon", [aT[:, j, :] for j in range(4)], 256, [tok["a", j] for j in range(4)], 1.0 / 512,
                   lambda k: MX[:, k, :])
        cvw = C("conv")
        for j in range(4):
            t = dv.do(lambda e, j=j: e.tensor_scalar(cs[:, j, :], pz[:, j, 0:256], cvw[:, 3 * j:3 * j + 1], None,
                                                     ALU.mult), tok["p", j])
            for i in (1, 2):
                t = dv.do(lambda e, j=j, i=i: e.scalar_tensor_tensor(
                    out=cs[:, j, :], in0=pz[:, j, i:i + 256], scalar=cvw[:, 3 * j + i:3 * j + i + 1],
                    in1=cs[:, j, :], op0=ALU.mult, op1=ALU.add), t)
            tok["c", j] = dv.do(lambda e, j=j: e.tensor_tensor(cs[:, j, :], cs[:, j, :], gb[:, j, :], ALU.mult),
                                t, tok["gb", j])
        ca += plain("con", [cs[:, j, :] for j in range(4)], 256, [tok["c", j] for j in range(4)], 1.0 / 512,
                    lambda k: MX[:, 4 + k, :])
        dump("mix", MX, ca)
        while 5 not in m_tok:
            ada_tiles(1)
        nx = []
        for d in range(8):
            b, t = project(T["mo"][d], [MX[:, k, :] for k in range(8)], 256, ca)
            free[b] = td = dv.do(lambda e, d=d, b=b: e.scalar_tensor_tensor(
                out=XT[:, d, 0:256], in0=psum[b][:, 0:256], scalar=M[:, 40 + d, 0:1], in1=XT[:, d, 0:256],
                op0=ALU.mult, op1=ALU.add), t, m_tok[5])
            nx.append(td)
            ada_tiles(1)
        dump("x2", XT[:, :, :], nx)
        x, t_pe = ffn("f2i", "f2o", 256, "g_ffn2", 6, nx, t, ht_used, more=(1, 1))
        assert ada[0] == 72
        turn[1] = [0, 1, 2, 3, 4, 5, 6, 7]

        xs = [XT[:, k, 0:256] for k in range(8)]
        x = plain("g_fin", xs, 256, x, 1.0 / 1024, lambda k: XT[:, k, 0:256])
        dump("x3", XT[:, :, :], x)

        ang = AB[:, 4608:4864]
        rt = AB[:, 3072:4608].rearrange("p (j t) -> p j t", j=6)
        posf = AB[:, 4864:5120]
        t0 = dv.do(lambda e: e.tensor_copy(posf[:, :], posi[:, :]), c2_in)
        TWO_PI = 2 * np.pi
        C1 = float(np.float32(6.28125))
        C2 = float(np.float32(TWO_PI - 6.28125))
        C2 = float(np.float32(np.round(C2 * 2 ** 22) / 2 ** 22))
        C3 = float(np.float32(TWO_PI - C1 - C2))
        MAGIC = 12582912.0
        PI_ = 3.1415925
        for i, inv in enumerate(("inv2", "inv3")):
            sn, cn, nn = rt[:, 2 * i, :], rt[:, 2 * i + 1, :], rt[:, 4, :]
            t1 = dv.do(lambda e, inv=inv: e.tensor_scalar(ang[:, :], posf[:, :], K(inv), None, ALU.mult), t0, c_in)
            t1 = dv.do(lambda e, nn=nn: e.tensor_scalar(nn, ang[:, :], 1.0 / TWO_PI, MAGIC, ALU.mult, ALU.add), t1)
            t1 = dv.do(lambda e, nn=nn: e.tensor_scalar(nn, nn, MAGIC, None, ALU.subtract), t1)
            for cc in (C1, C2, C3):
                t1 = dv.do(lambda e, nn=nn, cc=cc: e.scalar_tensor_tensor(
                    out=ang[:, :], in0=nn, scalar=-cc, in1=ang[:, :], op0=ALU.mult, op1=ALU.add), t1)
            t2 = dv.do(lambda e, cn=cn: e.tensor_scalar(cn, ang[:, :], np.pi / 2, None, ALU.add), t1)
            t3 = dv.do(lambda e, cn=cn, nn=nn: e.tensor_scalar(nn, cn, PI_, TWO_PI, ALU.is_gt, ALU.mult), t2)
            t3 = dv.do(lambda e, cn=cn, nn=nn: e.tensor_tensor(cn, cn, nn, ALU.subtract), t3)
            t3 = dv.do(lambda e, cn=cn: e.tensor_scalar(cn, cn, -PI_, PI_, ALU.max, ALU.min), t3)
            t4 = dv.do(lambda e, sn=sn: e.tensor_scalar(sn, ang[:, :], -PI_, PI_, ALU.max, ALU.min), t1)
            t0 = ac.do(lambda e, i=i: e.activation(rt[:, 2 * i:2 * i + 2, :], rt[:, 2 * i:2 * i + 2, :], ACT.Sin),
                       t3, t4)
        t_rt = t0
        dump("rt", rt[:, 0:4, :], t_rt)

        h = plain("g_n1", xs, 256, x, 1.0 / 1024, lambda k: HT[:, k, 0:256], t_pe)
        hs = [HT[:, k, 0:256] for k in range(8)]
        uT = AA[:, 0:1024].rearrange("p (j t) -> p j t", j=4)
        vA = AA[:, 1024:2048].rearrange("p (c d) -> p c d", c=2)
        q2 = AA[:, 2048:3072].rearrange("p (j t) -> p j t", j=4)
        ck = AA[:, 3072:3584].rearrange("p (j t) -> p j t", j=2)
        qi = AA[:, 3584:4096].rearrange("p (j t) -> p j t", j=2)
        ki = AA[:, 4096:4352]
        k2 = AA[:, 4352:4608]
        v2 = AA[:, 4608:4864].rearrange("p (j d) -> p j d", j=2)
        wi = AA[:, 4864:4872].rearrange("p (t h) -> p t h", t=2)
        yb = AA[:, 4872:5896].rearrange("p (j t) -> p j t", j=4)
        mg = AA[:, 5896:7944].rearrange("p (j t) -> p j t", j=8)
        scr = AA[:, 7944:8456].rearrange("p (i s) -> p i s", i=2)
        wk = AA[:, 8456:8968].rearrange("p (i s) -> p i s", i=2)
        sel = AA[:, 8968:9480].rearrange("p (i s) -> p i s", i=2)
        tmp = AA[:, 9480:9992].rearrange("p (j t) -> p j t", j=2)
        mx = AA[:, 9992:10120].rearrange("p (i s) -> p i s", i=2)
        onesr = AA[:, 10120:10376]
        P2 = AA[:, 10376:10888].rearrange("p (i s) -> p i s", i=2)
        gt = HT[:, :, 256:512]
        gt2 = XT[:, :, 256:512]
        PT2 = AB[:, 1024:2048].rearrange("p (j k q) -> p j k q", j=2, k=2)
        aa_free = t_pe
        st = sb("st", [128, 16])

        for j in range(2):
            b, t = project(T["w2"][j], hs, 256, h)
            tok["qi", j] = copy_out(ac, qi[:, j, :], b, psum[b][:, 0:256], t, aa_free)
        b, t = project(T["w2"][2], hs, 256, h)
        tok["ki"] = copy_out(ac, ki, b, psum[b][:, 0:256], t, aa_free)
        w, tw, s = load(T["w2w"], 8, 4)
        b = bank()
        for i in range(2):
            t = group(psum[b][:, 4 * i:4 * i + 4],
                      [(HT[:, k, 128 * i:128 * i + 128], w[:, k, :]) for k in range(8)], tw, free[b], h)
        used[s] = t
        tok["wi"] = free[b] = dv.do(lambda e, b=b: e.tensor_scalar(
            wi.rearrange("p t h -> p (t h)"), psum[b][:, 0:8], 0.5, None, ALU.mult), t, aa_free)
        for j in range(2):
            b, t = project(T["w2"][3 + j], hs, 256, h)
            tok["ck", j] = copy_out(ac, ck[:, j, :], b, psum[b][:, 0:256], t, aa_free)
        for j in range(4):
            b, t = project(T["w2"][5 + j], hs, 256, h)
            tok["q2", j] = copy_out(ac, q2[:, j, :], b, psum[b][:, 0:256], t, aa_free)
        for j in range(2):
            tok["qi", j] = rope(qi[:, j, :], qi[:, j, :], tok["qi", j], "perm3", rt[:, 3, :], rt[:, 2, :], j,
                                t_rt, aa_free)
        tok["ki"] = rope(ki, ki, tok["ki"], "perm3", rt[:, 3, :], rt[:, 2, :], 0)
        dump("qi", qi, tok["qi", 0], tok["qi", 1])

        t_or = dv.do(lambda e: e.memset(onesr, 1.0), aa_free)
        for i in range(2):
            t = None
            for hd in range(4):
                o = 64 * (hd % 2)
                b = bank()
                tp = pe.do(lambda e, b=b, i=i, o=o, hd=hd: e.matmul(
                    psum[b][:, 0:256], qi[o:o + 64, hd // 2, 128 * i:128 * i + 128], ki[o:o + 64, :],
                    start=True, stop=True), tok["qi", hd // 2], tok["ki"], free[b])
                ta = ac.do(lambda e, b=b, i=i, hd=hd: e.activation(
                    tmp[:, hd % 2, :], psum[b][:, 0:256], ACT.Relu, scale=0.125), tp, tok.get(("tm", hd % 2)),
                    tok["qi", 0], tok["qi", 1], tok["ki"])
                free[b] = ta
                if hd == 0:
                    t = dv.do(lambda e, i=i: e.tensor_scalar(scr[:, i, :], tmp[:, 0, :], wi[:, i, 0:1], None,
                                                             ALU.mult), ta, tok["wi"])
                else:
                    t = dv.do(lambda e, i=i, hd=hd: e.scalar_tensor_tensor(
                        out=scr[:, i, :], in0=tmp[:, hd % 2, :], scalar=wi[:, i, hd:hd + 1], in1=scr[:, i, :],
                        op0=ALU.mult, op1=ALU.add), ta, t)
                tok["tm", hd % 2] = t
            cap = K("cap")[:, 256 * i:256 * i + 256]
            t = dv.do(lambda e, i=i, cap=cap: e.tensor_tensor(scr[:, i, :], scr[:, i, :], cap, ALU.min), t)
            src = scr[:, i, :]
            for r in range(8):
                t = dv.do(lambda e, i=i, r=r, src=src: e.max(mx[:, i, 8 * r:8 * r + 8], src), t)
                if r < 7:
                    t = dv.do(lambda e, i=i, r=r, src=src: e.match_replace(
                        wk[:, i, :], mx[:, i, 8 * r:8 * r + 8], src, -3e38), t)
                    src = wk[:, i, :]
            th = mx[:, i, 63:64]
            t = dv.do(lambda e, i=i, th=th: e.tensor_scalar(sel[:, i, :], scr[:, i, :], th, None, ALU.is_gt), t)
            t = dv.do(lambda e, i=i: e.reduce_sum(mx[:, i, 0:1], sel[:, i, :], AX), t)
            t = dv.do(lambda e, i=i: e.tensor_scalar(mx[:, i, 1:2], mx[:, i, 0:1], -1.0, 64.0, ALU.mult, ALU.add), t)
            t = dv.do(lambda e, i=i, th=th: e.tensor_scalar(scr[:, i, :], scr[:, i, :], th, None, ALU.is_equal), t)
            t = dv.do(lambda e, i=i: e.tensor_tensor_scan(wk[:, i, :], onesr, scr[:, i, :], 0.0, ALU.mult, ALU.add),
                      t, t_or)
            t = dv.do(lambda e, i=i: e.scalar_tensor_tensor(
                out=wk[:, i, :], in0=wk[:, i, :], scalar=mx[:, i, 1:2], in1=scr[:, i, :],
                op0=ALU.is_le, op1=ALU.mult), t)
            t = dv.do(lambda e, i=i: e.tensor_tensor(sel[:, i, :], sel[:, i, :], wk[:, i, :], ALU.add), t)
            t = dv.do(lambda e, i=i: e.tensor_scalar(sel[:, i, :], sel[:, i, :], 2 * BIG, -BIG, ALU.mult, ALU.add), t)
            tok["sel", i] = dv.do(lambda e, i=i, cap=cap: e.tensor_tensor(sel[:, i, :], sel[:, i, :], cap, ALU.min), t)
        dump("sel", sel, tok["sel", 0], tok["sel", 1])

        c1 = plain("kvn", [ck[:, j, :] for j in range(2)], 256, [tok["ck", j] for j in range(2)], 1.0 / 256,
                   lambda k: ck[:, k, :])
        b, t = project(T["wuk"][0], [ck[:, j, :] for j in range(2)], 256, c1)
        tk = copy_out(ac, k2, b, psum[b][:, 0:256], t, aa_free)
        w, tw, s = load(T["wuv"][0], 2, 128)
        b = bank()
        for i in range(2):
            t = group(psum[b][:, 128 * i:128 * i + 128],
                      [(ck[:, k, 128 * i:128 * i + 128], w[:, k, :]) for k in range(2)], tw, free[b], c1)
        used[s] = t
        tok["v2"] = copy_out(ac, v2.rearrange("p j d -> p (j d)"), b, psum[b][:, 0:256], t, aa_free)
        (tk,) = plain("kn2", [k2], 256, [tk], 1.0 / 128, lambda k: k2)
        tk = rope(k2, k2, tk, "perm2", rt[:, 1, :], rt[:, 0, :], 0, tok["tm", 0], tok["tm", 1])
        for j in range(4):
            (t,) = plain("qn2", [q2[:, j, :]], 256, [tok["q2", j]], 1.0 / 128, lambda k, j=j: q2[:, j, :])
            tok["q2", j] = rope(q2[:, j, :], q2[:, j, :], t, "perm2", rt[:, 1, :], rt[:, 0, :], j % 2)

        tv = []
        for j in range(4):
            w, tw, s = load(T["w2"][9 + j], 8, 128)
            b = bank()
            for i in range(2):
                t = group(psum[b][:, 128 * i:128 * i + 128],
                          [(HT[:, k, 128 * i:128 * i + 128], w[:, k, :]) for k in range(8)], tw, free[b], h)
            used[s] = t
            t = ac.do(lambda e, j=j, b=b: e.activation(
                vA[:, :, 128 * j:128 * j + 128], psum[b][:, 0:256].rearrange("p (c d) -> p c d", c=2),
                ACT.Gelu_apprx_tanh), t, aa_free)
            free[b] = t
            tv.append(t)
        for j in range(4):
            b, t = project(T["w2"][13 + j], hs, 256, h)
            tok["u", j] = free[b] = ac.do(lambda e, j=j, b=b: e.activation(
                uT[:, j, :], psum[b][:, 0:256], ACT.Gelu_apprx_tanh), t, aa_free)

        S2 = 128 ** -0.5
        p_use = [None, None]
        pt_use = [None, None]
        for hd in range(4):
            ts = []
            for i in range(2):
                b = bank()
                t = pe.do(lambda e, b=b, i=i, hd=hd: e.matmul(
                    psum[b][:, 0:256], q2[:, hd, 128 * i:128 * i + 128], k2, start=True, stop=True),
                    tok["q2", hd], tk, free[b])
                t = dv.do(lambda e, b=b, i=i: e.scalar_tensor_tensor(
                    out=P2[:, i, :], in0=psum[b][:, 0:256], scalar=S2, in1=sel[:, i, :], op0=ALU.mult,
                    op1=ALU.min), t, tok["sel", i], p_use[i])
                free[b] = t
                tp, _ = softmax_rows(P2[:, i, :], P2[:, i, :], n_sm, 1.0, t)
                n_sm += 1
                b = bank()
                for k in range(2):
                    t = pe.do(lambda e, b=b, i=i, k=k: e.transpose(
                        psum[b][:, 128 * k:128 * k + 128], P2[:, i, 128 * k:128 * k + 128], K("ident")),
                        tp, free[b])
                p_use[i] = t
                ts.append(copy_out(dv, PT2[:, hd % 2, :, 128 * i:128 * i + 128], b,
                                   psum[b][:, 0:256].rearrange("p (k q) -> p k q", k=2), t, pt_use[hd % 2]))
            b = bank()
            pt_use[hd % 2] = t = group(psum[b][:, 0:256], [(v2[:, k, :], PT2[:, hd % 2, k, :]) for k in range(2)],
                                       ts, tok["v2"], free[b])
            tok["yb", hd] = copy_out(ac, yb[:, hd, :], b, psum[b][:, 0:256], t)
        dump("yb", yb, tok["yb", 3])

        tw_ = po.do(lambda e: e.affine_select(
            wsp[:, :].rearrange("p (g t) -> p g t", g=4), wsp[:, :].rearrange("p (g t) -> p g t", g=4),
            [[0, 4], [1, 128]], ALU.is_ge, 0.0, base=0, channel_multiplier=-1), c2_in)
        for c in range(2):
            t = dv.do(lambda e, c=c: e.bn_stats(st[:, 0:6], vA[:, c, :]), tv)
            t = dv.do(lambda e: e.bn_aggr(st[:, 6:8], st[:, 0:6]), t)
            t = dv.do(lambda e: e.tensor_scalar(st[:, 8:9], st[:, 7:8], EPS, None, ALU.add), t)
            t = dv.do(lambda e: e.reciprocal(st[:, 9:10], st[:, 8:9]), t)
            t = ac.do(lambda e: e.activation(st[:, 10:11], st[:, 9:10], ACT.Sqrt), t)
            t = dv.do(lambda e, c=c: e.tensor_scalar(vA[:, c, :], vA[:, c, :], st[:, 6:7], st[:, 10:11],
                                                     ALU.subtract, ALU.mult), t)
            t = dv.do(lambda e, c=c: e.tensor_tensor(vA[:, c, :], vA[:, c, :], bc[:, 0, :], ALU.mult), t, c2_in)
            t = dv.do(lambda e, c=c: e.tensor_tensor(vA[:, c, :], vA[:, c, :], bc[:, 1, :], ALU.add), t)
            b = bank()
            for g in range(4):
                tp = pe.do(lambda e, b=b, g=g, c=c: e.matmul(
                    psum[b][:, 128 * g:128 * g + 128], vA[:, c, 128 * g:128 * g + 128],
                    wsp[:, 128 * g:128 * g + 128], start=True, stop=True), t, tw_, free[b])
            t = dv.do(lambda e, b=b, c=c: e.tensor_tensor(sg[:, c, :], psum[b][:, :], bc[:, 2, :], ALU.add), tp)
            free[b] = t
            tok["ya", c] = dv.do(lambda e, c=c: e.tensor_tensor(
                uT[:, :, 128 * c:128 * c + 128], uT[:, :, 128 * c:128 * c + 128],
                sg[:, c, :].rearrange("p (g t) -> p g t", g=4), ALU.mult), t, [tok["u", j] for j in range(4)])
        dump("ya", uT, tok["ya", 0], tok["ya", 1])

        for j in range(16):
            b, t = project(T["w2"][17 + j], hs, 256, h)
            g_ = gt[:, j, :] if j < 8 else gt2[:, j - 8, :]
            tok["g", j] = free[b] = ac.do(lambda e, g_=g_, b=b: e.activation(g_, psum[b][:, 0:256], ACT.Sigmoid),
                                          t, t_pe, nx[7])
        ht_used = t
        tm = []
        for d in range(8):
            b1, t1 = project(T["wa"][d], [uT[:, k, :] for k in range(4)], 256, [[tok["ya", 0], tok["ya", 1]]] * 4)
            t1 = free[b1] = dv.do(lambda e, d=d, b1=b1: e.tensor_tensor(
                gt[:, d, :], gt[:, d, :], psum[b1][:, 0:256], ALU.mult), t1, tok["g", d])
            b2, t2 = project(T["wb"][d], [yb[:, k, :] for k in range(4)], 256, [tok["yb", k] for k in range(4)])
            t2 = free[b2] = dv.do(lambda e, d=d, b2=b2: e.tensor_tensor(
                gt2[:, d, :], gt2[:, d, :], psum[b2][:, 0:256], ALU.mult), t2, tok["g", 8 + d])
            tm.append(dv.do(lambda e, d=d: e.tensor_tensor(mg[:, d, :], gt[:, d, :], gt2[:, d, :], ALU.add), t1, t2))
        x2 = []
        for d in range(8):
            b, t = project(T["wo"][d], [mg[:, k, :] for k in range(8)], 256, tm)
            free[b] = td = dv.do(lambda e, d=d, b=b: e.tensor_tensor(
                XT[:, d, 0:256], XT[:, d, 0:256], psum[b][:, 0:256], ALU.add), t, x)
            x2.append(td)
        dump("h1", XT[:, :, :], x2)

        h = plain("g_n2", xs, 256, x2, 1.0 / 1024, lambda k: HT[:, k, 0:256], ht_used)
        hN = sb("hN", [128, 2, 1024])
        yN = AB[:, 0:2048].rearrange("p (t d) -> p t d", t=2)
        for t_ in range(2):
            for dst, srcs, tk_, eng in ((hN, HT, h, dv), (yN, XT, x2, ac)):
                for half in range(2):
                    b = bank()
                    for k in range(4):
                        kk = 4 * half + k
                        t = pe.do(lambda e, b=b, k=k, kk=kk, srcs=srcs, t_=t_: e.transpose(
                            psum[b][:, 128 * k:128 * k + 128], srcs[:, kk, 128 * t_:128 * t_ + 128], K("ident")),
                            tk_[kk], free[b])
                    tok[("n", srcs is HT, t_, half)] = copy_out(
                        eng, dst[:, t_, 512 * half:512 * half + 512], b, psum[b][:, :], t, pt_use[0], pt_use[1])
        qp = AB[:, 3072:7168].rearrange("p (j t) -> p j t", j=16)
        tq = []
        for j in range(16):
            b, t = project(T["wq"][j], hs, 256, h)
            tq.append(copy_out(ac, qp[:, j, :], b, psum[b][:, 0:256], t))
        at = [8192]

        def take(*shape, dt=F32):
            n = int(np.prod(shape))
            a = AA[:, at[0]:at[0] + n]
            at[0] += n
            assert at[0] <= 11264
            if dt is not F32:
                a = a.bitcast(dt)
            return a.rearrange("p (a b) -> p a b", a=shape[0]) if len(shape) == 2 else a

        sub = take(512)
        wk3 = take(128)
        top = take(16, 16)
        topi = take(16, 16, dt=U32)
        topf = take(16, 16)
        cand = take(2, 256)
        best = take(8, 16)
        bpos = take(8, 16, dt=U32)
        ij = take(2, 128, dt=U32)
        ijf = take(2, 128)
        isel = take(2, 128)
        oh = HT[:, :, :].rearrange("p k t -> p (k t)")[:, 0:2048].rearrange("p (h k i) -> p h k i", h=8, k=16)
        idx = AB[:, 2048:2304].bitcast(U32).rearrange("p (a b) -> p a b", a=2)
        gate = AB[:, 2304:2560].rearrange("p (a b) -> p a b", a=2)
        av = AB[:, 2560:2816].rearrange("p (a b) -> p a b", a=2)
        tg = {}
        sk_t = None
        w0, tw0, s0 = load(T["sk"][0], 8, 128)
        w1, tw1, s1 = load(T["sk"][1], 8, 128)
        sub_use = None
        for t_ in range(2):
            for h2 in range(4):
                b = bank()
                for i in range(4):
                    j = 4 * h2 + i
                    w = (w0 if j < 8 else w1)[:, j % 8, :]
                    tp = pe.do(lambda e, b=b, i=i, j=j, w=w, t_=t_: e.matmul(
                        psum[b][:, 128 * i:128 * i + 128], qp[:, j, 128 * t_:128 * t_ + 128], w,
                        start=True, stop=True), tq[j], tw0, tw1, free[b])
                ts = copy_out(ac, sub[:, :], b, psum[b][:, :], tp, sub_use, x2)
                for i in range(4):
                    j = 4 * h2 + i
                    s_ = sub[:, 128 * i:128 * i + 128]
                    t = dv.do(lambda e, j=j, s_=s_: e.max(top[:, j, 0:8], s_), ts)
                    dv.do(lambda e, j=j, s_=s_: e.max_index(topi[:, j, 0:8], top[:, j, 0:8], s_), t)
                    t = dv.do(lambda e, j=j, s_=s_: e.match_replace(wk3[:, :], top[:, j, 0:8], s_, -3e38), t)
                    t = dv.do(lambda e, j=j: e.max(top[:, j, 8:16], wk3[:, :]), t)
                    sub_use = t = dv.do(lambda e, j=j: e.max_index(topi[:, j, 8:16], top[:, j, 8:16], wk3[:, :]), t)
                for hd in (2 * h2, 2 * h2 + 1):
                    a = top[:, 2 * hd, :].unsqueeze(2).broadcast_to([128, 16, 16])
                    c_ = top[:, 2 * hd + 1, :].unsqueeze(1).broadcast_to([128, 16, 16])
                    cd = cand[:, 0, :]
                    t = dv.do(lambda e, a=a, c_=c_, cd=cd: e.tensor_tensor(
                        cd.rearrange("p (i j) -> p i j", i=16), a, c_, ALU.add), t)
                    t = dv.do(lambda e, hd=hd, cd=cd: e.max(best[:, hd, 0:8], cd), t)
                    dv.do(lambda e, hd=hd, cd=cd: e.max_index(bpos[:, hd, 0:8], best[:, hd, 0:8], cd), t)
                    t = dv.do(lambda e, hd=hd, cd=cd: e.match_replace(
                        cand[:, 1, :], best[:, hd, 0:8], cd, -3e38), t)
                    t = dv.do(lambda e, hd=hd: e.max(best[:, hd, 8:16], cand[:, 1, :]), t)
                    t = dv.do(lambda e, hd=hd: e.max_index(bpos[:, hd, 8:16], best[:, hd, 8:16], cand[:, 1, :]), t)
                    c = 4 * (hd % 4)
                    nm, su, ri = (small[:, 32 + c + i:33 + c + i] for i in range(3))
                    gg = gate[:, t_, 16 * hd:16 * hd + 16]
                    t5 = dv.do(lambda e, hd=hd, nm=nm: e.tensor_scalar(nm, best[:, hd, 0:1], -1.0, None, ALU.mult), t)
                    t5 = ac.do(lambda e, hd=hd, nm=nm, su=su, gg=gg: e.activation(
                        gg, best[:, hd, :], ACT.Exp, bias=nm, accum_out=su), t5)
                    t5 = dv.do(lambda e, ri=ri, su=su: e.reciprocal(ri, su), t5)
                    tg[t_, hd] = dv.do(lambda e, ri=ri, gg=gg: e.tensor_scalar(gg, gg, ri, None, ALU.mult), t5)
            bp = bpos[:, :, :].rearrange("p h k -> p (h k)")
            dv.do(lambda e: e.tensor_scalar(ij[:, 0, :], bp, 4, None, ALU.logical_shift_right), t)
            t = dv.do(lambda e: e.tensor_scalar(ij[:, 1, :], bp, 15, None, ALU.bitwise_and), t)
            t = dv.do(lambda e: e.tensor_copy(ijf[:, :, :], ij[:, :, :]), t)
            t = dv.do(lambda e: e.tensor_copy(topf[:, :, :], topi[:, :, :]), t)
            tv_ = topf[:, :, :].rearrange("p (h q) i -> p h q i", q=2)
            for q in range(2):
                a = ijf[:, q, :].unsqueeze(2).broadcast_to([128, 128, 16])
                io = K("iota").unsqueeze(1).broadcast_to([128, 128, 16])
                o3 = oh.rearrange("p h k i -> p (h k) i")
                t = dv.do(lambda e, a=a, io=io, o3=o3: e.tensor_tensor(o3, a, io, ALU.is_equal), t, tq[15])
                for hd in range(8):
                    v_ = tv_[:, hd, q, :].unsqueeze(1).broadcast_to([128, 16, 16])
                    t2 = dv.do(lambda e, hd=hd, v_=v_: e.tensor_tensor(oh[:, hd, :, :], oh[:, hd, :, :], v_,
                                                                      ALU.mult), t)
                t = dv.do(lambda e, q=q, o3=o3: e.reduce_sum(isel[:, q, :], o3, AX), t2)
            t = dv.do(lambda e: e.scalar_tensor_tensor(
                out=isel[:, 0, :], in0=isel[:, 0, :], scalar=128.0, in1=isel[:, 1, :], op0=ALU.mult,
                op1=ALU.add), t)
            tok["idx", t_] = dv.do(lambda e, t_=t_: e.tensor_copy(idx[:, t_, :], isel[:, 0, :]), t)
        used[s0] = used[s1] = tp
        dump("idx", idx[:, :, :], tok["idx", 1])
        dump("gate", gate[:, :, :], tg[1, 7])

        NB = 24
        s_g = [sem(f"g{i}") for i in range(NB)]
        gbuf = [ring[:, i, :] for i in range(NS)] + [AA[:, 1024 * i:1024 * i + 1024] for i in range(NB - NS)]
        g_use = []
        start = [used[-1 - i] for i in range(NS)] + [x2[7], tok["idx", 0]]

        def gather(tab, t_, k):
            n = len(g_use)
            s = n % NB
            po.wait(g_use[n - NB] if n >= NB else start, tok["idx", t_])
            po.items.append(lambda e, s=s, t_=t_, k=k: e.indirect_dma_start(
                gbuf[s], None, T[tab], bass.IndirectOffsetOnAxis(ap=idx[:, t_, k:k + 1], axis=0)
            ).then_inc(s_g[s], 16))
            g_use.append(None)
            return gbuf[s], (s_g[s], 16 * (n // NB + 1)), n

        blocks = [(t_, k) for t_ in range(2) for k in range(0, 128, 4)]
        pend = None
        t_acc = None

        def second(p):
            nonlocal t_acc
            (t_, k0), tgl, vs = p
            w_ = av[:, t_, k0:k0 + 4]
            t = dv.do(lambda e: e.tensor_tensor(w_, w_, gate[:, t_, k0:k0 + 4], ALU.mult), tgl, tg[t_, k0 // 16])
            for k in range(4):
                g_, ta, n = vs[k]
                t = dv.do(lambda e, k=k, g_=g_: e.scalar_tensor_tensor(
                    out=yN[:, t_, :], in0=g_, scalar=av[:, t_, k0 + k:k0 + k + 1], in1=yN[:, t_, :],
                    op0=ALU.mult, op1=ALU.add), t, ta, tok["n", False, t_, 0], tok["n", False, t_, 1])
                g_use[n] = t
            return t

        fin = {}
        for (t_, k0) in blocks:
            us = [gather("pu", t_, k0 + k) for k in range(4)]
            vs = [gather("pv", t_, k0 + k) for k in range(4)]
            for k in range(4):
                g_, ta, n = us[k]
                t = dv.do(lambda e, k=k, g_=g_, t_=t_, k0=k0: e.tensor_tensor_reduce(
                    g_, g_, hN[:, t_, :], 1.0, 0.0, ALU.mult, ALU.add, av[:, t_, k0 + k:k0 + k + 1]),
                    ta, tok["n", True, t_, 0], tok["n", True, t_, 1])
                g_use[n] = t
            if pend is not None:
                fin[pend[0][0]] = second(pend)
            tgl = ac.do(lambda e, t_=t_, k0=k0: e.activation(
                av[:, t_, k0:k0 + 4], av[:, t_, k0:k0 + 4], ACT.Gelu_apprx_tanh), t)
            pend = ((t_, k0), tgl, vs)
        fin[1] = second(pend)

        s_out = sem("s_out")
        for t_ in range(2):
            sp.dma(out[128 * t_:128 * t_ + 128, :], yN[:, t_, :], s_out, fin[t_])
        sp.wait((s_out, 32))
        for d in dumps:
            sp.wait(d)

        block = ctx.enter_context(nc.Block())

        @block.tensor
        def _(e):
            pe.run(e)

        @block.vector
        def _(e):
            dv.run(e)

        @block.scalar
        def _(e):
            ac.run(e)

        @block.gpsimd
        def _(e):
            po.run(e)

        @block.sync
        def _(e):
            sp.run(e)


def constants():
    f = np.float32
    k = np.zeros((128, KCN), f)

    def put(n, a):
        k[:, KC[n][0]:KC[n][1]] = a

    put("ident", np.eye(128))
    put("ones", 1.0)
    put("blk", np.kron(np.eye(2), np.ones((64, 64))))
    p = np.zeros((128, 128), f)
    for i in range(64):
        p[2 * i + 1, 2 * i] = -1.0
        p[2 * i, 2 * i + 1] = 1.0
    put("perm1", p)
    p = np.zeros((128, 128), f)
    for i in range(16):
        p[16 + i, i] = -1.0
        p[i, 16 + i] = 1.0
    put("perm2", p)
    p = np.zeros((128, 128), f)
    for o in (0, 64):
        for i in range(8):
            p[o + 8 + i, o + i] = -1.0
            p[o + i, o + 8 + i] = 1.0
    put("perm3", p)
    t = np.arange(256)
    inv = np.power(f(10000.0), (-np.arange(16, dtype=f) / f(16)).astype(f)).astype(f)
    a = np.concatenate([(t // 64).astype(f)[:, None] * inv, (t % 64).astype(f)[:, None] * inv], 1).astype(f)
    a = np.repeat(a.T, 2, axis=0)
    a = np.concatenate([a, a], 0)
    put("cos1", np.cos(a.astype(np.float64)))
    put("sin1", np.sin(a.astype(np.float64)))
    q = np.arange(128)
    for i in range(2):
        k[:, KC["cap"][0] + 256 * i:KC["cap"][0] + 256 * i + 256] = np.where(
            np.arange(256)[None, :] <= (q + 128 * i)[:, None], f(3e38), f(-BIG))
    put("iota", np.arange(16)[None, :])
    for n, rot, base in (("inv2", 32, [0]), ("inv3", 16, [0, 64])):
        half = rot // 2
        v = np.power(f(500000.0), (-np.arange(half, dtype=f) * f(2.0) / f(rot)).astype(f)).astype(f)
        col = np.zeros(128, f)
        for o in base:
            col[o:o + half] = v
            col[o + half:o + rot] = v
        put(n, col[:, None])
    return k


def tiles(w, nc=128):
    kk, n = w.shape
    return np.ascontiguousarray(
        w.reshape(kk // 128, 128, n // nc, nc).transpose(2, 1, 0, 3).reshape(n // nc, 128, -1))


def layout(i):
    def cols(v):
        v = np.asarray(v)
        return v.reshape(-1, 128).T

    mi, w2 = i["w_mix_in"][0], i["w_in_2"][0]
    mi = np.concatenate([mi[:, 0:512], mi[:, 512:576], mi[:, 512:576], mi[:, 576:640], mi[:, 576:640],
                         mi[:, 640:]], 1)
    w2r = np.concatenate([w2[:, 1792:2048], w2[:, 2048:2112], w2[:, 2048:2112], w2[:, 1536:1792],
                          w2[:, 1024:1536], w2[:, 512:1024], w2[:, 0:512], w2[:, 2116:4164]], 1)
    c2 = np.stack([cols(i["c"][0]), cols(i["c_ctx"])], 2).reshape(128, 16)
    cw = i["conv_w"][0].reshape(3, 4, 128).transpose(2, 1, 0).reshape(128, 12)
    vec = {
        "c2": c2, "b_ada": cols(i["b_ada"][0]), "g_ffn1": cols(i["norm_ffn1"][0]),
        "g_mix": cols(i["norm_mix"][0]), "g_ffn2": cols(i["norm_ffn2"][0]), "g_fin": cols(i["final_norm"]),
        "g_n1": cols(i["norm1_g_2"][0]), "g_n2": cols(i["norm2_g_2"][0]),
        "qn": np.tile(i["q_norm"][0], 2)[:, None], "kn": np.tile(i["k_norm"][0], 2)[:, None],
        "conv": cw, "aon": cols(i["attn_out_norm"][0]), "con": cols(i["conv_out_norm"][0]),
        "kvn": cols(i["kv_norm_g_2"][0]), "qn2": cols(i["q_norm_g_2"][0]), "kn2": cols(i["k_norm_g_2"][0]),
    }
    cvec = np.concatenate([vec[n] for n in CV], 1)
    xc = np.concatenate([i["x"][0], i["ctx"][0]], 0).T.reshape(8, 128, 512).transpose(1, 0, 2)
    sk = i["peer_subkeys_2"][0].reshape(16, 128, 128).transpose(2, 0, 1)
    return {
        "cvec": cvec, "kcst": constants(), "xT": xc,
        "vg": i["v_norm_g_2"][0], "vb": i["v_norm_b_2"][0], "bs": i["spatial_b_2"][0].reshape(512),
        "wsp": i["spatial_w_2"][0].transpose(2, 0, 1).reshape(128, 512),
        "pos": i["positions_2"][0],
        "w_ada": tiles(i["w_ada"][0]), "f1i": tiles(i["w_ffn1_in"][0]), "f1o": tiles(i["w_ffn1_out"][0]),
        "mi": tiles(mi), "mo": tiles(i["w_mix_out"][0]),
        "f2i": tiles(i["w_ffn2_in"][0]), "f2o": tiles(i["w_ffn2_out"][0]),
        "w2": tiles(w2r), "w2w": tiles(w2[:, 2112:2116], 4)[0],
        "wuk": tiles(i["w_uk_2"][0]), "wuv": tiles(i["w_uv_2"][0]),
        "wa": tiles(i["w_a_out_2"][0]), "wb": tiles(i["w_b_out_2"][0]), "wo": tiles(i["w_o_2"][0]),
        "wq": tiles(i["peer_wq_2"][0]),
        "sk": sk.reshape(128, 2, 1024).transpose(1, 0, 2),
        "pu": i["peer_u_2"][0], "pv": i["peer_v_2"][0],
    }


DBG = {}


def kernel(**inputs):
    import concourse.bacc as _bacc
    from concourse.bass_utils import run_bass_kernel_spmd as _run

    lay = layout({k: np.asarray(v) for k, v in inputs.items()})
    nc = _bacc.Bacc("TRN2", target_bir_lowering=False, num_devices=1)
    arrays, T = {}, {}
    for name, a in lay.items():
        a = np.ascontiguousarray(a)
        arrays[f"in_{name}"] = a
        T[name] = nc.dram_tensor(f"in_{name}", a.shape, mybir.dt.from_np(a.dtype), kind="ExternalInput").ap()
    out = nc.dram_tensor("out_0", (256, 1024), F32, kind="ExternalOutput").ap()
    dbg = {n: nc.dram_tensor("dbg_" + n, s, d, kind="ExternalOutput").ap() for n, (s, d) in DBG.items()}
    program(nc, T, out, dbg)
    r = _run(nc, [arrays], core_ids=[0])
    return r.results[0]["out_0"].reshape(1, 256, 1024)
```

```python
from contextlib import ExitStack

import numpy as np

import concourse.bass as bass
from concourse import mybir

F32 = mybir.dt.float32
U32 = mybir.dt.uint32
I32 = mybir.dt.int32
ALU = mybir.AluOpType
ACT = mybir.ActivationFunctionType
AX = mybir.AxisListType.X
EPS = 1e-6
BIG = 1e30
NS = 8
NSP = 4
AHEAD = 3
FR = mybir.dt.float32r

CV = {}
CVN = 0
for _n, _w in [("c2", 16), ("b_ada", 72), ("g_ffn1", 8), ("g_mix", 8), ("g_ffn2", 8), ("g_fin", 8),
               ("g_n1", 8), ("g_n2", 8), ("qn", 1), ("kn", 1), ("conv", 12), ("aon", 4), ("con", 4),
               ("kvn", 2), ("qn2", 1), ("kn2", 1)]:
    CV[_n] = (CVN, CVN + _w)
    CVN += _w

KC = {}
KCN = 0
for _n, _w in [("ident", 128), ("ones", 128), ("blk", 128), ("perm1", 128), ("perm2", 128), ("perm3", 128),
               ("cos1", 256), ("sin1", 256), ("cap", 512), ("iota", 16), ("inv2", 1), ("inv3", 1)]:
    KC[_n] = (KCN, KCN + _w)
    KCN += _w


class Queue:

    def __init__(self, sem):
        self.sem, self.count, self.items, self.seen = sem, 0, [], {}

    def wait(self, *tokens):
        for t in tokens:
            if t is None:
                continue
            if isinstance(t, list):
                self.wait(*t)
                continue
            sem, value = t
            if self.seen.get(sem.name, 0) >= value:
                continue
            self.seen[sem.name] = value
            self.items.append(lambda e, s=sem, v=value: e.wait_ge(s, v))

    def do(self, fn, *tokens):
        self.wait(*tokens)
        self.count += 1
        self.items.append(lambda e: fn(e).then_inc(self.sem, 1))
        return (self.sem, self.count)

    def quiet(self, fn, *tokens):
        self.wait(*tokens)
        self.items.append(fn)

    def dma(self, dst, src, sem, *tokens):
        self.wait(*tokens)
        self.items.append(lambda e: e.dma_start(dst, src).then_inc(sem, 16))

    def run(self, eng):
        for f in self.items:
            f(eng)


def program(nc, T, out, dbg=None):
    ctx = ExitStack()
    with ctx:
        def sb(name, shape, dt=F32):
            return ctx.enter_context(nc.sbuf_tensor(name, shape, dt))

        def sem(name):
            return ctx.enter_context(nc.semaphore(name))

        pe, dv, ac, po, sp = (Queue(sem("q_" + n)) for n in ("pe", "dve", "act", "pool", "sp"))
        psum = [ctx.enter_context(nc.psum_tensor(f"ps{i}", [128, 512], F32)) for i in range(8)]

        ring = sb("ring", [128, NS, 1024])
        with ExitStack() as once:
            WR, HR, AR = (once.enter_context(nc.sbuf_tensor(n, [128, w], FR))
                          for n, w in (("WR", 8192), ("HR", 8192), ("AR", 11264)))
        WF, HF, AA = (sb(n, [128, w]) for n, w in (("WF", 8192), ("HF", 8192), ("AF", 11264)))
        WS = WR[:, :].rearrange("p (s h c) -> p s h c", s=NSP, h=2)
        Hs = HR[:, :].rearrange("p (h k t) -> p h k t", h=2, k=8)
        XT = sb("XT", [128, 8, 512])
        AB = sb("AB", [128, 6144])
        F = sb("F", [128, 3, 512])
        cv = sb("cv", [128, CVN])
        kc = sb("kc", [128, KCN])
        sqf = sb("sq", [128, 1024])
        Rf = sb("R", [128, 1024])
        M = sb("M", [128, 72, 2])
        Mr = sb("Mr", [128, 72, 2])
        co = sb("co", [128, 8, 2])
        sc2 = sb("sc2", [128, 16])
        m2h = sb("m2h", [128, 8, 2])
        sg = sb("sg", [128, 2, 512])
        small = sb("small", [128, 64])

        def C(n):
            return cv[:, CV[n][0]:CV[n][1]]

        def K(n):
            return kc[:, KC[n][0]:KC[n][1]]

        free = {i: None for i in range(8)}
        turn = [0, [0, 1, 2, 3, 4, 5]]

        held = set()

        def bank():
            while True:
                b = turn[1][turn[0] % len(turn[1])]
                turn[0] += 1
                if b not in held:
                    return b

        s_w = [sem(f"w{i}") for i in range(NS)]
        s_hi, s_lo = sem("s_hi"), sem("s_lo")
        raw_free = []
        ws_free = []
        hooks = []

        def fetch(src, n_cols, *first):
            n = len(raw_free)
            dst = ring[:, n % NS, 0:n_cols]
            sp.dma(dst, src, s_w[n % NS], raw_free[n - NS] if n >= NS else None, *first)
            raw_free.append(None)
            return dst, (s_w[n % NS], 16 * (n // NS + 1)), n

        def load(src, nk, nc_):
            dst, t, n = fetch(src, nk * nc_)
            return dst.rearrange("p (k c) -> p k c", k=nk), t, n

        def load_split(src, nk, nc_):
            cols = nk * nc_
            dst, (ws, wv), n = fetch(src, cols)
            m = len(hooks)
            hook = ([], [])
            hooks.append(hook)
            ac.items.append(lambda e: [f(e) for f in hook[0]])
            dv.items.append(lambda e: [f(e) for f in hook[1]])
            at = hooks[max(0, m - AHEAD)]
            hi, lo = WS[:, m % NSP, 0, 0:cols], WS[:, m % NSP, 1, 0:cols]
            gone = ws_free[m - NSP] if m >= NSP else None
            at[0].append(lambda e: e.wait_ge(ws, wv))
            if gone:
                at[0].append(lambda e: e.wait_ge(*gone))
            at[0].append(lambda e: e.copy(hi, dst).then_inc(s_hi, 1))
            at[1].append(lambda e: e.wait_ge(s_hi, m + 1))
            at[1].append(lambda e: e.tensor_tensor(lo, dst, hi.bitcast(F32), ALU.subtract).then_inc(s_lo, 1))
            raw_free[n] = (s_lo, m + 1)
            ws_free.append(None)
            return [v.rearrange("p (k c) -> p k c", k=nk) for v in (hi, lo)], (s_lo, m + 1), m

        def mm3(o, l, r, first, last, *tokens, mark=False):
            for i, (a, b_) in enumerate(((0, 0), (0, 1), (1, 0))):
                f = (lambda e, i=i, a=a, b_=b_: e.matmul(o, l[a], r[b_], start=(first and i == 0),
                                                        stop=(last and i == 2)))
                if (last or mark) and i == 2:
                    return pe.do(f, *tokens)
                pe.quiet(f, *tokens)

        def group(o, pairs, *tokens):
            n = len(pairs)
            for i, (l, r) in enumerate(pairs):
                f = (lambda e, l=l, r=r, i=i: e.matmul(o, l, r, start=(i == 0), stop=(i == n - 1)))
                if i == n - 1:
                    t = pe.do(f, *tokens)
                else:
                    pe.quiet(f, *tokens)
            return t

        def group3(o, ls, rs, *tokens):
            n = len(ls)
            for i in range(n):
                t = mm3(o, ls[i], rs[i], i == 0, i == n - 1, *tokens)
            return t

        def parts(dst, src, *tokens):
            t = dv.do(lambda e: e.tensor_copy(dst[0], src), *tokens)
            return dv.do(lambda e: e.tensor_tensor(dst[1], src, dst[0].bitcast(F32), ALU.subtract), t)

        def Hp(k, a, b_):
            return (Hs[:, 0, k, a:b_], Hs[:, 1, k, a:b_])

        s_c = sem("s_c")
        ncst = [0]

        def const(dst, src):
            sp.dma(dst, src, s_c)
            ncst[0] += 16

        s_x = [sem("s_x0"), sem("s_x1")]
        s_sb = sem("s_sb")
        const(cv[:, :], T["cvec"])
        const(K("ones"), T["kcst"][:, KC["ones"][0]:KC["ones"][1]])
        c_in = (s_c, 32)
        sbc = AB[:, 0:2048].rearrange("p (s k) -> p s k", s=2)
        junk = AB[:, 2048:3072]
        for i, n in enumerate(("c", "cctx")):
            sp.dma(sbc[:, i, :], T[n].partition_broadcast(128), s_sb)
        for k in range(0, 8, 4):
            sp.dma(XT[:, k:k + 4, :], T["xT"][:, k:k + 4, :], s_x[k // 4])
        x_in = [(s_x[0], 16), (s_x[1], 16)]
        s_c2 = sem("s_c2")
        s_c3 = sem("s_c3")
        k_in = (s_c3, 32)

        def const_rest():
            sp.dma(kc[:, 0:KC["ones"][0]], T["kcst"][:, 0:KC["ones"][0]], s_c3)
            sp.dma(kc[:, KC["ones"][1]:KCN], T["kcst"][:, KC["ones"][1]:KCN], s_c3)
            for i, n in enumerate(("vg", "vb", "bs")):
                sp.dma(bc[:, i, :], T[n].partition_broadcast(128), s_c2)
            sp.dma(wsp, T["wsp"], s_c2)
            sp.dma(posi, T["pos"].partition_broadcast(128), s_c2)

        bc = AB[:, 4096:5632].rearrange("p (i c) -> p i c", i=3)
        wsp = AB[:, 5632:6144]
        posi = AB[:, 3328:3584].bitcast(I32)
        c2_in = (s_c2, 80)

        t_sc = ac.do(lambda e: e.activation(sc2[:, :], C("c2"), ACT.Silu), c_in)
        t_sb = ac.do(lambda e: e.activation(AB[:, 0:2048], AB[:, 0:2048], ACT.Silu), (s_sb, 32))
        scv = sc2[:, :].rearrange("p (k s) -> p k s", k=8)
        m_tok = {}
        ada = [2 * 8]
        BA = C("b_ada")

        def ada_dve(idx, j):
            i = 8 * idx + j
            n = 2 if idx < 5 else 1
            dst, tw, s_ = fetch(T["w_adaT"][i], 1024)
            for q in range(n):
                o = dst if q == n - 1 else junk
                t = dv.do(lambda e, q=q, o=o: e.tensor_tensor_reduce(
                    o, dst, sbc[:, q, :], 1.0, 0.0, ALU.mult, ALU.add, Mr[:, i, q:q + 1]), tw, t_sb,
                    t_junk[0] if o is junk else None)
                if o is junk:
                    t_junk[0] = t
            raw_free[s_] = t
            return t

        def ada_tiles(n):
            for _ in range(n):
                i = ada[0]
                if i == 72:
                    return
                ada[0] += 1
                idx, j = divmod(i, 8)
                t = ada_dve(idx, j)
                if j == 7:
                    n_ = 2 if idx < 5 else 1
                    bb = BA[:, 8 * idx:8 * idx + 8].unsqueeze(2).broadcast_to([128, 8, n_])
                    m_tok[idx] = tok_ada[0] = dv.do(lambda e, idx=idx, n_=n_, bb=bb: e.tensor_tensor(
                        M[:, 8 * idx:8 * idx + 8, 0:n_], Mr[:, 8 * idx:8 * idx + 8, 0:n_], bb, ALU.add), t, c_in)

        tok_ada = [None]
        t_junk = [None]

        def ada_pe(j):
            b = 6 + j % 2
            for q, idx in enumerate((1, 0)):
                w, tw, s_ = load(T["w_ada"][8 * idx + j], 8, 128)
                raw_free[s_] = t = group(psum[b][:, 2 * q:2 * q + 2],
                                         [(w[:, k, :], scv[:, k, :]) for k in range(8)], tw, t_sc, free[b])
            for q, idx in enumerate((1, 0)):
                free[b] = dv.do(lambda e, q=q, idx=idx: e.tensor_scalar(
                    M[:, 8 * idx + j, :], psum[b][:, 2 * q:2 * q + 2], BA[:, 8 * idx + j:8 * idx + j + 1], None,
                    ALU.add), t, c_in)
            return free[b]

        def ada_pair(j):
            for idx in (1, 0):
                t = ada_dve(idx, j)
                t = dv.do(lambda e, idx=idx: e.tensor_scalar(
                    M[:, 8 * idx + j, :], Mr[:, 8 * idx + j, :], BA[:, 8 * idx + j:8 * idx + j + 1], None,
                    ALU.add), t, c_in)
            return t

        sqt = [None] * 4
        nsq = [0]
        nR = [0]

        kept = set()

        def half(n, N):
            w = N // 256
            while True:
                n[0] += n[0] % w
                q = n[0] % 4
                n[0] += w
                if n is nR or not kept.intersection(range(q, q + w)):
                    return q, w

        class Squares:

            def __init__(self, N, n, lhs="ones"):
                self.N, self.n, self.lhs, self.i = N, n, lhs, 0

            def add(self, src, tok_, scale=1.0, via=None, gone=None):
                N = self.N
                if self.i == 0:
                    self.q, self.w = half(nsq, N)
                    kept.update(range(self.q, self.q + self.w))
                    self.sum = sqf[:, 256 * self.q:256 * (self.q + self.w)]
                    self.ta = ac.do(lambda e: e.activation(self.sum, src, ACT.Square, scale=scale), tok_,
                                    sqt[self.q:self.q + self.w], c_in)
                else:
                    if via is None:
                        q, w = half(nsq, N)
                        via, gone = sqf[:, 256 * q:256 * (q + w)], sqt[q:q + w]
                    else:
                        q = None
                    ta = ac.do(lambda e: e.activation(via, src, ACT.Square, scale=scale), tok_, gone, c_in)
                    self.ta = po.do(lambda e: e.tensor_tensor(self.sum, self.sum, via, ALU.add), ta, self.ta)
                    if q is not None:
                        sqt[q:q + w] = [self.ta] * w
                self.i += 1
                return self.ta

            def flush(self):
                self.b = b = bank()
                self.t = pe.do(lambda e: e.matmul(psum[b][:, 0:self.N], K(self.lhs), self.sum, start=True,
                                                  stop=True), self.ta, free[b], c_in, self.lhs != "ones" and k_in or None)
                sqt[self.q:self.q + self.w] = [self.t] * self.w
                kept.difference_update(range(self.q, self.q + self.w))

            def root(self, inv, mul=None):
                assert self.i == self.n
                self.flush()
                q, w = half(nR, self.N)
                r = Rf[:, 256 * q:256 * (q + w)]
                src = psum[self.b][:, 0:self.N]
                if mul is None:
                    t1 = dv.do(lambda e: e.tensor_scalar(r, src, inv, EPS, ALU.mult, ALU.add), self.t)
                    free[self.b] = t1
                else:
                    t1 = dv.do(lambda e: e.scalar_tensor_tensor(out=r, in0=src, scalar=inv, in1=mul[0],
                                                                op0=ALU.mult, op1=ALU.mult), self.t, mul[1])
                    free[self.b] = t1
                    t1 = dv.do(lambda e: e.tensor_scalar(r, r, EPS, None, ALU.add), t1)
                t2 = dv.do(lambda e: e.reciprocal(r, r), t1)
                t3 = ac.do(lambda e: e.activation(r, r, ACT.Sqrt), t2)
                return r, t3

        def rms(srcs, N, inv, toks, lhs="ones"):
            a = Squares(N, len(srcs), lhs)
            for s, t in zip(srcs, toks):
                a.add(s, t)
            return a.root(inv)

        ft = [None, None, None]
        nf = [0]

        def modulated(gain, ishift, N, toks, ht_free, root=None):
            for i in (ishift, ishift + 1):
                while i not in m_tok:
                    ada_tiles(1)
            ns = N // 256
            sh, scl = M[:, 8 * ishift:8 * ishift + 8, :], M[:, 8 * ishift + 8:8 * ishift + 16, :]
            tc = dv.do(lambda e: e.scalar_tensor_tensor(
                out=co[:, :, 0:ns], in0=scl[:, :, 0:ns], scalar=1.0,
                in1=C(gain).unsqueeze(2).broadcast_to([128, 8, ns]), op0=ALU.add, op1=ALU.mult),
                m_tok[ishift + 1], m_tok[ishift], c_in)
            r, tr = root() if root else rms([XT[:, k, 0:N] for k in range(8)], N, 1.0 / 1024, toks)
            done, late = [], None

            def rest(k, f, td):
                done.append(parts(Hp(k, 0, N), F[:, f, 0:N], td, ht_free))
                ft[f] = done[-1]

            for k in range(8):
                f = nf[0] % 3
                nf[0] += 1
                for s in range(N // 256):
                    a = slice(256 * s, 256 * s + 256)
                    td = dv.do(lambda e, k=k, s=s, a=a, f=f: e.scalar_tensor_tensor(
                        out=F[:, f, a], in0=XT[:, k, a], scalar=co[:, k, s:s + 1], in1=r[:, a],
                        op0=ALU.mult, op1=ALU.mult), tc, tr, toks[k], ft[f])
                    td = ac.do(lambda e, k=k, s=s, a=a, f=f: e.activation(
                        F[:, f, a], F[:, f, a], ACT.Identity, bias=sh[:, k, s:s + 1]), td)
                if late:
                    rest(*late)
                late = (k, f, td)
            rest(*late)
            return done

        def scaled(gain, srcs, N, toks, rr, dst, *ws):
            r, tr = rr
            return [dv.do(lambda e, k=k: e.scalar_tensor_tensor(
                out=dst(k), in0=srcs[k], scalar=C(gain)[:, k:k + 1], in1=r, op0=ALU.mult, op1=ALU.mult),
                tr, toks[k], *ws) for k in range(len(srcs))]

        def plain(gain, srcs, N, toks, inv, dst, *ws, lhs="ones"):
            return scaled(gain, srcs, N, toks, rms(srcs, N, inv, toks, lhs), dst, *ws)

        def scaled_parts(gain, srcs, N, toks, rr, dst, *ws):
            r, tr = rr
            done = []
            for k in range(len(srcs)):
                f = nf[0] % 3
                nf[0] += 1
                td = dv.do(lambda e, k=k, f=f: e.scalar_tensor_tensor(
                    out=F[:, f, 0:N], in0=srcs[k], scalar=C(gain)[:, k:k + 1], in1=r, op0=ALU.mult,
                    op1=ALU.mult), tr, toks[k], ft[f])
                done.append(parts(dst(k), F[:, f, 0:N], td, *ws))
                ft[f] = done[-1]
            return done

        def project(wsrc, rhs, N, toks, *ws):
            b = bank()
            nk = len(rhs)
            at = 0
            while at < nk:
                n = min(8, nk - at)
                (wh, wl), tw, m = load_split(wsrc[:, at * 128:(at + n) * 128], n, 128)
                for k in range(n):
                    i = at + k
                    t = mm3(psum[b][:, 0:N], (wh[:, k, :], wl[:, k, :]), rhs[i], i == 0, i == nk - 1,
                            tw, free[b], toks[i], *ws, mark=(k == n - 1))
                ws_free[m] = t
                at += n
            return b, t

        sgt = [None, None]

        def ffn(win, wout, N, gain, im, toks, act_free, ht_free, more=(0, 0), root=None, after=None):
            h = root if isinstance(root, list) else modulated(gain, im, N, toks, ht_free, root)
            rounds = [range(0, 22)] if N == 256 else [range(0, 11), range(11, 22)]
            nj = len(rounds[0])
            Ar = AR[:, :].rearrange("p (h k t) -> p h k t", h=2, k=nj)
            tm, new = None, [None] * 8
            for rn, js in enumerate(rounds):
                at = []
                for i, j in enumerate(js):
                    b1, t1 = project(T[win][j], [Hp(k, 0, N) for k in range(8)], N, h)
                    b2, t2 = project(T[win][22 + j], [Hp(k, 0, N) for k in range(8)], N, h)
                    q = j % 2
                    ta = ac.do(lambda e, q=q, b1=b1: e.activation(sg[:, q, 0:N], psum[b1][:, 0:N], ACT.Silu),
                               t1, sgt[q])
                    free[b1] = ta
                    td = dv.do(lambda e, q=q, b2=b2: e.tensor_tensor(
                        sg[:, q, 0:N], sg[:, q, 0:N], psum[b2][:, 0:N], ALU.mult), ta, t2)
                    free[b2] = td
                    sgt[q] = td = parts((Ar[:, 0, i, :], Ar[:, 1, i, :]), sg[:, q, 0:N], td, act_free)
                    at.append(td)
                    ada_tiles(more[0])
                while im + 2 not in m_tok:
                    ada_tiles(1)
                if tm is None:
                    ns = N // 256
                    tm = dv.do(lambda e: e.tensor_scalar(
                        m2h[:, :, 0:ns], M[:, 8 * im + 16:8 * im + 24, 0:ns], 0.5, None, ALU.mult), m_tok[im + 2])
                for d in range(8):
                    b, t = project(T[wout][d][:, 128 * js[0]:128 * js[0] + 128 * nj],
                                   [(Ar[:, 0, k, :], Ar[:, 1, k, :]) for k in range(nj)], N, at)
                    for s in range(N // 256):
                        a = slice(256 * s, 256 * s + 256)
                        td = dv.do(lambda e, d=d, s=s, a=a, b=b: e.scalar_tensor_tensor(
                            out=XT[:, d, a], in0=psum[b][:, a], scalar=m2h[:, d, s:s + 1], in1=XT[:, d, a],
                            op0=ALU.mult, op1=ALU.add), t, tm, new[d])
                    free[b] = td
                    new[d] = td
                    ada_tiles(more[1])
                    if after and rn == len(rounds) - 1:
                        after(d, td)
                act_free = t
            return new, t

        def copy_out(eng, dst, b, src, *tokens):
            if eng is ac:
                t = ac.do(lambda e: e.copy(dst, src), *tokens)
            else:
                t = dv.do(lambda e: e.tensor_copy(dst, src), *tokens)
            free[b] = t
            return t

        dumps = []

        def dump(name, ap, *toks):
            if dbg is not None and name in dbg:
                dumps.append((dbg[name], ap))
                s = sem("dbg_" + name)
                po.dma(dbg[name], ap, s, *toks)
                for q_ in (dv, ac):
                    q_.wait((s, 16))

        acc = []
        a = Squares(512, 8)
        for k in range(8):
            f = k % 3
            ta = a.add(XT[:, k, :], x_in[k // 4], via=F[:, f, :], gone=ft[f])
            ft[f] = ta if k else None
        h1 = [None] * 8
        pend_ = []

        def first_h(j, tm):
            t = dv.do(lambda e: e.scalar_tensor_tensor(
                out=co[:, j, :], in0=M[:, 8 + j, :], scalar=1.0, in1=C("g_ffn1")[:, j:j + 1].broadcast_to([128, 2]),
                op0=ALU.add, op1=ALU.mult), tm)
            f = nf[0] % 3
            nf[0] += 1
            for s in range(2):
                c_ = slice(256 * s, 256 * s + 256)
                td = dv.do(lambda e, s=s, c_=c_: e.scalar_tensor_tensor(
                    out=F[:, f, c_], in0=XT[:, j, c_], scalar=co[:, j, s:s + 1], in1=r1_[:, c_],
                    op0=ALU.mult, op1=ALU.mult), t, tr1, ft[f])
                td = ac.do(lambda e, s=s, c_=c_: e.activation(
                    F[:, f, c_], F[:, f, c_], ACT.Identity, bias=M[:, j, s:s + 1]), td)
            if pend_:
                rest_(*pend_.pop())
            pend_.append((j, f, td))

        def rest_(j, f, td):
            h1[j] = ft[f] = parts(Hp(j, 0, 512), F[:, f, :], td)

        td5 = ada_pair(5)
        td6 = ada_pair(6)
        r1_, tr1 = a.root(1.0 / 1024)
        tp = [ada_pe(0)]
        td7 = ada_pair(7)
        for j, tm in ((0, tp[0]), (5, td5), (6, td6)):
            first_h(j, tm)
        for j in range(1, 5):
            tp.append(ada_pe(j))
            first_h(j, tp[j])
            if j == 2:
                first_h(7, td7)
        rest_(*pend_.pop())
        const_rest()

        def follow(N, n_acc=1):
            def f(d, td):
                if d == 0:
                    acc[:] = [Squares(N, 8) for _ in range(n_acc)]
                acc[0].add(XT[:, d, 0:N], td)
                if n_acc == 2:
                    acc[1].add(XT[:, d, 0:N], td, scale=C("g_fin")[:, d:d + 1])
            return f

        x, t_pe = ffn("f1i", "f1o", 512, "g_ffn1", 0, [x_in] * 8, None, None, more=(2, 1), root=h1,
                      after=follow(512))
        assert ada[0] == 72
        dump("x1", XT[:, :, :], x)
        h = modulated("g_mix", 3, 512, x, t_pe, root=lambda: acc[0].root(1.0 / 1024))

        todo = []

        def fill(n=1):
            for _ in range(n):
                if todo:
                    todo.pop(0)()

        def together(*gens, each=1):
            gens = list(gens)
            while gens:
                for g in list(gens):
                    try:
                        next(g)
                    except StopIteration:
                        gens.remove(g)
                fill(each)

        turn[1] = [0, 1, 2, 3, 4, 5, 6, 7]
        qT = AA[:, 0:1024].rearrange("p (j t) -> p j t", j=4)
        kT = AA[:, 1024:2048].rearrange("p (j t) -> p j t", j=2)
        vN = AA[:, 2048:2560].rearrange("p (j d) -> p j d", j=4)
        gb = AA[:, 2560:3584].rearrange("p (j t) -> p j t", j=4)
        gc = AA[:, 3584:4608].rearrange("p (j t) -> p j t", j=4)
        pz = AA[:, 4608:4608 + 4 * 258].rearrange("p (j t) -> p j t", j=4)
        cs = AA[:, 5640:6664].rearrange("p (j t) -> p j t", j=4)
        aT = AA[:, 6664:7688].rearrange("p (j t) -> p j t", j=4)
        tmp_at = [AA[:, 7688:8200].rearrange("p (j t) -> p j t", j=2)]
        Pb = AA[:, 8200:10248].rearrange("p (j s) -> p j s", j=4)
        PT = AB[:, 0:2048].rearrange("p (j k q) -> p j k q", j=2, k=2 * 2)

        def MX(k):
            return Hp(k, 256, 512)

        aa_free = t_pe
        tok = {}
        H256 = [Hp(k, 0, 256) for k in range(8)]
        H512 = [Hp(k, 0, 512) for k in range(8)]

        def natural(src, dst, ntok, h):
            (wh, wl), tw, m = load_split(src, 8, 128)
            b = bank()
            for i in range(ntok):
                t = group3(psum[b][:, 128 * i:128 * i + 128],
                           [Hp(k, 128 * i, 128 * i + 128) for k in range(8)],
                           [(wh[:, k, :], wl[:, k, :]) for k in range(8)], tw, free[b], h)
            ws_free[m] = t
            return b, t

        for j in range(4):
            b, t = project(T["mi"][j], H256, 256, h)
            tok["q", j] = copy_out(ac, qT[:, j, :], b, psum[b][:, 0:256], t, aa_free)
        for j in range(2):
            b, t = project(T["mi"][4 + j], H512, 512, h)
            tok["k", j] = copy_out(ac, kT[:, j, :], b, psum[b][:, :], t, aa_free)
        b, t = natural(T["mi"][6], None, 4, h)
        tok["v"] = copy_out(ac, vN.rearrange("p j d -> p (j d)"), b, psum[b][:, :], t, aa_free)
        hx_free = t
        tz = po.do(lambda e: e.memset(AA[:, 4608:4608 + 4 * 258], 0.0), aa_free)

        def conv_tile(j, which):
            def f():
                b, t = project(T["mi"][7 + j + 4 * which], H256, 256, h)
                tok["ht"] = t
                if which == 0:
                    tok["gb", j] = copy_out(ac, gb[:, j, :], b, psum[b][:, 0:256], t, aa_free)
                elif which == 1:
                    tok["gc", j] = copy_out(ac, gc[:, j, :], b, psum[b][:, 0:256], t, aa_free)
                else:
                    free[b] = tok["p", j] = dv.do(lambda e: e.tensor_tensor(
                        pz[:, j, 1:257], gc[:, j, :], psum[b][:, 0:256], ALU.mult), t, tok["gc", j], tz)
            return f

        for j in range(4):
            for which in (1, 2, 0):
                todo.append(conv_tile(j, which))

        def rope(dst, src, tin, perm, cos, sin, ti, *ws):
            b = bank()
            tmp = tmp_at[0]
            tp = pe.do(lambda e: e.matmul(psum[b][:, 0:256], K(perm), src, start=True, stop=True), tin, free[b], k_in)
            t1 = dv.do(lambda e: e.tensor_tensor(tmp[:, ti, :], psum[b][:, 0:256], sin, ALU.mult), tp, *ws)
            free[b] = t1
            t2 = dv.do(lambda e: e.tensor_tensor(dst, src, cos, ALU.mult), tp, t1)
            return dv.do(lambda e: e.tensor_tensor(dst, dst, tmp[:, ti, :], ALU.add), t2)

        def head_norm(key, X, gain, N, inv, lhs, rot, ti):
            a = Squares(N, 1, lhs)
            a.add(X, tok[key])
            yield
            rr = a.root(inv)
            yield
            (t,) = scaled(gain, [X], N, [tok[key]], rr, lambda k: X)
            yield
            X_ = X[:, 0:256]
            tok[key] = rope(X_, X_, t, *rot, ti)

        rot1 = ("perm1", K("cos1"), K("sin1"))
        together(head_norm(("q", 0), qT[:, 0, :], "qn", 256, 1.0 / 64, "blk", rot1, 0),
                 head_norm(("k", 0), kT[:, 0, :], "kn", 512, 1.0 / 64, "blk", rot1, 1))
        together(head_norm(("q", 1), qT[:, 1, :], "qn", 256, 1.0 / 64, "blk", rot1, 0),
                 head_norm(("k", 1), kT[:, 1, :], "kn", 512, 1.0 / 64, "blk", rot1, 1))

        def softmax_rows(Sap, Pap, n, scale, *toks):
            c = 4 * (n % 8)
            m, nm, su, ri = (small[:, c + i:c + i + 1] for i in range(4))
            t1 = dv.do(lambda e: e.reduce_max(m, Sap, AX), *toks)
            t2 = dv.do(lambda e: e.tensor_scalar(nm, m, -scale, None, ALU.mult), t1)
            t3 = ac.do(lambda e: e.activation(Pap, Sap, ACT.Exp, bias=nm, scale=scale, accum_out=su), t2, *toks)
            t4 = dv.do(lambda e: e.reciprocal(ri, su), t3)
            t5 = dv.do(lambda e: e.tensor_scalar(Pap, Pap, ri, None, ALU.mult), t4)
            return t5, t3

        p_use = [None] * 4
        pt_use = [tok_ada[0], tok_ada[0]]
        n_sm = [0]

        def attention(heads, score, nk, P_, PT_, values, finish):
            items = [(hd, i) for hd in heads for i in range(2)]
            state = {}

            def front(n):
                hd, i = items[n]
                q = n_sm[0] % 4
                state[n] = (q, score(hd, i, P_[:, q, :], n_sm[0], p_use[q]))
                n_sm[0] += 1

            def back(n):
                hd, i = items[n]
                q, tp = state[n]
                b = bank()
                for k in range(nk):
                    t = pe.do(lambda e, k=k: e.transpose(
                        psum[b][:, 128 * k:128 * k + 128], P_[:, q, 128 * k:128 * k + 128], K("ident")),
                        tp, free[b])
                p_use[q] = t
                state["c", hd, i] = copy_out(
                    ac, PT_[:, hd % 2, :, 128 * i:128 * i + 128], b,
                    psum[b][:, 0:128 * nk].rearrange("p (k q) -> p k q", k=nk), t, pt_use[hd % 2])

            def pv(hd):
                pt_use[hd % 2] = values(hd, [state["c", hd, 0], state["c", hd, 1]])
                finish(hd, pt_use[hd % 2])

            N_ = len(items)
            for n in range(N_ + 3):
                if n < N_:
                    front(n)
                if 2 <= n < N_ + 2:
                    back(n - 2)
                if n >= 4 and n % 2 == 0:
                    pv(items[n - 4][0])
                if n == N_ + 2 and N_ % 2 == 0:
                    pass
                yield

        def score1(hd, i, P_, n, pu):
            o, j, kv = 64 * (hd % 2), hd // 2, hd // 4
            b = bank()
            t = pe.do(lambda e: e.matmul(
                psum[b][:, :], qT[o:o + 64, j, 128 * i:128 * i + 128], kT[o:o + 64, kv, :],
                start=True, stop=True), tok["q", j], tok["k", kv], free[b])
            tp, rd = softmax_rows(psum[b][:, :], P_, n, 0.125, t, pu, aa_free)
            free[b] = rd
            return tp

        bo = [None]

        def values1(hd, ts):
            o, kv = 64 * (hd % 2), hd // 4
            if hd % 2 == 0:
                bo[0] = bank()
                held.add(bo[0])
            b = bo[0]
            return group(psum[b][o:o + 64, 0:256],
                         [(vN[:, k, 64 * kv:64 * kv + 64], PT[:, hd % 2, k, :]) for k in range(4)],
                         ts, tok["v"], free[b])

        def finish1(hd, t):
            if hd % 2:
                b = bo[0]
                held.discard(b)
                tok["a", hd // 2] = copy_out(ac, aT[:, hd // 2, :], b, psum[b][:, 0:256], t)

        together(attention([0, 1, 2, 3], score1, 4, Pb, PT, values1, finish1),
                 head_norm(("q", 2), qT[:, 2, :], "qn", 256, 1.0 / 64, "blk", rot1, 0),
                 head_norm(("q", 3), qT[:, 3, :], "qn", 256, 1.0 / 64, "blk", rot1, 1))
        cvw = C("conv")

        def conv(j):
            t = dv.do(lambda e: e.tensor_scalar(cs[:, j, :], pz[:, j, 0:256], cvw[:, 3 * j:3 * j + 1], None,
                                                ALU.mult), tok["p", j])
            yield
            for i in (1, 2):
                t = dv.do(lambda e, i=i: e.scalar_tensor_tensor(
                    out=cs[:, j, :], in0=pz[:, j, i:i + 256], scalar=cvw[:, 3 * j + i:3 * j + i + 1],
                    in1=cs[:, j, :], op0=ALU.mult, op1=ALU.add), t)
            yield
            tok["c", j] = dv.do(lambda e: e.tensor_tensor(cs[:, j, :], cs[:, j, :], gb[:, j, :], ALU.mult),
                                t, tok["gb", j])

        fill(3)

        def convs():
            for j in range(4):
                while ("gb", j) not in tok:
                    fill(1)
                yield from conv(j)

        together(attention([4, 5, 6, 7], score1, 4, Pb, PT, values1, finish1), convs())
        while todo:
            fill(1)
        a1, a2 = Squares(256, 4), Squares(256, 4)
        for j in range(4):
            a2.add(cs[:, j, :], tok["c", j])
        r2 = a2.root(1.0 / 512)
        for j in range(4):
            a1.add(aT[:, j, :], tok["a", j])
        cb = scaled_parts("con", [cs[:, j, :] for j in range(4)], 256, [tok["c", j] for j in range(4)], r2,
                          lambda k: MX(4 + k), hx_free)
        r1 = a1.root(1.0 / 512)
        ca = scaled_parts("aon", [aT[:, j, :] for j in range(4)], 256, [tok["a", j] for j in range(4)], r1,
                          lambda k: MX(k), hx_free)
        nx = []
        fol = follow(256)
        for d in range(8):
            b, t = project(T["mo"][d], [MX(4 + k) for k in range(4)] + [MX(k) for k in range(4)], 256, cb + ca)
            free[b] = td = dv.do(lambda e, d=d, b=b: e.scalar_tensor_tensor(
                out=XT[:, d, 0:256], in0=psum[b][:, 0:256], scalar=M[:, 40 + d, 0:1], in1=XT[:, d, 0:256],
                op0=ALU.mult, op1=ALU.add), t, m_tok[5])
            nx.append(td)
            fol(d, td)
        dump("x2", XT[:, :, :], nx)
        x, t_pe = ffn("f2i", "f2o", 256, "g_ffn2", 6, nx, t, tok["ht"],
                      root=lambda: acc[0].root(1.0 / 1024), after=follow(256, 2))

        ra = acc[0].root(1.0 / 1024)
        rsq = F[:, 0, 0:256]
        t = dv.do(lambda e: e.tensor_tensor(rsq, ra[0], ra[0], ALU.mult), ra[1], ft[0])
        rb = acc[1].root(1.0 / 1024, (rsq, t))
        ft[0] = t
        xs = [XT[:, k, 0:256] for k in range(8)]
        x = scaled("g_fin", xs, 256, x, ra, lambda k: XT[:, k, 0:256])
        nf[0] = 0
        ft[0] = x[7]
        dump("x3", XT[:, :, :], x)
        h = scaled_parts("g_n1", xs, 256, x, rb, lambda k: Hp(k, 0, 256), t_pe)

        uT = AA[:, 0:1024].rearrange("p (j t) -> p j t", j=4)
        vA = AA[:, 1024:2048].rearrange("p (c d) -> p c d", c=2)
        q2 = AA[:, 2048:3072].rearrange("p (j t) -> p j t", j=4)
        ck = AA[:, 3072:3584].rearrange("p (j t) -> p j t", j=2)
        qi = AA[:, 3584:4096].rearrange("p (j t) -> p j t", j=2)
        ki = AA[:, 4096:4352]
        k2 = AA[:, 4352:4608]
        v2 = AA[:, 4608:4864].rearrange("p (j d) -> p j d", j=2)
        wi = AA[:, 4864:4872].rearrange("p (t h) -> p t h", t=2)
        relu = AA[:, 4872:5384].rearrange("p (j t) -> p j t", j=2)
        scr = AA[:, 5384:5896].rearrange("p (i s) -> p i s", i=2)
        wk = AA[:, 5896:6408].rearrange("p (i s) -> p i s", i=2)
        sel = AA[:, 6408:6920].rearrange("p (i s) -> p i s", i=2)
        tmp_at[0] = AA[:, 6920:7432].rearrange("p (j t) -> p j t", j=2)
        mx = AA[:, 7432:7560].rearrange("p (i s) -> p i s", i=2)
        onesr = AA[:, 7560:7816]
        P2 = AA[:, 7816:8840].rearrange("p (i s) -> p i s", i=4)
        PT2 = AB[:, 0:1024].rearrange("p (j k q) -> p j k q", j=2, k=2)
        rt = AB[:, 2048:3328].rearrange("p (j t) -> p j t", j=5)
        ang = AB[:, 3584:3840]
        posf = AB[:, 3840:4096]
        gt = sgx = XT[:, :, 256:512]
        ya_p = [(Hs[:, 0, k, 256:512], Hs[:, 1, k, 256:512]) for k in range(4)]
        yb_p = [(Hs[:, 0, 4 + k, 256:512], Hs[:, 1, 4 + k, 256:512]) for k in range(4)]
        aa_free = t_pe
        st = small[:, 32:48]

        TWO_PI = 2 * np.pi
        C1 = 6.28125
        C2 = float(np.round((TWO_PI - C1) * 2 ** 22) / 2 ** 22)
        C3 = float(np.float32(TWO_PI - C1 - C2))
        MAGIC = 12582912.0
        PI_ = 3.1415925

        def tables():
            t0 = dv.do(lambda e: e.tensor_copy(posf, posi), c2_in)
            for i, inv in enumerate(("inv3", "inv2")):
                o = 2 - 2 * i
                sn, cn, nn = rt[:, o, :], rt[:, o + 1, :], rt[:, 4, :]
                t1 = dv.do(lambda e, inv=inv: e.tensor_scalar(ang, posf, K(inv), None, ALU.mult), t0, c_in)
                t1 = dv.do(lambda e, nn=nn: e.tensor_scalar(nn, ang, 1.0 / TWO_PI, MAGIC, ALU.mult, ALU.add), t1)
                t1 = dv.do(lambda e, nn=nn: e.tensor_scalar(nn, nn, MAGIC, None, ALU.subtract), t1)
                for cc in (C1, C2, C3):
                    t1 = dv.do(lambda e, nn=nn, cc=cc: e.scalar_tensor_tensor(
                        out=ang, in0=nn, scalar=-cc, in1=ang, op0=ALU.mult, op1=ALU.add), t1)
                yield
                t2 = dv.do(lambda e, cn=cn: e.tensor_scalar(cn, ang, np.pi / 2, None, ALU.add), t1)
                t3 = dv.do(lambda e, cn=cn, nn=nn: e.tensor_scalar(nn, cn, PI_, TWO_PI, ALU.is_gt, ALU.mult), t2)
                t3 = dv.do(lambda e, cn=cn, nn=nn: e.tensor_tensor(cn, cn, nn, ALU.subtract), t3)
                t3 = dv.do(lambda e, cn=cn: e.tensor_scalar(cn, cn, -PI_, PI_, ALU.max, ALU.min), t3)
                t4 = dv.do(lambda e, sn=sn: e.tensor_scalar(sn, ang, -PI_, PI_, ALU.max, ALU.min), t1)
                t0 = tok["rt", o] = ac.do(lambda e, o=o: e.activation(
                    rt[:, o:o + 2, :], rt[:, o:o + 2, :], ACT.Sin), t3, t4)
                yield

        def proj2(key, n, dst, func=None):
            def f():
                b, t = project(T["w2"][n], H256, 256, h)
                tok["ht"] = t
                if func is None:
                    tok[key] = copy_out(ac, dst, b, psum[b][:, 0:256], t, aa_free)
                else:
                    tok[key] = free[b] = ac.do(lambda e: e.activation(dst, psum[b][:, 0:256], func), t, aa_free,
                                               nx[7])
            return f

        def vtile(j):
            def f():
                b, t = natural(T["w2"][9 + j], None, 2, h)
                tok["ht"] = t
                tok["vA", j] = free[b] = ac.do(lambda e: e.activation(
                    vA[:, :, 128 * j:128 * j + 128], psum[b][:, 0:256].rearrange("p (c d) -> p c d", c=2),
                    ACT.Gelu_apprx_tanh), t, aa_free)
            return f

        todo += [proj2(("ck", j), 3 + j, ck[:, j, :]) for j in range(2)]
        todo += [proj2(("q2", j), 5 + j, q2[:, j, :]) for j in range(4)]
        todo += [vtile(j) for j in range(4)]
        todo += [proj2(("u", j), 13 + j, uT[:, j, :], ACT.Gelu_apprx_tanh) for j in range(4)]
        for j in range(2):
            proj2(("qi", j), j, qi[:, j, :])()
        proj2("ki", 2, ki)()
        wp, tw, m = load_split(T["w2w"], 8, 4)
        b = bank()
        for i in range(2):
            t = group3(psum[b][:, 4 * i:4 * i + 4], [Hp(k, 128 * i, 128 * i + 128) for k in range(8)],
                       [(wp[0][:, k, :], wp[1][:, k, :]) for k in range(8)], tw, free[b], h)
        ws_free[m] = t
        tok["wi"] = free[b] = dv.do(lambda e, b=b: e.tensor_scalar(
            wi.rearrange("p t h -> p (t h)"), psum[b][:, 0:8], 0.5, None, ALU.mult), t, aa_free)

        def rope2(key, X, perm, o, ti):
            yield
            tok[key] = rope(X, X, tok[key], perm, rt[:, o + 1, :], rt[:, o, :], ti, tok["rt", o], aa_free)

        together(tables())
        together(rope2(("qi", 0), qi[:, 0, :], "perm3", 2, 0), rope2(("qi", 1), qi[:, 1, :], "perm3", 2, 1))
        together(rope2("ki", ki, "perm3", 2, 0))
        t_or = dv.do(lambda e: e.memset(onesr, 1.0), aa_free)

        def choose(i):
            t = None
            for hd in range(4):
                o = 64 * (hd % 2)
                b = bank()
                tp = pe.do(lambda e, b=b, o=o, hd=hd: e.matmul(
                    psum[b][:, 0:256], qi[o:o + 64, hd // 2, 128 * i:128 * i + 128], ki[o:o + 64, :],
                    start=True, stop=True), tok["qi", hd // 2], tok["ki"], free[b])
                ta = free[b] = ac.do(lambda e, b=b, hd=hd: e.activation(
                    relu[:, i, :], psum[b][:, 0:256], ACT.Relu, scale=0.125), tp, t)
                if hd == 0:
                    t = dv.do(lambda e: e.tensor_scalar(scr[:, i, :], relu[:, i, :], wi[:, i, 0:1], None,
                                                        ALU.mult), ta, tok["wi"])
                else:
                    t = dv.do(lambda e, hd=hd: e.scalar_tensor_tensor(
                        out=scr[:, i, :], in0=relu[:, i, :], scalar=wi[:, i, hd:hd + 1], in1=scr[:, i, :],
                        op0=ALU.mult, op1=ALU.add), ta, t)
                yield
            cap = K("cap")[:, 256 * i:256 * i + 256]
            t = dv.do(lambda e: e.tensor_tensor(scr[:, i, :], scr[:, i, :], cap, ALU.min), t)
            src = scr[:, i, :]
            for r in range(8):
                t = dv.do(lambda e, r=r, src=src: e.max(mx[:, i, 8 * r:8 * r + 8], src), t)
                if r < 7:
                    t = dv.do(lambda e, r=r, src=src: e.match_replace(
                        wk[:, i, :], mx[:, i, 8 * r:8 * r + 8], src, -3e38), t)
                    src = wk[:, i, :]
                if r % 2:
                    yield
            th = mx[:, i, 63:64]
            sl, w_ = sel[:, i, :], wk[:, i, :]
            t = dv.do(lambda e: e.tensor_scalar(sl, scr[:, i, :], th, None, ALU.is_gt), t)
            t = dv.do(lambda e: e.reduce_sum(mx[:, i, 0:1], sl, AX), t)
            t = dv.do(lambda e: e.tensor_scalar(mx[:, i, 1:2], mx[:, i, 0:1], -1.0, 64.0, ALU.mult, ALU.add), t)
            t = dv.do(lambda e: e.tensor_scalar(scr[:, i, :], scr[:, i, :], th, None, ALU.is_equal), t)
            t = dv.do(lambda e: e.tensor_tensor_scan(w_, onesr, scr[:, i, :], 0.0, ALU.mult, ALU.add), t, t_or)
            yield
            t = dv.do(lambda e: e.scalar_tensor_tensor(out=w_, in0=w_, scalar=mx[:, i, 1:2], in1=scr[:, i, :],
                                                       op0=ALU.is_le, op1=ALU.mult), t)
            t = dv.do(lambda e: e.tensor_tensor(sl, sl, w_, ALU.add), t)
            t = dv.do(lambda e: e.tensor_scalar(sl, sl, 2 * BIG, -BIG, ALU.mult, ALU.add), t)
            tok["sel", i] = dv.do(lambda e: e.tensor_tensor(sl, sl, cap, ALU.min), t)

        def keys():
            while ("ck", 1) not in tok:
                fill(1)
            cks = [ck[:, j, :] for j in range(2)]
            a = Squares(256, 2)
            for j in range(2):
                a.add(cks[j], tok["ck", j])
            yield
            rr = a.root(1.0 / 256)
            yield
            c1 = scaled("kvn", cks, 256, [tok["ck", j] for j in range(2)], rr, lambda k: cks[k])
            wk_, tw, s = load(T["wuk"][0], 2, 128)
            wv_, tw2, s2 = load(T["wuv"][0], 2, 128)
            yield
            b = bank()
            raw_free[s] = t = group(psum[b][:, 0:256], [(wk_[:, k, :], cks[k]) for k in range(2)], tw, free[b], c1)
            tok["k2"] = copy_out(ac, k2, b, psum[b][:, 0:256], t, aa_free)
            b = bank()
            for i in range(2):
                t = group(psum[b][:, 128 * i:128 * i + 128],
                          [(ck[:, k, 128 * i:128 * i + 128], wv_[:, k, :]) for k in range(2)], tw2, free[b], c1)
            raw_free[s2] = t
            tok["v2"] = copy_out(ac, v2.rearrange("p j d -> p (j d)"), b, psum[b][:, 0:256], t, aa_free)
            yield
            yield from head_norm2("k2", k2, "kn2", 0)

        def head_norm2(key, X, gain, ti):
            while key not in tok:
                fill(1)
            a = Squares(256, 1)
            a.add(X, tok[key])
            yield
            rr = a.root(1.0 / 128)
            yield
            (t,) = scaled(gain, [X], 256, [tok[key]], rr, lambda k: X)
            yield
            tok[key] = rope(X, X, t, "perm2", rt[:, 1, :], rt[:, 0, :], ti, tok["rt", 0])

        together(choose(0), keys())
        together(choose(1), head_norm2(("q2", 0), q2[:, 0, :], "qn2", 0), head_norm2(("q2", 1), q2[:, 1, :], "qn2", 1))
        todo += [proj2(("g", j), 17 + j, sgx[:, j, :], ACT.Sigmoid) for j in range(8)]
        g1 = AA[:, 8840:10888].rearrange("p (j t) -> p j t", j=8)
        todo += [proj2(("g", 8 + j), 25 + j, g1[:, j, :], ACT.Sigmoid) for j in range(8)]

        S2 = 128 ** -0.5

        def score2(hd, i, P_, n, pu):
            b = bank()
            t = pe.do(lambda e: e.matmul(psum[b][:, 0:256], q2[:, hd, 128 * i:128 * i + 128], k2,
                                         start=True, stop=True), tok["q2", hd], tok["k2"], free[b])
            t = free[b] = dv.do(lambda e: e.scalar_tensor_tensor(
                out=P_, in0=psum[b][:, 0:256], scalar=S2, in1=sel[:, i, :], op0=ALU.mult, op1=ALU.min),
                t, tok["sel", i], pu, aa_free)
            return softmax_rows(P_, P_, n, 1.0, t)[0]

        def values2(hd, ts):
            bo[0] = b = bank()
            return group(psum[b][:, 0:256], [(v2[:, k, :], PT2[:, hd % 2, k, :]) for k in range(2)],
                         ts, tok["v2"], free[b])

        def finish2(hd, t):
            b = bo[0]
            tok["yb", hd] = free[b] = parts(yb_p[hd], psum[b][:, 0:256], t, nx)

        tw_ = po.do(lambda e: e.affine_select(
            wsp.rearrange("p (g t) -> p g t", g=4), wsp.rearrange("p (g t) -> p g t", g=4),
            [[0, 4], [1, 128]], ALU.is_ge, 0.0, base=0, channel_multiplier=-1), c2_in)

        def gated(c):
            while ("u", 3) not in tok:
                fill(1)
            s_ = st[:, 8 * c:8 * c + 8]
            bn = mx[:, c, 8:14]
            v = vA[:, c, :]
            t = dv.do(lambda e: e.bn_stats(bn, v), [tok["vA", j] for j in range(4)], tok["sel", 0], tok["sel", 1])
            t = dv.do(lambda e: e.bn_aggr(s_[:, 0:2], bn), t)
            t = dv.do(lambda e: e.tensor_scalar(s_[:, 2:3], s_[:, 1:2], EPS, None, ALU.add), t)
            t = dv.do(lambda e: e.reciprocal(s_[:, 3:4], s_[:, 2:3]), t)
            t = ac.do(lambda e: e.activation(s_[:, 4:5], s_[:, 3:4], ACT.Sqrt), t)
            yield
            t = dv.do(lambda e: e.tensor_scalar(v, v, s_[:, 0:1], s_[:, 4:5], ALU.subtract, ALU.mult), t)
            t = dv.do(lambda e: e.tensor_tensor(v, v, bc[:, 0, :], ALU.mult), t, c2_in)
            t = dv.do(lambda e: e.tensor_tensor(v, v, bc[:, 1, :], ALU.add), t)
            yield
            b = bank()
            for g in range(4):
                tp = pe.do(lambda e, g=g: e.matmul(
                    psum[b][:, 128 * g:128 * g + 128], vA[:, c, 128 * g:128 * g + 128],
                    wsp[:, 128 * g:128 * g + 128], start=True, stop=True), t, tw_, free[b])
            t = free[b] = dv.do(lambda e: e.tensor_tensor(sg[:, c, :], psum[b][:, :], bc[:, 2, :], ALU.add), tp,
                                sgt[0], sgt[1])
            yield
            t = dv.do(lambda e: e.tensor_tensor(
                sg[:, c, :].rearrange("p (g t) -> p g t", g=4), sg[:, c, :].rearrange("p (g t) -> p g t", g=4),
                uT[:, :, 128 * c:128 * c + 128], ALU.mult), t, [tok["u", j] for j in range(4)])
            tok["ya", c] = parts((Hs[:, 0, 0:4, 256 + 128 * c:384 + 128 * c], Hs[:, 1, 0:4, 256 + 128 * c:384 + 128 * c]),
                                 sg[:, c, :].rearrange("p (g t) -> p g t", g=4), t, nx)

        together(attention([0, 1], score2, 2, P2, PT2, values2, finish2),
                 head_norm2(("q2", 2), q2[:, 2, :], "qn2", 0), head_norm2(("q2", 3), q2[:, 3, :], "qn2", 1))
        together(attention([2, 3], score2, 2, P2, PT2, values2, finish2), gated(0), gated(1))
        while todo:
            fill(1)

        tya = [[tok["ya", 0], tok["ya", 1]]] * 4
        tyb = [tok["yb", k] for k in range(4)]
        mgp = AR[:, 0:4096].rearrange("p (h j t) -> p h j t", h=2, j=8)
        tm = []
        for d in range(8):
            b1, t1 = project(T["wa"][d], ya_p, 256, tya)
            b2, t2 = project(T["wb"][d], yb_p, 256, tyb)
            f = nf[0] % 3
            nf[0] += 1
            t1 = free[b1] = dv.do(lambda e, d=d, b1=b1, f=f: e.tensor_tensor(
                F[:, f, 0:256], sgx[:, d, :], psum[b1][:, 0:256], ALU.mult), t1, tok["g", d], ft[f])
            t2 = free[b2] = dv.do(lambda e, d=d, b2=b2, f=f: e.tensor_tensor(
                F[:, f, 256:512], g1[:, d, :], psum[b2][:, 0:256], ALU.mult), t2, tok["g", 8 + d], ft[f])
            t1 = dv.do(lambda e, f=f: e.tensor_tensor(F[:, f, 0:256], F[:, f, 0:256], F[:, f, 256:512], ALU.add),
                       t1, t2)
            ft[f] = t1 = parts((mgp[:, 0, d, :], mgp[:, 1, d, :]), F[:, f, 0:256], t1, tyb, tya[0], pt_use)
            tm.append(t1)
        x2 = []
        fol = follow(256)
        for d in range(8):
            b, t = project(T["wo"][d], [(mgp[:, 0, k, :], mgp[:, 1, k, :]) for k in range(8)], 256, tm)
            free[b] = td = dv.do(lambda e, d=d, b=b: e.tensor_tensor(
                XT[:, d, 0:256], XT[:, d, 0:256], psum[b][:, 0:256], ALU.add), t, x)
            x2.append(td)
            fol(d, td)
        wo_done = t
        dump("h1", XT[:, :, :], x2)

        ht_used = tok["ht"]
        skw = XT[:, :, 256:512].rearrange("p k (a n) -> p k a n", a=2)
        s_k = sem("s_k")
        sp.dma(skw, T["sk"], s_k, tm)
        hN = AA[:, 0:2048].rearrange("p (t d) -> p t d", t=2)
        yN = AA[:, 2048:4096].rearrange("p (t d) -> p t d", t=2)
        hF = AA[:, 4096:6144].rearrange("p (k t) -> p k t", k=8)
        r, tr = acc[0].root(1.0 / 1024)
        Hq = HR[:, 0:4096].rearrange("p (h k t) -> p h k t", h=2, k=8)
        H256 = [(Hq[:, 0, k, :], Hq[:, 1, k, :]) for k in range(8)]
        h, hf = [], []
        for k in range(8):
            t = dv.do(lambda e, k=k: e.scalar_tensor_tensor(
                out=hF[:, k, :], in0=xs[k], scalar=C("g_n2")[:, k:k + 1], in1=r, op0=ALU.mult, op1=ALU.mult),
                tr, x2[k], tyb, tya[0])
            hf.append(t)
            h.append(parts(H256[k], hF[:, k, :], t, ht_used, tm))
        turn[1] = [0, 1, 2, 3]
        turn[0] = 0

        def turned(dst, srcs, toks, t_, half):
            def f():
                b = bank()
                for k in range(4):
                    kk = 4 * half + k
                    t = pe.do(lambda e, k=k, kk=kk: e.transpose(
                        psum[b][:, 128 * k:128 * k + 128], srcs[kk][:, 128 * t_:128 * t_ + 128], K("ident")),
                        toks[kk], free[b])
                tok["n", dst is hN, t_, half] = copy_out(
                    ac, dst[:, t_, 512 * half:512 * half + 512], b, psum[b][:, :], t, wo_done)
            return f

        hFs = [hF[:, k, :] for k in range(8)]
        qp = AB[:, 0:4096].rearrange("p (j t) -> p j t", j=16)
        idx = AB[:, 4096:4352].bitcast(U32).rearrange("p (a b) -> p a b", a=2)
        gate = AB[:, 4352:4608].rearrange("p (a b) -> p a b", a=2)
        av = AB[:, 4608:4864].rearrange("p (a b) -> p a b", a=2)
        D = F[:, :, :].rearrange("p a b -> p (a b)")[:, 0:1024].rearrange("p (s c) -> p s c", s=8)
        at = [8192]

        def take(*shape, dt=F32):
            n = int(np.prod(shape))
            a = AA[:, at[0]:at[0] + n]
            at[0] += n
            assert at[0] <= 11264
            if dt is not F32:
                a = a.bitcast(dt)
            return a.rearrange("p (a b) -> p a b", a=shape[0]) if len(shape) == 2 else a

        sub = take(4, 256)
        wk3 = take(128)
        top = take(2, 16)
        topi = take(2, 16, dt=U32)
        topf = take(2, 16)
        cand = take(2, 256)
        best = take(16, 16)
        bpos = take(16, dt=U32)
        ij = take(2, 16, dt=U32)
        ijf = take(2, 16)
        oh = take(512)
        isel = take(2, 16)
        ties = [tm, x2, list(pt_use), tyb]
        tg = {}
        sub_use = [None] * 4
        nsub = [0]

        def queries(hd):
            for j in (2 * hd, 2 * hd + 1):
                b, t = project(T["wq"][j], H256, 256, h)
                tok["qp", j] = copy_out(ac, qp[:, j, :], b, psum[b][:, 0:256], t, ties, c2_in, tya[0])
            tok["wq"] = t

        def route(t_, hd):
            if ("qp", 2 * hd) not in tok:
                queries(hd)
            u = nsub[0] % 4
            nsub[0] += 1
            b = bank()
            for p in range(2):
                j = 2 * hd + p
                tp = pe.do(lambda e, p=p, j=j: e.matmul(
                    psum[b][:, 128 * p:128 * p + 128], qp[:, j, 128 * t_:128 * t_ + 128], skw[:, j // 2, j % 2, :],
                    start=True, stop=True), tok["qp", j], (s_k, 16), free[b])
            ts = copy_out(ac, sub[:, u, :], b, psum[b][:, 0:256], tp, sub_use[u], ties)
            yield
            for p in range(2):
                s_ = sub[:, u, 128 * p:128 * p + 128]
                t = dv.do(lambda e, p=p, s_=s_: e.max(top[:, p, 0:8], s_), ts)
                dv.do(lambda e, p=p, s_=s_: e.max_index(topi[:, p, 0:8], top[:, p, 0:8], s_), t)
                t = dv.do(lambda e, p=p, s_=s_: e.match_replace(wk3, top[:, p, 0:8], s_, -3e38), t)
                t = dv.do(lambda e, p=p: e.max(top[:, p, 8:16], wk3), t)
                sub_use[u] = t = dv.do(lambda e, p=p: e.max_index(topi[:, p, 8:16], top[:, p, 8:16], wk3), t)
            yield
            a = top[:, 0, :].unsqueeze(2).broadcast_to([128, 16, 16])
            c_ = top[:, 1, :].unsqueeze(1).broadcast_to([128, 16, 16])
            cd, c2_, bs_ = cand[:, 0, :], cand[:, 1, :], best[:, 8 * t_ + hd, :]
            t = dv.do(lambda e: e.tensor_tensor(cd.rearrange("p (i j) -> p i j", i=16), a, c_, ALU.add), t)
            t = dv.do(lambda e: e.max(bs_[:, 0:8], cd), t)
            dv.do(lambda e: e.max_index(bpos[:, 0:8], bs_[:, 0:8], cd), t)
            t = dv.do(lambda e: e.match_replace(c2_, bs_[:, 0:8], cd, -3e38), t)
            t = dv.do(lambda e: e.max(bs_[:, 8:16], c2_), t)
            t = dv.do(lambda e: e.max_index(bpos[:, 8:16], bs_[:, 8:16], c2_), t)
            dv.do(lambda e: e.tensor_scalar(ij[:, 0, :], bpos, 4, None, ALU.logical_shift_right), t)
            t = dv.do(lambda e: e.tensor_scalar(ij[:, 1, :], bpos, 15, None, ALU.bitwise_and), t)
            yield
            t = dv.do(lambda e: e.tensor_copy(ijf, ij), t)
            t = dv.do(lambda e: e.tensor_copy(topf, topi), t)
            oh3 = oh.rearrange("p (k i) -> p k i", i=16)
            oh4 = oh.rearrange("p (q k i) -> p q k i", q=2, k=16)
            f3 = ijf.rearrange("p q k -> p (q k)").unsqueeze(2).broadcast_to([128, 32, 16])
            io = K("iota").unsqueeze(1).broadcast_to([128, 32, 16])
            v4 = topf.unsqueeze(2).broadcast_to([128, 2, 16, 16])
            t = dv.do(lambda e: e.tensor_tensor(oh3, f3, io, ALU.is_equal), t)
            t = dv.do(lambda e: e.tensor_tensor(oh4, oh4, v4, ALU.mult), t)
            t = dv.do(lambda e: e.reduce_sum(isel.rearrange("p q k -> p (q k)"), oh3, AX), t)
            t = dv.do(lambda e: e.scalar_tensor_tensor(
                out=isel[:, 0, :], in0=isel[:, 0, :], scalar=128.0, in1=isel[:, 1, :], op0=ALU.mult,
                op1=ALU.add), t)
            tok["idx", t_, hd] = dv.do(lambda e: e.tensor_copy(idx[:, t_, 16 * hd:16 * hd + 16], isel[:, 0, :]), t)
            c = 16 + 4 * (hd % 4)
            nm, su, ri = (small[:, 32 + c + i:33 + c + i] for i in range(3))
            gg = gate[:, t_, 16 * hd:16 * hd + 16]
            t = dv.do(lambda e: e.tensor_scalar(nm, bs_[:, 0:1], -1.0, None, ALU.mult), t)
            t = ac.do(lambda e: e.activation(gg, bs_, ACT.Exp, bias=nm, accum_out=su), t)
            yield
            t = dv.do(lambda e: e.reciprocal(ri, su), t)
            tg[t_, hd] = dv.do(lambda e: e.tensor_scalar(gg, gg, ri, None, ALU.mult), t)

        def run(g):
            for _ in g:
                pass

        queries(0)
        for t_, half_ in ((0, 0), (0, 1)):
            turned(hN, hFs, hf, t_, half_)()
        late = [turned(yN, xs, x2, t_, half_) for t_ in range(2) for half_ in range(2)]
        early = [turned(hN, hFs, hf, 1, half_) for half_ in range(2)]
        first = route(0, 0)
        next(first)
        for hd in range(1, 8):
            queries(hd)
            next(first, None)
        tok["wq_all"] = [tok["wq"], (s_lo, len(hooks)), (s_hi, len(hooks))]
        for f in early + late:
            f()
        hf_free = [tok["n", True, 1, 0], tok["n", True, 1, 1]]
        work = [first] + [route(t_, hd) for t_ in range(2) for hd in range(8)][1:]

        def more_work():
            while work:
                try:
                    next(work[0])
                    return
                except StopIteration:
                    work.pop(0)

        gbuf = [(AA[:, 6144:7168], ties), (AA[:, 7168:8192], ties),
                (AA[:, 4096:5120], [ties, hf_free, h]), (AA[:, 5120:6144], [ties, hf_free, h])]
        gbuf += [(HF[:, 4096 + 1024 * i:5120 + 1024 * i], [tm, x2]) for i in range(4)]
        gbuf += [(sg[:, :, :].rearrange("p a b -> p (a b)"), [tm, sgt]), (sqf[:, :], [x2, h, tr]), (Rf[:, :], h)]
        NE = len(gbuf)
        gbuf += [(ring[:, i, :], "wq") for i in range(NS)]
        gbuf += [(r_[:, 1024 * i:1024 * i + 1024], "wq") for r_, n in ((WF, 8), (HF, 4)) for i in range(n)]
        NB = len(gbuf)
        s_g = [sem(f"g{i}") for i in range(NB)]
        g_use = {}
        order = list(range(NB))

        def gather(tab, t_, k):
            n = order.pop(0)
            buf, start = gbuf[n]
            cnt, before = g_use.get(n, (0, None))
            po.wait(tok["wq_all"] if start == "wq" else start, before, tok["idx", t_, k // 16])
            po.items.append(lambda e: e.indirect_dma_start(
                buf, None, T[tab], bass.IndirectOffsetOnAxis(ap=idx[:, t_, k:k + 1], axis=0)
            ).then_inc(s_g[n], 16))
            g_use[n] = (cnt + 1, "due")
            return buf, (s_g[n], 16 * (cnt + 1)), n

        def let_go(n, t):
            g_use[n] = (g_use[n][0], t)
            order.append(n)

        d_use = [None] * 8
        nd = [0]

        def second(p):
            (t_, k0, nk), tgl, vs = p
            w_ = av[:, t_, k0:k0 + nk]
            t = dv.do(lambda e: e.tensor_tensor(w_, w_, gate[:, t_, k0:k0 + nk], ALU.mult), tgl, tg[t_, k0 // 16])
            ab = 6 - 2 * t_
            for k in range(nk):
                g_, ta, n = vs[k]
                q = nd[0] % 8
                nd[0] += 1
                td = ac.do(lambda e, q=q, k=k: e.activation(
                    D[:, q, :], K("ident"), ACT.Copy, scale=av[:, t_, k0 + k:k0 + k + 1]), t, d_use[q], ft)
                first, last = k0 + k == 0, k0 + k == 127
                for half_ in range(2):
                    f = (lambda e, q=q, g_=g_, half_=half_, first=first, last=last: e.matmul(
                        psum[ab + half_][:, :], D[:, q, :], g_[:, 512 * half_:512 * half_ + 512], start=first,
                        stop=last))
                    if half_:
                        tp = pe.do(f, td, ta, free[ab], free[ab + 1])
                    else:
                        pe.quiet(f, td, ta, free[ab], free[ab + 1])
                d_use[q] = tp
                let_go(n, tp)
            return tp

        s_out = sem("s_out")

        def finish(t_, t):
            ab = 6 - 2 * t_
            for half_ in range(2):
                a = slice(512 * half_, 512 * half_ + 512)
                t1 = dv.do(lambda e, a=a, half_=half_: e.tensor_tensor(
                    yN[:, t_, a], yN[:, t_, a], psum[ab + half_][:, :], ALU.add), t, tok["n", False, t_, half_])
                sp.dma(out[128 * t_:128 * t_ + 128, a], yN[:, t_, a], s_out, t1)

        pend = None
        n = 0
        while n < 256:
            t_, k0 = divmod(n, 128)
            while ("idx", t_, k0 // 16) not in tok:
                more_work()
            nk = 1 if n < 4 else 4
            n += nk
            us = [gather("pu", t_, k0 + k) for k in range(nk)]
            vs = [gather("pv", t_, k0 + k) for k in range(nk)]
            for k in range(nk):
                g_, ta, nb = us[k]
                t = dv.do(lambda e, k=k, g_=g_, t_=t_, k0=k0: e.tensor_tensor_reduce(
                    g_, g_, hN[:, t_, :], 1.0, 0.0, ALU.mult, ALU.add, av[:, t_, k0 + k:k0 + k + 1]),
                    ta, tok["n", True, t_, 0], tok["n", True, t_, 1])
                let_go(nb, t)
            if pend is not None:
                tp = second(pend)
                if pend[0][1] + pend[0][2] == 128:
                    finish(pend[0][0], tp)
            tgl = ac.do(lambda e, t_=t_, k0=k0, nk=nk: e.activation(
                av[:, t_, k0:k0 + nk], av[:, t_, k0:k0 + nk], ACT.Gelu_apprx_tanh), t)
            pend = ((t_, k0, nk), tgl, vs)
            more_work()
        finish(1, second(pend))
        dump("idx", idx, tg[1, 7])
        dump("gate", gate, tg[1, 7])
        sp.wait((s_out, 64))

        block = ctx.enter_context(nc.Block())

        @block.tensor
        def _(e):
            pe.run(e)

        @block.vector
        def _(e):
            dv.run(e)

        @block.scalar
        def _(e):
            ac.run(e)

        @block.gpsimd
        def _(e):
            po.run(e)

        @block.sync
        def _(e):
            sp.run(e)


def constants():
    f = np.float32
    k = np.zeros((128, KCN), f)

    def put(n, a):
        k[:, KC[n][0]:KC[n][1]] = a

    put("ident", np.eye(128))
    put("ones", 1.0)
    put("blk", np.kron(np.eye(2), np.ones((64, 64))))
    p = np.zeros((128, 128), f)
    for i in range(64):
        p[2 * i + 1, 2 * i] = -1.0
        p[2 * i, 2 * i + 1] = 1.0
    put("perm1", p)
    p = np.zeros((128, 128), f)
    for i in range(16):
        p[16 + i, i] = -1.0
        p[i, 16 + i] = 1.0
    put("perm2", p)
    p = np.zeros((128, 128), f)
    for o in (0, 64):
        for i in range(8):
            p[o + 8 + i, o + i] = -1.0
            p[o + i, o + 8 + i] = 1.0
    put("perm3", p)
    t = np.arange(256)
    inv = np.power(f(10000.0), (-np.arange(16, dtype=f) / f(16)).astype(f)).astype(f)
    a = np.concatenate([(t // 64).astype(f)[:, None] * inv, (t % 64).astype(f)[:, None] * inv], 1).astype(f)
    a = np.repeat(a.T, 2, axis=0)
    a = np.concatenate([a, a], 0)
    put("cos1", np.cos(a.astype(np.float64)))
    put("sin1", np.sin(a.astype(np.float64)))
    q = np.arange(128)
    for i in range(2):
        k[:, KC["cap"][0] + 256 * i:KC["cap"][0] + 256 * i + 256] = np.where(
            np.arange(256)[None, :] <= (q + 128 * i)[:, None], f(3e38), f(-BIG))
    put("iota", np.arange(16)[None, :])
    for n, rot, base in (("inv2", 32, [0]), ("inv3", 16, [0, 64])):
        half = rot // 2
        v = np.power(f(500000.0), (-np.arange(half, dtype=f) * f(2.0) / f(rot)).astype(f)).astype(f)
        col = np.zeros(128, f)
        for o in base:
            col[o:o + half] = v
            col[o + half:o + rot] = v
        put(n, col[:, None])
    return k


def tiles(w, nc=128):
    kk, n = w.shape
    return np.ascontiguousarray(
        w.reshape(kk // 128, 128, n // nc, nc).transpose(2, 1, 0, 3).reshape(n // nc, 128, -1))


def layout(i):
    def cols(v):
        v = np.asarray(v)
        return v.reshape(-1, 128).T

    mi, w2 = i["w_mix_in"][0], i["w_in_2"][0]
    mi = np.concatenate([mi[:, 0:512], mi[:, 512:576], mi[:, 512:576], mi[:, 576:640], mi[:, 576:640],
                         mi[:, 640:]], 1)
    w2r = np.concatenate([w2[:, 1792:2048], w2[:, 2048:2112], w2[:, 2048:2112], w2[:, 1536:1792],
                          w2[:, 1024:1536], w2[:, 512:1024], w2[:, 0:512], w2[:, 2116:4164]], 1)
    c2 = np.stack([cols(i["c"][0]), cols(i["c_ctx"])], 2).reshape(128, 16)
    cw = i["conv_w"][0].reshape(3, 4, 128).transpose(2, 1, 0).reshape(128, 12)
    vec = {
        "c2": c2, "b_ada": cols(i["b_ada"][0]), "g_ffn1": cols(i["norm_ffn1"][0]),
        "g_mix": cols(i["norm_mix"][0]), "g_ffn2": cols(i["norm_ffn2"][0]), "g_fin": cols(i["final_norm"]),
        "g_n1": cols(i["norm1_g_2"][0]), "g_n2": cols(i["norm2_g_2"][0]),
        "qn": np.tile(i["q_norm"][0], 2)[:, None], "kn": np.tile(i["k_norm"][0], 2)[:, None],
        "conv": cw, "aon": cols(i["attn_out_norm"][0]), "con": cols(i["conv_out_norm"][0]),
        "kvn": cols(i["kv_norm_g_2"][0]), "qn2": cols(i["q_norm_g_2"][0]), "kn2": cols(i["k_norm_g_2"][0]),
    }
    cvec = np.concatenate([vec[n] for n in CV], 1)
    xc = np.concatenate([i["x"][0], i["ctx"][0]], 0).T.reshape(8, 128, 512).transpose(1, 0, 2)
    sk = i["peer_subkeys_2"][0].reshape(16, 128, 128).transpose(2, 0, 1)
    return {
        "cvec": cvec, "kcst": constants(), "xT": xc,
        "vg": i["v_norm_g_2"][0], "vb": i["v_norm_b_2"][0], "bs": i["spatial_b_2"][0].reshape(512),
        "wsp": i["spatial_w_2"][0].transpose(2, 0, 1).reshape(128, 512),
        "pos": i["positions_2"][0],
        "w_ada": tiles(i["w_ada"][0][:, :2048]),
        "w_adaT": i["w_ada"][0].T.reshape(72, 128, 1024), "c": i["c"][0], "cctx": i["c_ctx"], "f1i": tiles(i["w_ffn1_in"][0]), "f1o": tiles(i["w_ffn1_out"][0]),
        "mi": tiles(mi), "mo": tiles(np.concatenate([i["w_mix_out"][0][512:], i["w_mix_out"][0][:512]])),
        "f2i": tiles(i["w_ffn2_in"][0]), "f2o": tiles(i["w_ffn2_out"][0]),
        "w2": tiles(w2r), "w2w": tiles(w2[:, 2112:2116], 4)[0],
        "wuk": tiles(i["w_uk_2"][0]), "wuv": tiles(i["w_uv_2"][0]),
        "wa": tiles(i["w_a_out_2"][0]), "wb": tiles(i["w_b_out_2"][0]), "wo": tiles(i["w_o_2"][0]),
        "wq": tiles(i["peer_wq_2"][0]),
        "sk": sk.reshape(128, 8, 2, 128),
        "pu": i["peer_u_2"][0], "pv": i["peer_v_2"][0],
    }


DBG = {}


def kernel(**inputs):
    import concourse.bacc as _bacc
    from concourse.bass_utils import run_bass_kernel_spmd as _run

    lay = layout({k: np.asarray(v) for k, v in inputs.items()})
    nc = _bacc.Bacc("TRN2", target_bir_lowering=False, num_devices=1)
    arrays, T = {}, {}
    for name, a in lay.items():
        a = np.ascontiguousarray(a)
        arrays[f"in_{name}"] = a
        T[name] = nc.dram_tensor(f"in_{name}", a.shape, mybir.dt.from_np(a.dtype), kind="ExternalInput").ap()
    out = nc.dram_tensor("out_0", (256, 1024), F32, kind="ExternalOutput").ap()
    dbg = {n: nc.dram_tensor("dbg_" + n, s, d, kind="ExternalOutput").ap() for n, (s, d) in DBG.items()}
    program(nc, T, out, dbg)
    r = _run(nc, [arrays], core_ids=[0])
    return r.results[0]["out_0"].reshape(1, 256, 1024)
```

```python
from contextlib import ExitStack

import numpy as np

import concourse.bass as bass
from concourse import mybir

F32 = mybir.dt.float32
U32 = mybir.dt.uint32
I32 = mybir.dt.int32
ALU = mybir.AluOpType
ACT = mybir.ActivationFunctionType
AX = mybir.AxisListType.X
EPS = 1e-6
BIG = 1e30
NS = 8
NSP = 4
AHEAD = 3
FR = mybir.dt.float32r

CV = {}
CVN = 0
for _n, _w in [("c2", 16), ("b_ada", 72), ("g_ffn1", 8), ("g_mix", 8), ("g_ffn2", 8), ("g_fin", 8),
               ("g_n1", 8), ("g_n2", 8), ("qn", 1), ("kn", 1), ("conv", 12), ("aon", 4), ("con", 4),
               ("kvn", 2), ("qn2", 1), ("kn2", 1)]:
    CV[_n] = (CVN, CVN + _w)
    CVN += _w

KC = {}
KCN = 0
for _n, _w in [("ident", 128), ("ones", 128), ("blk", 128), ("perm1", 128), ("perm2", 128), ("perm3", 128),
               ("cos1", 256), ("sin1", 256), ("cap", 512), ("iota", 16), ("inv2", 1), ("inv3", 1)]:
    KC[_n] = (KCN, KCN + _w)
    KCN += _w


class Queue:

    def __init__(self, sem):
        self.sem, self.count, self.items, self.seen = sem, 0, [], {}

    def wait(self, *tokens):
        for t in tokens:
            if t is None:
                continue
            if isinstance(t, list):
                self.wait(*t)
                continue
            sem, value = t
            if self.seen.get(sem.name, 0) >= value:
                continue
            self.seen[sem.name] = value
            self.items.append(lambda e, s=sem, v=value: e.wait_ge(s, v))

    def do(self, fn, *tokens):
        self.wait(*tokens)
        self.count += 1
        self.items.append(lambda e: fn(e).then_inc(self.sem, 1))
        return (self.sem, self.count)

    def quiet(self, fn, *tokens):
        self.wait(*tokens)
        self.items.append(fn)

    def dma(self, dst, src, sem, *tokens):
        self.wait(*tokens)
        self.items.append(lambda e: e.dma_start(dst, src).then_inc(sem, 16))

    def run(self, eng):
        for f in self.items:
            f(eng)


def program(nc, T, out, dbg=None):
    ctx = ExitStack()
    with ctx:
        def sb(name, shape, dt=F32):
            return ctx.enter_context(nc.sbuf_tensor(name, shape, dt))

        def sem(name):
            return ctx.enter_context(nc.semaphore(name))

        pe, dv, ac, po, sp = (Queue(sem("q_" + n)) for n in ("pe", "dve", "act", "pool", "sp"))
        psum = [ctx.enter_context(nc.psum_tensor(f"ps{i}", [128, 512], F32)) for i in range(8)]

        ring = sb("ring", [128, NS, 1024])
        with ExitStack() as once:
            WR, HR, AR = (once.enter_context(nc.sbuf_tensor(n, [128, w], FR))
                          for n, w in (("WR", 8192), ("HR", 8192), ("AR", 11264)))
        WF, HF, AA = (sb(n, [128, w]) for n, w in (("WF", 8192), ("HF", 8192), ("AF", 11264)))
        WS = WR[:, :].rearrange("p (s h c) -> p s h c", s=NSP, h=2)
        Hs = HR[:, :].rearrange("p (h k t) -> p h k t", h=2, k=8)
        XT = sb("XT", [128, 8, 512])
        AB = sb("AB", [128, 6144])
        F = sb("F", [128, 3, 512])
        cv = sb("cv", [128, CVN])
        kc = sb("kc", [128, KCN])
        sqf = sb("sq", [128, 1024])
        Rf = sb("R", [128, 1024])
        M = sb("M", [128, 72, 2])
        Mr = sb("Mr", [128, 72, 2])
        co = sb("co", [128, 8, 2])
        sc2 = sb("sc2", [128, 16])
        m2h = sb("m2h", [128, 8, 2])
        sg = sb("sg", [128, 2, 512])
        small = sb("small", [128, 64])
        bnb = sb("bnb", [128, 12])

        def C(n):
            return cv[:, CV[n][0]:CV[n][1]]

        def K(n):
            return kc[:, KC[n][0]:KC[n][1]]

        free = {i: None for i in range(8)}
        turn = [0, [0, 1, 2, 3, 4, 5]]

        held = set()

        def bank():
            while True:
                b = turn[1][turn[0] % len(turn[1])]
                turn[0] += 1
                if b not in held:
                    return b

        s_w = [sem(f"w{i}") for i in range(NS)]
        s_hi, s_lo = sem("s_hi"), sem("s_lo")
        raw_free = []
        ws_free = []
        hooks = []

        def fetch(src, n_cols, *first):
            n = len(raw_free)
            dst = ring[:, n % NS, 0:n_cols]
            sp.dma(dst, src, s_w[n % NS], raw_free[n - NS] if n >= NS else None, *first)
            raw_free.append(None)
            return dst, (s_w[n % NS], 16 * (n // NS + 1)), n

        def load(src, nk, nc_):
            dst, t, n = fetch(src, nk * nc_)
            return dst.rearrange("p (k c) -> p k c", k=nk), t, n

        before = ([], [])

        def hook_here(hook):
            ac.items.append(lambda e: [f(e) for f in hook[0]])
            dv.items.append(lambda e: [f(e) for f in hook[1]])

        def load_split(src, nk, nc_):
            cols = nk * nc_
            dst, (ws, wv), n = fetch(src, cols)
            m = len(hooks)
            hook = ([], [])
            hooks.append(hook)
            hook_here(hook)
            at = hooks[m - AHEAD] if m >= AHEAD else before
            hi, lo = WS[:, m % NSP, 0, 0:cols], WS[:, m % NSP, 1, 0:cols]
            gone = ws_free[m - NSP] if m >= NSP else None
            at[0].append(lambda e: e.wait_ge(ws, wv))
            if gone:
                at[0].append(lambda e: e.wait_ge(*gone))
            at[0].append(lambda e: e.copy(hi, dst).then_inc(s_hi, 1))
            at[1].append(lambda e: e.wait_ge(s_hi, m + 1))
            at[1].append(lambda e: e.tensor_tensor(lo, dst, hi.bitcast(F32), ALU.subtract).then_inc(s_lo, 1))
            raw_free[n] = (s_lo, m + 1)
            ws_free.append(None)
            return [v.rearrange("p (k c) -> p k c", k=nk) for v in (hi, lo)], (s_lo, m + 1), m

        def mm3(o, l, r, first, last, *tokens, mark=False):
            for i, (a, b_) in enumerate(((0, 0), (0, 1), (1, 0))):
                f = (lambda e, i=i, a=a, b_=b_: e.matmul(o, l[a], r[b_], start=(first and i == 0),
                                                        stop=(last and i == 2)))
                if (last or mark) and i == 2:
                    return pe.do(f, *tokens)
                pe.quiet(f, *tokens)

        def group(o, pairs, *tokens):
            n = len(pairs)
            for i, (l, r) in enumerate(pairs):
                f = (lambda e, l=l, r=r, i=i: e.matmul(o, l, r, start=(i == 0), stop=(i == n - 1)))
                if i == n - 1:
                    t = pe.do(f, *tokens)
                else:
                    pe.quiet(f, *tokens)
            return t

        def group3(o, ls, rs, *tokens):
            n = len(ls)
            for i in range(n):
                t = mm3(o, ls[i], rs[i], i == 0, i == n - 1, *tokens)
            return t

        def parts(dst, src, *tokens):
            t = dv.do(lambda e: e.tensor_copy(dst[0], src), *tokens)
            return dv.do(lambda e: e.tensor_tensor(dst[1], src, dst[0].bitcast(F32), ALU.subtract), t)

        def Hp(k, a, b_):
            return (Hs[:, 0, k, a:b_], Hs[:, 1, k, a:b_])

        s_c = sem("s_c")
        ncst = [0]

        def const(dst, src):
            sp.dma(dst, src, s_c)
            ncst[0] += 16

        s_x = [sem("s_x0"), sem("s_x1")]
        s_sb = sem("s_sb")
        const(cv[:, :], T["cvec"])
        const(K("ones"), T["kcst"][:, KC["ones"][0]:KC["ones"][1]])
        c_in = (s_c, 32)
        sbc = AB[:, 0:2048].rearrange("p (s k) -> p s k", s=2)
        junk = AB[:, 2048:3072]
        for i, n in enumerate(("c", "cctx")):
            sp.dma(sbc[:, i, :], T[n].partition_broadcast(128), s_sb)
        x_in = [(s_x[0], 16), (s_x[1], 16)]
        s_c2 = sem("s_c2")
        s_c3 = sem("s_c3")
        k_in = (s_c3, 32)

        def const_rest():
            sp.dma(kc[:, 0:KC["ones"][0]], T["kcst"][:, 0:KC["ones"][0]], s_c3)
            sp.dma(kc[:, KC["ones"][1]:KCN], T["kcst"][:, KC["ones"][1]:KCN], s_c3)

        def const_last(*ws):
            for i, n in enumerate(("vg", "vb", "bs")):
                sp.dma(bc[:, i, :], T[n].partition_broadcast(128), s_c2, *ws)
            sp.dma(wsp, T["wsp"], s_c2)
            sp.dma(posi, T["pos"].partition_broadcast(128), s_c2)
        bc = AB[:, 4096:5632].rearrange("p (i c) -> p i c", i=3)
        wsp = AB[:, 5632:6144]
        posi = AB[:, 3328:3584].bitcast(I32)
        c2_in = (s_c2, 80)

        t_sc = ac.do(lambda e: e.activation(sc2[:, :], C("c2"), ACT.Silu), c_in)
        t_sb = ac.do(lambda e: e.activation(AB[:, 0:2048], AB[:, 0:2048], ACT.Silu), (s_sb, 32))
        scv = sc2[:, :].rearrange("p (k s) -> p k s", k=8)
        m_tok = {}
        ada = [2 * 8]
        BA = C("b_ada")

        def ada_dve(idx, j):
            i = 8 * idx + j
            n = 2 if idx < 5 else 1
            if idx < 2:
                dst, tw, s_ = fetch(T["w_adaT"][i], 1024)
            else:
                s_ = (i - 16) % 3
                dst = AB[:, 3072 + 1024 * s_:4096 + 1024 * s_]
                tw = (s_a[s_], 16 * ((i - 16) // 3 + 1))
            for q in range(n):
                o = dst if q == n - 1 else junk
                t = dv.do(lambda e, q=q, o=o: e.tensor_tensor_reduce(
                    o, dst, sbc[:, q, :], 1.0, 0.0, ALU.mult, ALU.add, Mr[:, i, q:q + 1]), tw, t_sb,
                    t_junk[0] if o is junk else None)
                if o is junk:
                    t_junk[0] = t
            if idx < 2:
                raw_free[s_] = t
            else:
                ada_fetch(i + 3, t)
            return t

        s_a = [sem(f"a{i}") for i in range(3)]

        def ada_fetch(i, gone):
            if i < 72:
                s_ = (i - 16) % 3
                po.dma(AB[:, 3072 + 1024 * s_:4096 + 1024 * s_], T["w_adaT"][i], s_a[s_], gone)

        def ada_tiles(n):
            for _ in range(n):
                i = ada[0]
                if i == 72:
                    return
                ada[0] += 1
                idx, j = divmod(i, 8)
                t = ada_dve(idx, j)
                if j == 7:
                    n_ = 2 if idx < 5 else 1
                    bb = BA[:, 8 * idx:8 * idx + 8].unsqueeze(2).broadcast_to([128, 8, n_])
                    m_tok[idx] = tok_ada[0] = dv.do(lambda e, idx=idx, n_=n_, bb=bb: e.tensor_tensor(
                        M[:, 8 * idx:8 * idx + 8, 0:n_], Mr[:, 8 * idx:8 * idx + 8, 0:n_], bb, ALU.add), t, c_in)

        tok_ada = [None]
        t_junk = [None]

        def ada_pe(j):
            b = 3 + j
            for q, idx in enumerate((1, 0)):
                w, tw, s_ = load(T["w_ada"][8 * idx + j], 8, 128)
                raw_free[s_] = t = group(psum[b][:, 2 * q:2 * q + 2],
                                         [(w[:, k, :], scv[:, k, :]) for k in range(8)], tw, t_sc, free[b])
            return t

        def ada_add(j, t):
            b = 3 + j
            for q, idx in enumerate((1, 0)):
                free[b] = dv.do(lambda e, q=q, idx=idx: e.tensor_scalar(
                    M[:, 8 * idx + j, :], psum[b][:, 2 * q:2 * q + 2], BA[:, 8 * idx + j:8 * idx + j + 1], None,
                    ALU.add), t, c_in)
            return free[b]

        def ada_pair(j):
            for idx in (1, 0):
                t = ada_dve(idx, j)
                t = dv.do(lambda e, idx=idx: e.tensor_scalar(
                    M[:, 8 * idx + j, :], Mr[:, 8 * idx + j, :], BA[:, 8 * idx + j:8 * idx + j + 1], None,
                    ALU.add), t, c_in)
            return t

        sqt = [None] * 4
        nsq = [0]
        nR = [0]

        kept = set()

        def half(n, N):
            w = N // 256
            while True:
                n[0] += n[0] % w
                q = n[0] % 4
                n[0] += w
                if n is nR or not kept.intersection(range(q, q + w)):
                    return q, w

        class Squares:

            def __init__(self, N, n, lhs="ones"):
                self.N, self.n, self.lhs, self.i = N, n, lhs, 0

            def add(self, src, tok_, scale=1.0, via=None, gone=None):
                N = self.N
                if self.i == 0:
                    self.q, self.w = half(nsq, N)
                    kept.update(range(self.q, self.q + self.w))
                    self.sum = sqf[:, 256 * self.q:256 * (self.q + self.w)]
                    self.ta = ac.do(lambda e: e.activation(self.sum, src, ACT.Square, scale=scale), tok_,
                                    sqt[self.q:self.q + self.w], c_in)
                elif self.i == self.n - 1:
                    q, w = half(nsq, N)
                    via = sqf[:, 256 * q:256 * (q + w)]
                    sc = scale
                    ta = dv.do(lambda e: e.scalar_tensor_tensor(out=via, in0=src, scalar=sc, in1=src, op0=ALU.mult,
                                                                op1=ALU.mult), tok_, sqt[q:q + w], c_in)
                    if not isinstance(sc, float):
                        ta = dv.do(lambda e: e.tensor_scalar(via, via, sc, None, ALU.mult), ta)
                    self.last = (q, w, via, ta)
                else:
                    if via is None:
                        q, w = half(nsq, N)
                        via, gone = sqf[:, 256 * q:256 * (q + w)], sqt[q:q + w]
                    else:
                        q = None
                    ta = ac.do(lambda e: e.activation(via, src, ACT.Square, scale=scale), tok_, gone, c_in)
                    self.ta = po.do(lambda e: e.tensor_tensor(self.sum, self.sum, via, ALU.add), ta, self.ta)
                    if q is not None:
                        sqt[q:q + w] = [self.ta] * w
                self.i += 1
                return self.ta

            def flush(self):
                self.b = b = bank()
                kw = None if self.lhs == "ones" else k_in
                one = self.n == 1
                f = lambda e: e.matmul(psum[b][:, 0:self.N], K(self.lhs), self.sum, start=True, stop=one)
                self.t = pe.do(f, self.ta, free[b], c_in, kw)
                sqt[self.q:self.q + self.w] = [self.t] * self.w
                if not one:
                    q, w, via, ta = self.last
                    self.t = pe.do(lambda e: e.matmul(psum[b][:, 0:self.N], K(self.lhs), via, start=False,
                                                      stop=True), ta)
                    sqt[q:q + w] = [self.t] * w
                kept.difference_update(range(self.q, self.q + self.w))

            def root(self, inv, mul=None):
                assert self.i == self.n
                self.flush()
                q, w = half(nR, self.N)
                r = Rf[:, 256 * q:256 * (q + w)]
                src = psum[self.b][:, 0:self.N]
                if mul is None:
                    t1 = dv.do(lambda e: e.tensor_scalar(r, src, inv, EPS, ALU.mult, ALU.add), self.t)
                    free[self.b] = t1
                else:
                    t1 = dv.do(lambda e: e.scalar_tensor_tensor(out=r, in0=src, scalar=inv, in1=mul[0],
                                                                op0=ALU.mult, op1=ALU.mult), self.t, mul[1])
                    free[self.b] = t1
                    t1 = dv.do(lambda e: e.tensor_scalar(r, r, EPS, None, ALU.add), t1)
                t2 = dv.do(lambda e: e.reciprocal(r, r), t1)
                t3 = ac.do(lambda e: e.activation(r, r, ACT.Sqrt), t2)
                return r, t3

        def rms(srcs, N, inv, toks, lhs="ones"):
            a = Squares(N, len(srcs), lhs)
            for s, t in zip(srcs, toks):
                a.add(s, t)
            return a.root(inv)

        ft = [None, None, None]
        nf = [0]

        def shifted(k, f, ns, td, sh, *ws):
            for s in range(ns):
                c_ = slice(256 * s, 256 * s + 256)
                hi, lo = Hp(k, 256 * s, 256 * s + 256)
                th = ac.do(lambda e, s=s, c_=c_, hi=hi: e.activation(
                    hi, F[:, f, c_], ACT.Identity, bias=sh[:, s:s + 1]), td[s], *ws)
                t = dv.do(lambda e, s=s, c_=c_, hi=hi, lo=lo: e.scalar_tensor_tensor(
                    out=lo, in0=F[:, f, c_], scalar=sh[:, s:s + 1], in1=hi.bitcast(F32), op0=ALU.add,
                    op1=ALU.subtract), th)
            return t

        def modulated(gain, ishift, N, toks, ht_free, root=None):
            for i in (ishift, ishift + 1):
                while i not in m_tok:
                    ada_tiles(1)
            ns = N // 256
            sh, scl = M[:, 8 * ishift:8 * ishift + 8, :], M[:, 8 * ishift + 8:8 * ishift + 16, :]
            tc = dv.do(lambda e: e.scalar_tensor_tensor(
                out=co[:, :, 0:ns], in0=scl[:, :, 0:ns], scalar=1.0,
                in1=C(gain).unsqueeze(2).broadcast_to([128, 8, ns]), op0=ALU.add, op1=ALU.mult),
                m_tok[ishift + 1], m_tok[ishift], c_in)
            r, tr = root() if root else rms([XT[:, k, 0:N] for k in range(8)], N, 1.0 / 1024, toks)
            done, late = [], None

            def rest(k, f, td):
                done.append(shifted(k, f, ns, td, sh[:, k, :], ht_free))
                ft[f] = done[-1]

            for k in range(8):
                f = nf[0] % 3
                nf[0] += 1
                td = []
                for s in range(ns):
                    a = slice(256 * s, 256 * s + 256)
                    td.append(dv.do(lambda e, k=k, s=s, a=a, f=f: e.scalar_tensor_tensor(
                        out=F[:, f, a], in0=XT[:, k, a], scalar=co[:, k, s:s + 1], in1=r[:, a],
                        op0=ALU.mult, op1=ALU.mult), tc, tr, toks[k], ft[f]))
                if late:
                    rest(*late)
                late = (k, f, td)
            rest(*late)
            return done

        def scaled(gain, srcs, N, toks, rr, dst, *ws):
            r, tr = rr
            return [dv.do(lambda e, k=k: e.scalar_tensor_tensor(
                out=dst(k), in0=srcs[k], scalar=C(gain)[:, k:k + 1], in1=r, op0=ALU.mult, op1=ALU.mult),
                tr, toks[k], *ws) for k in range(len(srcs))]

        def plain(gain, srcs, N, toks, inv, dst, *ws, lhs="ones"):
            return scaled(gain, srcs, N, toks, rms(srcs, N, inv, toks, lhs), dst, *ws)

        def scaled_parts(gain, srcs, N, toks, rr, dst, *ws):
            r, tr = rr
            done, late = [], None

            def rest(k, f, td):
                hi, lo = dst(k)
                th = ac.do(lambda e: e.copy(hi, F[:, f, 0:N]), td, *ws)
                ft[f] = dv.do(lambda e: e.tensor_tensor(lo, F[:, f, 0:N], hi.bitcast(F32), ALU.subtract), th)
                done.append(ft[f])

            for k in range(len(srcs)):
                f = nf[0] % 3
                nf[0] += 1
                td = dv.do(lambda e, k=k, f=f: e.scalar_tensor_tensor(
                    out=F[:, f, 0:N], in0=srcs[k], scalar=C(gain)[:, k:k + 1], in1=r, op0=ALU.mult,
                    op1=ALU.mult), tr, toks[k], ft[f])
                if late:
                    rest(*late)
                late = (k, f, td)
            rest(*late)
            return done

        def project(wsrc, rhs, N, toks, *ws):
            b = bank()
            nk = len(rhs)
            at = 0
            while at < nk:
                n = min(8, nk - at)
                (wh, wl), tw, m = load_split(wsrc[:, at * 128:(at + n) * 128], n, 128)
                for k in range(n):
                    i = at + k
                    t = mm3(psum[b][:, 0:N], (wh[:, k, :], wl[:, k, :]), rhs[i], i == 0, i == nk - 1,
                            tw, free[b], toks[i], *ws, mark=(k == n - 1))
                ws_free[m] = t
                at += n
            return b, t

        sgt = [None, None]

        def ffn(win, wout, N, gain, im, toks, act_free, ht_free, more=False, root=None, after=None):
            h = root if isinstance(root, list) else modulated(gain, im, N, toks, ht_free, root)
            rounds = [range(0, 22)] if N == 256 else [range(0, 11), range(11, 22)]
            nj = len(rounds[0])
            Ar = AR[:, :].rearrange("p (h k t) -> p h k t", h=2, k=nj)
            tm, new = None, [None] * 8
            for rn, js in enumerate(rounds):
                at = []
                for i, j in enumerate(js):
                    b1, t1 = project(T[win][j], [Hp(k, 0, N) for k in range(8)], N, h)
                    ada_tiles(1 + (i % 2 == 0) if more else 0)
                    b2, t2 = project(T[win][22 + j], [Hp(k, 0, N) for k in range(8)], N, h)
                    q = j % 2
                    ta = ac.do(lambda e, q=q, b1=b1: e.activation(sg[:, q, 0:N], psum[b1][:, 0:N], ACT.Silu),
                               t1, sgt[q])
                    free[b1] = ta
                    td = dv.do(lambda e, q=q, b2=b2: e.tensor_tensor(
                        sg[:, q, 0:N], sg[:, q, 0:N], psum[b2][:, 0:N], ALU.mult), ta, t2)
                    free[b2] = td
                    sgt[q] = td = parts((Ar[:, 0, i, :], Ar[:, 1, i, :]), sg[:, q, 0:N], td, act_free)
                    at.append(td)
                while im + 2 not in m_tok:
                    ada_tiles(1)
                if tm is None:
                    ns = N // 256
                    tm = dv.do(lambda e: e.tensor_scalar(
                        m2h[:, :, 0:ns], M[:, 8 * im + 16:8 * im + 24, 0:ns], 0.5, None, ALU.mult), m_tok[im + 2])
                for d in range(8):
                    b, t = project(T[wout][d][:, 128 * js[0]:128 * js[0] + 128 * nj],
                                   [(Ar[:, 0, k, :], Ar[:, 1, k, :]) for k in range(nj)], N, at)
                    ada_tiles((2 - rn if d < 6 or rn == 0 else 0) if more else 0)
                    for s in range(N // 256):
                        a = slice(256 * s, 256 * s + 256)
                        td = dv.do(lambda e, d=d, s=s, a=a, b=b: e.scalar_tensor_tensor(
                            out=XT[:, d, a], in0=psum[b][:, a], scalar=m2h[:, d, s:s + 1], in1=XT[:, d, a],
                            op0=ALU.mult, op1=ALU.add), t, tm, new[d])
                    free[b] = td
                    new[d] = td
                    if after and rn == len(rounds) - 1:
                        after(d, td)
                act_free = t
            return new, t

        def copy_out(eng, dst, b, src, *tokens):
            if eng is ac:
                t = ac.do(lambda e: e.copy(dst, src), *tokens)
            else:
                t = dv.do(lambda e: e.tensor_copy(dst, src), *tokens)
            free[b] = t
            return t

        dumps = []

        def dump(name, ap, *toks):
            if dbg is not None and name in dbg:
                dumps.append((dbg[name], ap))
                s = sem("dbg_" + name)
                po.dma(dbg[name], ap, s, *toks)
                for q_ in (dv, ac):
                    q_.wait((s, 16))

        acc = []
        tp = [ada_pe(0)]
        td5 = ada_pair(5)
        for k in range(0, 8, 4):
            sp.dma(XT[:, k:k + 4, :], T["xT"][:, k:k + 4, :], s_x[k // 4])
        tp.append(ada_pe(1))
        a = Squares(512, 8)
        for k in range(8):
            f = k % 3
            ta = a.add(XT[:, k, :], x_in[k // 4], via=F[:, f, :], gone=ft[f])
            ft[f] = ta if k else None
        h1 = [None] * 8
        pend_ = []

        def first_h(j, tm):
            t = dv.do(lambda e: e.scalar_tensor_tensor(
                out=co[:, j, :], in0=M[:, 8 + j, :], scalar=1.0, in1=C("g_ffn1")[:, j:j + 1].broadcast_to([128, 2]),
                op0=ALU.add, op1=ALU.mult), tm)
            f = nf[0] % 3
            nf[0] += 1
            td = []
            for s in range(2):
                c_ = slice(256 * s, 256 * s + 256)
                td.append(dv.do(lambda e, s=s, c_=c_: e.scalar_tensor_tensor(
                    out=F[:, f, c_], in0=XT[:, j, c_], scalar=co[:, j, s:s + 1], in1=r1_[:, c_],
                    op0=ALU.mult, op1=ALU.mult), t, tr1, ft[f]))
            if pend_:
                last_h(*pend_.pop())
            pend_.append((j, f, td))

        def last_h(j, f, td):
            h1[j] = ft[f] = shifted(j, f, 2, td, M[:, j, :])

        td6 = ada_pair(6)
        td7 = ada_pair(7)
        r1_, tr1 = a.root(1.0 / 1024)
        tp += [ada_pe(j) for j in range(2, 5)]
        for j, tm in ((5, td5), (6, td6), (7, td7)):
            first_h(j, tm)
        for j in range(5):
            if j == 4:
                hook_here(before)
            first_h(j, ada_add(j, tp[j]))
        last_h(*pend_.pop())
        const_rest()

        def follow(N, n_acc=1):
            def f(d, td):
                if d == 0:
                    acc[:] = [Squares(N, 8) for _ in range(n_acc)]
                acc[0].add(XT[:, d, 0:N], td)
                if n_acc == 2:
                    acc[1].add(XT[:, d, 0:N], td, scale=C("g_fin")[:, d:d + 1])
            return f

        for i in range(16, 19):
            ada_fetch(i, None)
        x, t_pe = ffn("f1i", "f1o", 512, "g_ffn1", 0, [x_in] * 8, None, None, more=True, root=h1,
                      after=follow(512))
        assert ada[0] == 72
        dump("x1", XT[:, :, :], x)
        h = modulated("g_mix", 3, 512, x, t_pe, root=lambda: acc[0].root(1.0 / 1024))

        todo = []

        def fill(n=1):
            for _ in range(n):
                if todo:
                    todo.pop(0)()

        def together(*gens, each=1):
            gens = list(gens)
            while gens:
                for g in list(gens):
                    try:
                        next(g)
                    except StopIteration:
                        gens.remove(g)
                fill(each)

        turn[1] = [0, 1, 2, 3, 4, 5, 6, 7]
        qT = AA[:, 0:1024].rearrange("p (j t) -> p j t", j=4)
        kT = AA[:, 1024:2048].rearrange("p (j t) -> p j t", j=2)
        vN = AA[:, 2048:2560].rearrange("p (j d) -> p j d", j=4)
        gb = AA[:, 2560:3584].rearrange("p (j t) -> p j t", j=4)
        gc = AA[:, 3584:4608].rearrange("p (j t) -> p j t", j=4)
        pz = AA[:, 4608:4608 + 4 * 258].rearrange("p (j t) -> p j t", j=4)
        cs = AA[:, 5640:6664].rearrange("p (j t) -> p j t", j=4)
        aT = AA[:, 6664:7688].rearrange("p (j t) -> p j t", j=4)
        Pb = AA[:, 8200:10248].rearrange("p (j s) -> p j s", j=4)
        PT = AB[:, 0:2048].rearrange("p (j k q) -> p j k q", j=2, k=2 * 2)

        def MX(k):
            return Hp(k, 256, 512)

        aa_free = t_pe
        tok = {}
        H256 = [Hp(k, 0, 256) for k in range(8)]
        H512 = [Hp(k, 0, 512) for k in range(8)]

        def natural(src, dst, ntok, h):
            (wh, wl), tw, m = load_split(src, 8, 128)
            b = bank()
            for i in range(ntok):
                t = group3(psum[b][:, 128 * i:128 * i + 128],
                           [Hp(k, 128 * i, 128 * i + 128) for k in range(8)],
                           [(wh[:, k, :], wl[:, k, :]) for k in range(8)], tw, free[b], h)
            ws_free[m] = t
            return b, t

        for j in range(4):
            b, t = project(T["mi"][j], H256, 256, h)
            tok["q", j] = copy_out(ac, qT[:, j, :], b, psum[b][:, 0:256], t, aa_free)
        for j in range(2):
            b, t = project(T["mi"][4 + j], H512, 512, h)
            tok["k", j] = copy_out(ac, kT[:, j, :], b, psum[b][:, :], t, aa_free)
        b, t = natural(T["mi"][6], None, 4, h)
        tok["v"] = copy_out(ac, vN.rearrange("p j d -> p (j d)"), b, psum[b][:, :], t, aa_free)
        hx_free = t
        const_last(tok_ada[0])
        tz = po.do(lambda e: e.memset(AA[:, 4608:4608 + 4 * 258], 0.0), aa_free)

        def conv_tile(j, which):
            def f():
                b, t = project(T["mi"][7 + j + 4 * which], H256, 256, h)
                tok["ht"] = t
                if which == 0:
                    tok["gb", j] = copy_out(ac, gb[:, j, :], b, psum[b][:, 0:256], t, aa_free)
                elif which == 1:
                    tok["gc", j] = copy_out(ac, gc[:, j, :], b, psum[b][:, 0:256], t, aa_free)
                else:
                    free[b] = tok["p", j] = dv.do(lambda e: e.tensor_tensor(
                        pz[:, j, 1:257], gc[:, j, :], psum[b][:, 0:256], ALU.mult), t, tok["gc", j], tz)
            return f

        for j in range(4):
            for which in (1, 2, 0):
                todo.append(conv_tile(j, which))

        def rope(X, N, tin, perm, cos, sin, ti, *ws):
            b = bank()
            tmp = sg[:, ti, 0:N]
            if N == 512:
                cos, sin = (v.unsqueeze(1).broadcast_to([128, 2, 256]) for v in (cos, sin))

            def v_(ap):
                return ap if N == 256 else ap.rearrange("p (j t) -> p j t", j=2)

            tp = pe.do(lambda e: e.matmul(psum[b][:, 0:N], K(perm), X, start=True, stop=True), tin, free[b], k_in)
            t1 = dv.do(lambda e: e.tensor_tensor(v_(tmp), v_(psum[b][:, 0:N]), sin, ALU.mult), tp, sgt[ti], *ws)
            free[b] = t1
            t2 = dv.do(lambda e: e.tensor_tensor(v_(X), v_(X), cos, ALU.mult), tp, t1)
            sgt[ti] = dv.do(lambda e: e.tensor_tensor(X, X, tmp, ALU.add), t2)
            return sgt[ti]

        def head_norm(keys_, X, gain, N, inv, lhs, rot, ti, nrot, *ws):
            toks = [tok[k] for k in keys_]
            a = Squares(N, 1, lhs)
            a.add(X, toks)
            yield
            rr = a.root(inv)
            yield
            (t,) = scaled(gain, [X], N, [toks], rr, lambda k: X)
            yield
            t = rope(X[:, 0:nrot], nrot, t, *rot, ti, *ws)
            for k in keys_:
                tok[k] = t

        rot1 = ("perm1", K("cos1"), K("sin1"))

        def qpair(j):
            return head_norm([("q", j), ("q", j + 1)], qT[:, j:j + 2, :].rearrange("p j t -> p (j t)"), "qn", 512,
                             1.0 / 64, "blk", rot1, 0, 512)

        def khead(j):
            return head_norm([("k", j)], kT[:, j, :], "kn", 512, 1.0 / 64, "blk", rot1, 1, 256)

        together(qpair(0), khead(0))
        def softmax_rows(Sap, Pap, n, scale, *toks):
            c = 4 * (n % 8)
            m, nm, su, ri = (small[:, c + i:c + i + 1] for i in range(4))
            t1 = dv.do(lambda e: e.reduce_max(m, Sap, AX), *toks)
            t2 = dv.do(lambda e: e.tensor_scalar(nm, m, -scale, None, ALU.mult), t1)
            t3 = ac.do(lambda e: e.activation(Pap, Sap, ACT.Exp, bias=nm, scale=scale, accum_out=su), t2, *toks)
            t4 = dv.do(lambda e: e.reciprocal(ri, su), t3)
            t5 = dv.do(lambda e: e.tensor_scalar(Pap, Pap, ri, None, ALU.mult), t4)
            return t5, t3

        p_use = [None] * 4
        pt_use = [tok_ada[0]] * 4
        n_sm = [0]

        def attention(items, ready, score, nk, P_, PT_, values, finish):
            state = {}
            npt = PT_.shape[1]

            def front(n):
                hd, i = items[n]
                q = n_sm[0] % 4
                state[n] = (q, score(hd, i, P_[:, q, :], n_sm[0], p_use[q]))
                n_sm[0] += 1

            def back(n):
                hd, i = items[n]
                q, tp = state[n]
                b = bank()
                for k in range(nk):
                    t = pe.do(lambda e, k=k: e.transpose(
                        psum[b][:, 128 * k:128 * k + 128], P_[:, q, 128 * k:128 * k + 128], K("ident")),
                        tp, free[b])
                p_use[q] = t
                state["c", hd, i] = copy_out(
                    ac, PT_[:, hd % npt, :, 128 * i:128 * i + 128], b,
                    psum[b][:, 0:128 * nk].rearrange("p (k q) -> p k q", k=nk), t, pt_use[hd % npt])

            def pv(hd):
                pt_use[hd % npt] = values(hd, [state["c", hd, 0], state["c", hd, 1]])
                finish(hd, pt_use[hd % npt])

            N_ = len(items)
            for n in range(N_ + 3):
                if n < N_:
                    while not ready(*items[n]):
                        yield
                    front(n)
                if 2 <= n < N_ + 2:
                    back(n - 2)
                if n >= 3 and items[n - 3][1] == 1:
                    pv(items[n - 3][0])
                yield

        def score1(hd, i, P_, n, pu):
            o, j, kv = 64 * (hd % 2), hd // 2, hd // 4
            b = bank()
            t = pe.do(lambda e: e.matmul(
                psum[b][:, :], qT[o:o + 64, j, 128 * i:128 * i + 128], kT[o:o + 64, kv, :],
                start=True, stop=True), tok["q", j], tok["k", kv], free[b])
            tp, rd = softmax_rows(psum[b][:, :], P_, n, 0.125, t, pu, aa_free)
            free[b] = rd
            return tp

        bo = [None]

        def values1(hd, ts):
            o, kv = 64 * (hd % 2), hd // 4
            if hd % 2 == 0:
                bo[0] = bank()
                held.add(bo[0])
            b = bo[0]
            return group(psum[b][o:o + 64, 0:256],
                         [(vN[:, k, 64 * kv:64 * kv + 64], PT[:, hd % 2, k, :]) for k in range(4)],
                         ts, tok["v"], free[b])

        def finish1(hd, t):
            if hd % 2:
                b = bo[0]
                held.discard(b)
                tok["a", hd // 2] = copy_out(ac, aT[:, hd // 2, :], b, psum[b][:, 0:256], t)

        cvw = C("conv")

        def conv(j):
            t = dv.do(lambda e: e.tensor_scalar(cs[:, j, :], pz[:, j, 0:256], cvw[:, 3 * j:3 * j + 1], None,
                                                ALU.mult), tok["p", j])
            yield
            for i in (1, 2):
                t = dv.do(lambda e, i=i: e.scalar_tensor_tensor(
                    out=cs[:, j, :], in0=pz[:, j, i:i + 256], scalar=cvw[:, 3 * j + i:3 * j + i + 1],
                    in1=cs[:, j, :], op0=ALU.mult, op1=ALU.add), t)
            yield
            tok["c", j] = dv.do(lambda e: e.tensor_tensor(cs[:, j, :], cs[:, j, :], gb[:, j, :], ALU.mult),
                                t, tok["gb", j])

        def convs():
            for j in range(4):
                while ("gb", j) not in tok:
                    fill(1)
                yield from conv(j)

        normed = []

        def others():
            gens = [qpair(2), khead(1)]
            while gens:
                for g in list(gens):
                    if next(g, g) is g:
                        gens.remove(g)
                yield
            normed.append(True)

        together(attention([(hd, i) for hd in range(8) for i in range(2)], lambda hd, i: hd < 4 or normed,
                           score1, 4, Pb, PT, values1, finish1), others(), convs())
        while todo:
            fill(1)
        a1, a2 = Squares(256, 4), Squares(256, 4)
        for j in range(4):
            a2.add(cs[:, j, :], tok["c", j])
        r2 = a2.root(1.0 / 512)
        for j in range(4):
            a1.add(aT[:, j, :], tok["a", j])
        cb = scaled_parts("con", [cs[:, j, :] for j in range(4)], 256, [tok["c", j] for j in range(4)], r2,
                          lambda k: MX(4 + k), hx_free)
        r1 = a1.root(1.0 / 512)
        ca = scaled_parts("aon", [aT[:, j, :] for j in range(4)], 256, [tok["a", j] for j in range(4)], r1,
                          lambda k: MX(k), hx_free)
        nx = []
        fol = follow(256)
        for d in range(8):
            b, t = project(T["mo"][d], [MX(4 + k) for k in range(4)] + [MX(k) for k in range(4)], 256, cb + ca)
            free[b] = td = dv.do(lambda e, d=d, b=b: e.scalar_tensor_tensor(
                out=XT[:, d, 0:256], in0=psum[b][:, 0:256], scalar=M[:, 40 + d, 0:1], in1=XT[:, d, 0:256],
                op0=ALU.mult, op1=ALU.add), t, m_tok[5])
            nx.append(td)
            fol(d, td)
        dump("x2", XT[:, :, :], nx)
        x, t_pe = ffn("f2i", "f2o", 256, "g_ffn2", 6, nx, t, tok["ht"],
                      root=lambda: acc[0].root(1.0 / 1024), after=follow(256, 2))

        ra = acc[0].root(1.0 / 1024)
        rsq = F[:, 0, 0:256]
        t = dv.do(lambda e: e.tensor_tensor(rsq, ra[0], ra[0], ALU.mult), ra[1], ft[0])
        rb = acc[1].root(1.0 / 1024, (rsq, t))
        ft[0] = t
        xs = [XT[:, k, 0:256] for k in range(8)]
        x = scaled("g_fin", xs, 256, x, ra, lambda k: XT[:, k, 0:256])
        nf[0] = 0
        ft[0] = x[7]
        dump("x3", XT[:, :, :], x)
        h = scaled_parts("g_n1", xs, 256, x, rb, lambda k: Hp(k, 0, 256), t_pe)

        uT = AA[:, 0:1024].rearrange("p (j t) -> p j t", j=4)
        vA = AA[:, 1024:2048].rearrange("p (c d) -> p c d", c=2)
        q2 = AA[:, 2048:3072].rearrange("p (j t) -> p j t", j=4)
        ck = AA[:, 3072:3584].rearrange("p (j t) -> p j t", j=2)
        qi = AA[:, 3584:4096].rearrange("p (j t) -> p j t", j=2)
        ki = AA[:, 4096:4352]
        k2 = AA[:, 4352:4608]
        v2 = AA[:, 4608:4864].rearrange("p (j d) -> p j d", j=2)
        wi = AA[:, 4864:4872].rearrange("p (t h) -> p t h", t=2)
        relu = AA[:, 4872:5384].rearrange("p (j t) -> p j t", j=2)
        scr = AA[:, 5384:5896].rearrange("p (i s) -> p i s", i=2)
        wk = AA[:, 5896:6408].rearrange("p (i s) -> p i s", i=2)
        sel = AA[:, 6408:6920].rearrange("p (i s) -> p i s", i=2)
        mx = AA[:, 7432:7560].rearrange("p (i s) -> p i s", i=2)
        onesr = AA[:, 7560:7816]
        P2 = AA[:, 7816:8840].rearrange("p (i s) -> p i s", i=4)
        PT2 = AB[:, 0:2048].rearrange("p (j k q) -> p j k q", j=4, k=2)
        rt = AB[:, 2048:3328].rearrange("p (j t) -> p j t", j=5)
        ang = AB[:, 3584:3840]
        posf = AB[:, 3840:4096]
        gt = sgx = XT[:, :, 256:512]
        ya_p = [(Hs[:, 0, k, 256:512], Hs[:, 1, k, 256:512]) for k in range(4)]
        yb_p = [(Hs[:, 0, 4 + k, 256:512], Hs[:, 1, 4 + k, 256:512]) for k in range(4)]
        aa_free = t_pe
        st = small[:, 32:48]

        TWO_PI = 2 * np.pi
        C1 = 6.28125
        C2 = float(np.round((TWO_PI - C1) * 2 ** 22) / 2 ** 22)
        C3 = float(np.float32(TWO_PI - C1 - C2))
        MAGIC = 12582912.0
        PI_ = 3.1415925

        def tables():
            t0 = dv.do(lambda e: e.tensor_copy(posf, posi), c2_in)
            for i, inv in enumerate(("inv3", "inv2")):
                o = 2 - 2 * i
                sn, cn, nn = rt[:, o, :], rt[:, o + 1, :], rt[:, 4, :]
                t1 = dv.do(lambda e, inv=inv: e.tensor_scalar(ang, posf, K(inv), None, ALU.mult), t0, c_in)
                t1 = dv.do(lambda e, nn=nn: e.tensor_scalar(nn, ang, 1.0 / TWO_PI, MAGIC, ALU.mult, ALU.add), t1)
                t1 = dv.do(lambda e, nn=nn: e.tensor_scalar(nn, nn, MAGIC, None, ALU.subtract), t1)
                for cc in (C1, C2, C3):
                    t1 = dv.do(lambda e, nn=nn, cc=cc: e.scalar_tensor_tensor(
                        out=ang, in0=nn, scalar=-cc, in1=ang, op0=ALU.mult, op1=ALU.add), t1)
                yield
                t2 = dv.do(lambda e, cn=cn: e.tensor_scalar(cn, ang, np.pi / 2, None, ALU.add), t1)
                t3 = dv.do(lambda e, cn=cn, nn=nn: e.tensor_scalar(nn, cn, PI_, TWO_PI, ALU.is_gt, ALU.mult), t2)
                t3 = dv.do(lambda e, cn=cn, nn=nn: e.tensor_tensor(cn, cn, nn, ALU.subtract), t3)
                t3 = dv.do(lambda e, cn=cn: e.tensor_scalar(cn, cn, -PI_, PI_, ALU.max, ALU.min), t3)
                t4 = dv.do(lambda e, sn=sn: e.tensor_scalar(sn, ang, -PI_, PI_, ALU.max, ALU.min), t1)
                t0 = tok["rt", o] = ac.do(lambda e, o=o: e.activation(
                    rt[:, o:o + 2, :], rt[:, o:o + 2, :], ACT.Sin), t3, t4)
                yield

        def proj2(key, n, dst, func=None, scale=1.0):
            def f():
                b, t = project(T["w2"][n], H256, 256, h)
                tok["ht"] = t
                if func is None:
                    tok[key] = copy_out(ac, dst, b, psum[b][:, 0:256], t, aa_free)
                else:
                    tok[key] = free[b] = ac.do(lambda e: e.activation(dst, psum[b][:, 0:256], func, scale=scale), t, aa_free,
                                               nx[7])
            return f

        def vtile(j):
            def f():
                b, t = natural(T["w2"][9 + j], None, 2, h)
                tok["ht"] = t
                tok["vA", j] = free[b] = ac.do(lambda e: e.activation(
                    vA[:, :, 128 * j:128 * j + 128], psum[b][:, 0:256].rearrange("p (c d) -> p c d", c=2),
                    ACT.Gelu_apprx_tanh), t, aa_free)
            return f

        todo += [proj2(("ck", j), 3 + j, ck[:, j, :]) for j in range(2)]
        todo += [proj2(("q2", j), 5 + j, q2[:, j, :]) for j in range(4)]
        todo += [vtile(j) for j in range(4)]
        todo += [proj2(("u", j), 13 + j, uT[:, j, :], ACT.Gelu_apprx_tanh) for j in range(4)]
        g1 = AA[:, 8840:10888].rearrange("p (j t) -> p j t", j=8)
        todo += [proj2(("g", j), 17 + j, sgx[:, j, :], ACT.Tanh, 0.5) for j in range(8)]
        todo += [proj2(("g", 8 + j), 25 + j, g1[:, j, :], ACT.Tanh, 0.5) for j in range(8)]
        for j in range(2):
            proj2(("qi", j), j, qi[:, j, :])()
        proj2("ki", 2, ki)()
        wp, tw, m = load_split(T["w2w"], 8, 4)
        b = bank()
        for i in range(2):
            t = group3(psum[b][:, 4 * i:4 * i + 4], [Hp(k, 128 * i, 128 * i + 128) for k in range(8)],
                       [(wp[0][:, k, :], wp[1][:, k, :]) for k in range(8)], tw, free[b], h)
        ws_free[m] = t
        tok["wi"] = free[b] = dv.do(lambda e, b=b: e.tensor_scalar(
            wi.rearrange("p t h -> p (t h)"), psum[b][:, 0:8], 0.5, None, ALU.mult), t, aa_free)

        def rope2(key, X, perm, o, ti):
            yield
            tok[key] = rope(X, 256, tok[key], perm, rt[:, o + 1, :], rt[:, o, :], ti, tok["rt", o])

        together(tables())
        together(rope2(("qi", 0), qi[:, 0, :], "perm3", 2, 0), rope2(("qi", 1), qi[:, 1, :], "perm3", 2, 1))
        together(rope2("ki", ki, "perm3", 2, 0))
        t_or = dv.do(lambda e: e.memset(onesr, 1.0), aa_free)

        def choose(i):
            t = None
            for hd in range(4):
                o = 64 * (hd % 2)
                b = bank()
                tp = pe.do(lambda e, b=b, o=o, hd=hd: e.matmul(
                    psum[b][:, 0:256], qi[o:o + 64, hd // 2, 128 * i:128 * i + 128], ki[o:o + 64, :],
                    start=True, stop=True), tok["qi", hd // 2], tok["ki"], free[b])
                ta = free[b] = ac.do(lambda e, b=b, hd=hd: e.activation(
                    relu[:, i, :], psum[b][:, 0:256], ACT.Relu, scale=0.125), tp, t)
                if hd == 0:
                    t = dv.do(lambda e: e.tensor_scalar(scr[:, i, :], relu[:, i, :], wi[:, i, 0:1], None,
                                                        ALU.mult), ta, tok["wi"])
                else:
                    t = dv.do(lambda e, hd=hd: e.scalar_tensor_tensor(
                        out=scr[:, i, :], in0=relu[:, i, :], scalar=wi[:, i, hd:hd + 1], in1=scr[:, i, :],
                        op0=ALU.mult, op1=ALU.add), ta, t)
                yield
            cap = K("cap")[:, 256 * i:256 * i + 256]
            t = dv.do(lambda e: e.tensor_tensor(scr[:, i, :], scr[:, i, :], cap, ALU.min), t)
            src = scr[:, i, :]
            for r in range(8):
                t = dv.do(lambda e, r=r, src=src: e.max(mx[:, i, 8 * r:8 * r + 8], src), t)
                if r < 7:
                    t = dv.do(lambda e, r=r, src=src: e.match_replace(
                        wk[:, i, :], mx[:, i, 8 * r:8 * r + 8], src, -3e38), t)
                    src = wk[:, i, :]
                if r % 2:
                    yield
            th = mx[:, i, 63:64]
            sl, w_ = sel[:, i, :], wk[:, i, :]
            t = dv.do(lambda e: e.tensor_scalar(sl, scr[:, i, :], th, None, ALU.is_gt), t)
            t = dv.do(lambda e: e.reduce_sum(mx[:, i, 0:1], sl, AX), t)
            t = dv.do(lambda e: e.tensor_scalar(mx[:, i, 1:2], mx[:, i, 0:1], -1.0, 64.0, ALU.mult, ALU.add), t)
            t = dv.do(lambda e: e.tensor_scalar(scr[:, i, :], scr[:, i, :], th, None, ALU.is_equal), t)
            t = dv.do(lambda e: e.tensor_tensor_scan(w_, onesr, scr[:, i, :], 0.0, ALU.mult, ALU.add), t, t_or)
            yield
            t = dv.do(lambda e: e.scalar_tensor_tensor(out=w_, in0=w_, scalar=mx[:, i, 1:2], in1=scr[:, i, :],
                                                       op0=ALU.is_le, op1=ALU.mult), t)
            t = dv.do(lambda e: e.tensor_tensor(sl, sl, w_, ALU.add), t)
            t = dv.do(lambda e: e.tensor_scalar(sl, sl, 2 * BIG, -BIG, ALU.mult, ALU.add), t)
            tok["sel", i] = dv.do(lambda e: e.tensor_tensor(sl, sl, cap, ALU.min), t)

        def keys():
            while ("ck", 1) not in tok:
                fill(1)
            cks = [ck[:, j, :] for j in range(2)]
            a = Squares(256, 2)
            for j in range(2):
                a.add(cks[j], tok["ck", j])
            yield
            rr = a.root(1.0 / 256)
            yield
            c1 = scaled("kvn", cks, 256, [tok["ck", j] for j in range(2)], rr, lambda k: cks[k])
            wk_, tw, s = load(T["wuk"][0], 2, 128)
            wv_, tw2, s2 = load(T["wuv"][0], 2, 128)
            yield
            b = bank()
            raw_free[s] = t = group(psum[b][:, 0:256], [(wk_[:, k, :], cks[k]) for k in range(2)], tw, free[b], c1)
            tok["k2"] = copy_out(ac, k2, b, psum[b][:, 0:256], t, aa_free)
            b = bank()
            for i in range(2):
                t = group(psum[b][:, 128 * i:128 * i + 128],
                          [(ck[:, k, 128 * i:128 * i + 128], wv_[:, k, :]) for k in range(2)], tw2, free[b], c1)
            raw_free[s2] = t
            tok["v2"] = copy_out(ac, v2.rearrange("p j d -> p (j d)"), b, psum[b][:, 0:256], t, aa_free)
            yield
            yield from head_norm(["k2"], k2, "kn2", 256, 1.0 / 128, "ones", rot2, 1, 256, tok["rt", 0])

        rot2 = ("perm2", rt[:, 1, :], rt[:, 0, :])

        def q2pair(j):
            while ("q2", j + 1) not in tok:
                fill(1)
            yield from head_norm([("q2", j), ("q2", j + 1)], q2[:, j:j + 2, :].rearrange("p j t -> p (j t)"), "qn2",
                                 512, 1.0 / 128, "ones", rot2, 0, 512, tok["rt", 0])

        together(choose(0), keys())
        together(q2pair(0), q2pair(2))

        S2 = 128 ** -0.5

        def score2(hd, i, P_, n, pu):
            b = bank()
            t = pe.do(lambda e: e.matmul(psum[b][:, 0:256], q2[:, hd, 128 * i:128 * i + 128], k2,
                                         start=True, stop=True), tok["q2", hd], tok["k2"], free[b])
            t = free[b] = dv.do(lambda e: e.scalar_tensor_tensor(
                out=P_, in0=psum[b][:, 0:256], scalar=S2, in1=sel[:, i, :], op0=ALU.mult, op1=ALU.min),
                t, tok["sel", i], pu, aa_free)
            return softmax_rows(P_, P_, n, 1.0, t)[0]

        def values2(hd, ts):
            bo[0] = b = bank()
            return group(psum[b][:, 0:256], [(v2[:, k, :], PT2[:, hd, k, :]) for k in range(2)],
                         ts, tok["v2"], free[b])

        def finish2(hd, t):
            b = bo[0]
            tok["yb", hd] = free[b] = parts(yb_p[hd], psum[b][:, 0:256], t, nx)

        tw_ = po.do(lambda e: e.affine_select(
            wsp.rearrange("p (g t) -> p g t", g=4), wsp.rearrange("p (g t) -> p g t", g=4),
            [[0, 4], [1, 128]], ALU.is_ge, 0.0, base=0, channel_multiplier=-1), c2_in)

        def gated(c):
            while ("u", 3) not in tok:
                fill(1)
            s_ = st[:, 8 * c:8 * c + 8]
            bn = bnb[:, 6 * c:6 * c + 6]
            v = vA[:, c, :]
            t = dv.do(lambda e: e.bn_stats(bn, v), [tok["vA", j] for j in range(4)])
            t = dv.do(lambda e: e.bn_aggr(s_[:, 0:2], bn), t)
            t = dv.do(lambda e: e.tensor_scalar(s_[:, 2:3], s_[:, 1:2], EPS, None, ALU.add), t)
            t = dv.do(lambda e: e.reciprocal(s_[:, 3:4], s_[:, 2:3]), t)
            t = ac.do(lambda e: e.activation(s_[:, 4:5], s_[:, 3:4], ACT.Sqrt), t)
            yield
            t = dv.do(lambda e: e.tensor_scalar(v, v, s_[:, 0:1], s_[:, 4:5], ALU.subtract, ALU.mult), t)
            t = dv.do(lambda e: e.tensor_tensor(v, v, bc[:, 0, :], ALU.mult), t, c2_in)
            t = dv.do(lambda e: e.tensor_tensor(v, v, bc[:, 1, :], ALU.add), t)
            yield
            b = bank()
            for g in range(4):
                tp = pe.do(lambda e, g=g: e.matmul(
                    psum[b][:, 128 * g:128 * g + 128], vA[:, c, 128 * g:128 * g + 128],
                    wsp[:, 128 * g:128 * g + 128], start=True, stop=True), t, tw_, free[b])
            t = free[b] = dv.do(lambda e: e.tensor_tensor(sg[:, c, :], psum[b][:, :], bc[:, 2, :], ALU.add), tp,
                                sgt[0], sgt[1])
            yield
            t = dv.do(lambda e: e.tensor_tensor(
                sg[:, c, :].rearrange("p (g t) -> p g t", g=4), sg[:, c, :].rearrange("p (g t) -> p g t", g=4),
                uT[:, :, 128 * c:128 * c + 128], ALU.mult), t, [tok["u", j] for j in range(4)])
            tok["ya", c] = parts((Hs[:, 0, 0:4, 256 + 128 * c:384 + 128 * c], Hs[:, 1, 0:4, 256 + 128 * c:384 + 128 * c]),
                                 sg[:, c, :].rearrange("p (g t) -> p g t", g=4), t, nx)

        together(choose(1), attention([(hd, i) for i in range(2) for hd in range(4)],
                                      lambda hd, i: ("sel", i) in tok, score2, 2, P2, PT2, values2, finish2),
                 gated(0), gated(1))
        while todo:
            fill(1)

        tya = [[tok["ya", 0], tok["ya", 1]]] * 4
        tyb = [tok["yb", k] for k in range(4)]
        mgp = AR[:, 0:4096].rearrange("p (h j t) -> p h j t", h=2, j=8)
        tm = []
        for d in range(8):
            b1, t1 = project(T["wa"][d], ya_p, 256, tya)
            b2, t2 = project(T["wb"][d], yb_p, 256, tyb)
            f = nf[0] % 3
            nf[0] += 1
            t1 = free[b1] = dv.do(lambda e, d=d, b1=b1, f=f: e.scalar_tensor_tensor(
                out=F[:, f, 0:256], in0=sgx[:, d, :], scalar=1.0, in1=psum[b1][:, 0:256], op0=ALU.add,
                op1=ALU.mult), t1, tok["g", d], ft[f])
            t2 = free[b2] = dv.do(lambda e, d=d, b2=b2, f=f: e.scalar_tensor_tensor(
                out=F[:, f, 256:512], in0=g1[:, d, :], scalar=1.0, in1=psum[b2][:, 0:256], op0=ALU.add,
                op1=ALU.mult), t2, tok["g", 8 + d], ft[f])
            t1 = po.do(lambda e, f=f: e.tensor_tensor(F[:, f, 0:256], F[:, f, 0:256], F[:, f, 256:512], ALU.add),
                       t1, t2)
            hi, lo = mgp[:, 0, d, :], mgp[:, 1, d, :]
            th = ac.do(lambda e, f=f, hi=hi: e.copy(hi, F[:, f, 0:256]), t1, tyb, tya[0], pt_use)
            ft[f] = t1 = po.do(lambda e, f=f, hi=hi, lo=lo: e.tensor_tensor(
                lo, F[:, f, 0:256], hi.bitcast(F32), ALU.subtract), th, t1)
            tm.append(t1)
        x2 = []
        fol = follow(256)
        for d in range(8):
            b, t = project(T["wo"][d], [(mgp[:, 0, k, :], mgp[:, 1, k, :]) for k in range(8)], 256, tm)
            free[b] = td = dv.do(lambda e, d=d, b=b: e.scalar_tensor_tensor(
                out=XT[:, d, 0:256], in0=psum[b][:, 0:256], scalar=0.5, in1=XT[:, d, 0:256], op0=ALU.mult,
                op1=ALU.add), t, x)
            x2.append(td)
            fol(d, td)
        wo_done = t
        dump("h1", XT[:, :, :], x2)

        ht_used = tok["ht"]
        skw = XT[:, :, 256:512].rearrange("p k (a n) -> p k a n", a=2)
        s_k = sem("s_k")
        sp.dma(skw, T["sk"], s_k, tm)
        hN = AA[:, 0:2048].rearrange("p (t d) -> p t d", t=2)
        yN = AA[:, 2048:4096].rearrange("p (t d) -> p t d", t=2)
        hF = AA[:, 4096:6144].rearrange("p (k t) -> p k t", k=8)
        r, tr = acc[0].root(1.0 / 1024)
        Hq = HR[:, 0:4096].rearrange("p (h k t) -> p h k t", h=2, k=8)
        H256 = [(Hq[:, 0, k, :], Hq[:, 1, k, :]) for k in range(8)]
        h, hf = [], []
        for k in range(8):
            hf.append(dv.do(lambda e, k=k: e.scalar_tensor_tensor(
                out=hF[:, k, :], in0=xs[k], scalar=C("g_n2")[:, k:k + 1], in1=r, op0=ALU.mult, op1=ALU.mult),
                tr, x2[k], tyb, tya[0]))
            th = ac.do(lambda e, k=k: e.copy(H256[k][0], hF[:, k, :]), hf[k], ht_used, tm)
            if k:
                h.append(dv.do(lambda e, k=k: e.tensor_tensor(H256[k - 1][1], hF[:, k - 1, :], H256[k - 1][0].bitcast(
                    F32), ALU.subtract), th_before))
            th_before = th
        h.append(dv.do(lambda e: e.tensor_tensor(H256[7][1], hF[:, 7, :], H256[7][0].bitcast(F32), ALU.subtract),
                       th_before))
        turn[1] = [0, 1, 2, 3]
        turn[0] = 0

        def turned(dst, srcs, toks, t_, half):
            def f():
                b = bank()
                for k in range(4):
                    kk = 4 * half + k
                    t = pe.do(lambda e, k=k, kk=kk: e.transpose(
                        psum[b][:, 128 * k:128 * k + 128], srcs[kk][:, 128 * t_:128 * t_ + 128], K("ident")),
                        toks[kk], free[b])
                tok["n", dst is hN, t_, half] = copy_out(
                    ac, dst[:, t_, 512 * half:512 * half + 512], b, psum[b][:, :], t, wo_done)
            return f

        hFs = [hF[:, k, :] for k in range(8)]
        qp = AB[:, 0:4096].rearrange("p (j t) -> p j t", j=16)
        idx = AB[:, 4096:4352].bitcast(U32).rearrange("p (a b) -> p a b", a=2)
        gate = AB[:, 4352:4608].rearrange("p (a b) -> p a b", a=2)
        av = AB[:, 4608:4864].rearrange("p (a b) -> p a b", a=2)
        D = F[:, :, :].rearrange("p a b -> p (a b)")[:, 0:1024].rearrange("p (s c) -> p s c", s=8)
        at = [8192]

        def take(*shape, dt=F32):
            n = int(np.prod(shape))
            a = AA[:, at[0]:at[0] + n]
            at[0] += n
            assert at[0] <= 11264
            if dt is not F32:
                a = a.bitcast(dt)
            return a.rearrange("p (a b) -> p a b", a=shape[0]) if len(shape) == 2 else a

        sub = take(4, 256)
        wk3 = take(128)
        top = take(2, 16)
        topi = take(2, 16, dt=U32)
        topf = take(2, 16)
        cand = take(2, 256)
        best = take(16, 16)
        bpos = take(16, dt=U32)
        ij = take(2, 16, dt=U32)
        ijf = take(2, 16)
        oh = take(512)
        isel = take(2, 16)
        ties = [tm, x2, list(pt_use), tyb]
        tg = {}
        sub_use = [None] * 4
        nsub = [0]

        def queries(hd):
            for j in (2 * hd, 2 * hd + 1):
                b, t = project(T["wq"][j], H256, 256, h)
                tok["qp", j] = copy_out(ac, qp[:, j, :], b, psum[b][:, 0:256], t, ties, c2_in, tya[0])
            tok["wq"] = t

        def route(t_, hd):
            if ("qp", 2 * hd) not in tok:
                queries(hd)
            u = nsub[0] % 4
            nsub[0] += 1
            b = bank()
            for p in range(2):
                j = 2 * hd + p
                tp = pe.do(lambda e, p=p, j=j: e.matmul(
                    psum[b][:, 128 * p:128 * p + 128], qp[:, j, 128 * t_:128 * t_ + 128], skw[:, j // 2, j % 2, :],
                    start=True, stop=True), tok["qp", j], (s_k, 16), free[b])
            ts = copy_out(ac, sub[:, u, :], b, psum[b][:, 0:256], tp, sub_use[u], ties)
            yield
            for p in range(2):
                s_ = sub[:, u, 128 * p:128 * p + 128]
                t = dv.do(lambda e, p=p, s_=s_: e.max(top[:, p, 0:8], s_), ts)
                dv.do(lambda e, p=p, s_=s_: e.max_index(topi[:, p, 0:8], top[:, p, 0:8], s_), t)
                t = dv.do(lambda e, p=p, s_=s_: e.match_replace(wk3, top[:, p, 0:8], s_, -3e38), t)
                t = dv.do(lambda e, p=p: e.max(top[:, p, 8:16], wk3), t)
                sub_use[u] = t = dv.do(lambda e, p=p: e.max_index(topi[:, p, 8:16], top[:, p, 8:16], wk3), t)
            yield
            a = top[:, 0, :].unsqueeze(2).broadcast_to([128, 16, 16])
            c_ = top[:, 1, :].unsqueeze(1).broadcast_to([128, 16, 16])
            cd, c2_, bs_ = cand[:, 0, :], cand[:, 1, :], best[:, 8 * t_ + hd, :]
            t = dv.do(lambda e: e.tensor_tensor(cd.rearrange("p (i j) -> p i j", i=16), a, c_, ALU.add), t)
            t = dv.do(lambda e: e.max(bs_[:, 0:8], cd), t)
            dv.do(lambda e: e.max_index(bpos[:, 0:8], bs_[:, 0:8], cd), t)
            t = dv.do(lambda e: e.match_replace(c2_, bs_[:, 0:8], cd, -3e38), t)
            t = dv.do(lambda e: e.max(bs_[:, 8:16], c2_), t)
            t = dv.do(lambda e: e.max_index(bpos[:, 8:16], bs_[:, 8:16], c2_), t)
            dv.do(lambda e: e.tensor_scalar(ij[:, 0, :], bpos, 4, None, ALU.logical_shift_right), t)
            t = dv.do(lambda e: e.tensor_scalar(ij[:, 1, :], bpos, 15, None, ALU.bitwise_and), t)
            yield
            t = dv.do(lambda e: e.tensor_copy(ijf, ij), t)
            t = dv.do(lambda e: e.tensor_copy(topf, topi), t)
            oh3 = oh.rearrange("p (k i) -> p k i", i=16)
            oh4 = oh.rearrange("p (q k i) -> p q k i", q=2, k=16)
            f3 = ijf.rearrange("p q k -> p (q k)").unsqueeze(2).broadcast_to([128, 32, 16])
            io = K("iota").unsqueeze(1).broadcast_to([128, 32, 16])
            v4 = topf.unsqueeze(2).broadcast_to([128, 2, 16, 16])
            t = dv.do(lambda e: e.tensor_tensor(oh3, f3, io, ALU.is_equal), t)
            t = dv.do(lambda e: e.tensor_tensor(oh4, oh4, v4, ALU.mult), t)
            t = dv.do(lambda e: e.reduce_sum(isel.rearrange("p q k -> p (q k)"), oh3, AX), t)
            t = dv.do(lambda e: e.scalar_tensor_tensor(
                out=isel[:, 0, :], in0=isel[:, 0, :], scalar=128.0, in1=isel[:, 1, :], op0=ALU.mult,
                op1=ALU.add), t)
            tok["idx", t_, hd] = dv.do(lambda e: e.tensor_copy(idx[:, t_, 16 * hd:16 * hd + 16], isel[:, 0, :]), t)
            c = 16 + 4 * (hd % 4)
            nm, su, ri = (small[:, 32 + c + i:33 + c + i] for i in range(3))
            gg = gate[:, t_, 16 * hd:16 * hd + 16]
            t = dv.do(lambda e: e.tensor_scalar(nm, bs_[:, 0:1], -1.0, None, ALU.mult), t)
            t = ac.do(lambda e: e.activation(gg, bs_, ACT.Exp, bias=nm, accum_out=su), t)
            yield
            t = dv.do(lambda e: e.reciprocal(ri, su), t)
            tg[t_, hd] = dv.do(lambda e: e.tensor_scalar(gg, gg, ri, None, ALU.mult), t)

        def run(g):
            for _ in g:
                pass

        queries(0)
        run(route(0, 0))
        for t_ in range(2):
            for half_ in range(2):
                turned(hN, hFs, hf, t_, half_)()
        hf_free = [tok["n", True, 1, 0], tok["n", True, 1, 1]]
        work = [route(t_, hd) for t_ in range(2) for hd in range(8)][1:]

        def more_work():
            while work:
                try:
                    next(work[0])
                    return
                except StopIteration:
                    work.pop(0)

        gbuf = [(AA[:, 6144:7168], ties), (AA[:, 7168:8192], ties),
                (AA[:, 4096:5120], [ties, hf_free, h]), (AA[:, 5120:6144], [ties, hf_free, h])]
        gbuf += [(HF[:, 4096 + 1024 * i:5120 + 1024 * i], [tm, x2]) for i in range(4)]
        gbuf += [(sg[:, :, :].rearrange("p a b -> p (a b)"), [tm, sgt]), (sqf[:, :], [x2, h, tr]), (Rf[:, :], h)]
        NE = len(gbuf)
        gbuf += [(ring[:, i, :], "wq") for i in range(NS)]
        gbuf += [(r_[:, 1024 * i:1024 * i + 1024], "wq") for r_, n in ((WF, 8), (HF, 4)) for i in range(n)]
        NB = len(gbuf)
        s_g = [sem(f"g{i}") for i in range(NB)]
        g_use = {}
        order = list(range(NE))

        def gather(tab, t_, k):
            n = order.pop(0)
            buf, start = gbuf[n]
            cnt, before = g_use.get(n, (0, None))
            po.wait(tok["wq_all"] if start == "wq" else start, before, tok["idx", t_, k // 16])
            po.items.append(lambda e: e.indirect_dma_start(
                buf, None, T[tab], bass.IndirectOffsetOnAxis(ap=idx[:, t_, k:k + 1], axis=0)
            ).then_inc(s_g[n], 16))
            g_use[n] = (cnt + 1, "due")
            return buf, (s_g[n], 16 * (cnt + 1)), n

        def let_go(n, t):
            g_use[n] = (g_use[n][0], t)
            order.append(n)

        d_use = [None] * 8
        nd = [0]

        def second(p):
            (t_, k0, nk), tgl, vs = p
            w_ = av[:, t_, k0:k0 + nk]
            t = dv.do(lambda e: e.tensor_tensor(w_, w_, gate[:, t_, k0:k0 + nk], ALU.mult), tgl, tg[t_, k0 // 16])
            ab = 6 - 2 * t_
            for k in range(nk):
                g_, ta, n = vs[k]
                q = nd[0] % 8
                nd[0] += 1
                td = ac.do(lambda e, q=q, k=k: e.activation(
                    D[:, q, :], K("ident"), ACT.Copy, scale=av[:, t_, k0 + k:k0 + k + 1]), t, d_use[q], ft)
                first, last = k0 + k == 0, k0 + k == 127
                for half_ in range(2):
                    f = (lambda e, q=q, g_=g_, half_=half_, first=first, last=last: e.matmul(
                        psum[ab + half_][:, :], D[:, q, :], g_[:, 512 * half_:512 * half_ + 512], start=first,
                        stop=last))
                    if half_:
                        tp = pe.do(f, td, ta, free[ab], free[ab + 1])
                    else:
                        pe.quiet(f, td, ta, free[ab], free[ab + 1])
                d_use[q] = tp
                let_go(n, tp)
            return tp

        s_out = sem("s_out")

        def finish(t_, t):
            ab = 6 - 2 * t_
            for half_ in range(2):
                a = slice(512 * half_, 512 * half_ + 512)
                t1 = dv.do(lambda e, a=a, half_=half_: e.tensor_tensor(
                    yN[:, t_, a], yN[:, t_, a], psum[ab + half_][:, :], ALU.add), t, tok["n", False, t_, half_])
                sp.dma(out[128 * t_:128 * t_ + 128, a], yN[:, t_, a], s_out, t1)

        def u_gather(t_, k0, nk):
            while ("idx", t_, k0 // 16) not in tok:
                more_work()
            return t_, k0, nk, [gather("pu", t_, k0 + k) for k in range(nk)]

        def u_dot(t_, k0, nk, us):
            for k in range(nk):
                g_, ta, nb = us[k]
                t = dv.do(lambda e, k=k, g_=g_: e.tensor_tensor_reduce(
                    g_, g_, hN[:, t_, :], 1.0, 0.0, ALU.mult, ALU.add, av[:, t_, k0 + k:k0 + k + 1]),
                    ta, tok["n", True, t_, 0], tok["n", True, t_, 1])
                let_go(nb, t)
            return t

        def u_gelu(t_, k0, nk, t):
            return ac.do(lambda e: e.activation(av[:, t_, k0:k0 + nk], av[:, t_, k0:k0 + nk],
                                                ACT.Gelu_apprx_tanh), t)

        ahead, before_ = {}, None
        for hd in range(1, 8):
            queries(hd)
            k0 = 4 * (hd - 1)
            g_ = u_gather(0, k0, 4)
            if before_:
                ahead[before_[1]] = u_gelu(*before_[:3], u_dot(*before_))
            before_ = g_
            more_work()
        ahead[before_[1]] = u_gelu(*before_[:3], u_dot(*before_))
        tok["wq_all"] = [tok["wq"], (s_lo, len(hooks)), (s_hi, len(hooks))]
        order[:] = list(range(NE, NB)) + order
        pend = None
        for n in range(0, 256, 4):
            t_, k0 = divmod(n, 128)
            if n not in ahead:
                us = u_gather(t_, k0, 4)
            vs = [gather("pv", t_, k0 + k) for k in range(4)]
            if n not in ahead:
                tu = u_dot(*us)
            if pend is not None:
                tp = second(pend)
                if pend[0][1] + pend[0][2] == 128:
                    finish(pend[0][0], tp)
            pend = ((t_, k0, 4), ahead[n] if n in ahead else u_gelu(t_, k0, 4, tu), vs)
            if n == 24:
                for i in range(4):
                    turned(yN, xs, x2, i // 2, i % 2)()
            more_work()
        finish(1, second(pend))
        dump("idx", idx, tg[1, 7])
        dump("gate", gate, tg[1, 7])
        sp.wait((s_out, 64))

        block = ctx.enter_context(nc.Block())

        @block.tensor
        def _(e):
            pe.run(e)

        @block.vector
        def _(e):
            dv.run(e)

        @block.scalar
        def _(e):
            ac.run(e)

        @block.gpsimd
        def _(e):
            po.run(e)

        @block.sync
        def _(e):
            sp.run(e)


def constants():
    f = np.float32
    k = np.zeros((128, KCN), f)

    def put(n, a):
        k[:, KC[n][0]:KC[n][1]] = a

    put("ident", np.eye(128))
    put("ones", 1.0)
    put("blk", np.kron(np.eye(2), np.ones((64, 64))))
    p = np.zeros((128, 128), f)
    for i in range(64):
        p[2 * i + 1, 2 * i] = -1.0
        p[2 * i, 2 * i + 1] = 1.0
    put("perm1", p)
    p = np.zeros((128, 128), f)
    for i in range(16):
        p[16 + i, i] = -1.0
        p[i, 16 + i] = 1.0
    put("perm2", p)
    p = np.zeros((128, 128), f)
    for o in (0, 64):
        for i in range(8):
            p[o + 8 + i, o + i] = -1.0
            p[o + i, o + 8 + i] = 1.0
    put("perm3", p)
    t = np.arange(256)
    inv = np.power(f(10000.0), (-np.arange(16, dtype=f) / f(16)).astype(f)).astype(f)
    a = np.concatenate([(t // 64).astype(f)[:, None] * inv, (t % 64).astype(f)[:, None] * inv], 1).astype(f)
    a = np.repeat(a.T, 2, axis=0)
    a = np.concatenate([a, a], 0)
    put("cos1", np.cos(a.astype(np.float64)))
    put("sin1", np.sin(a.astype(np.float64)))
    q = np.arange(128)
    for i in range(2):
        k[:, KC["cap"][0] + 256 * i:KC["cap"][0] + 256 * i + 256] = np.where(
            np.arange(256)[None, :] <= (q + 128 * i)[:, None], f(3e38), f(-BIG))
    put("iota", np.arange(16)[None, :])
    for n, rot, base in (("inv2", 32, [0]), ("inv3", 16, [0, 64])):
        half = rot // 2
        v = np.power(f(500000.0), (-np.arange(half, dtype=f) * f(2.0) / f(rot)).astype(f)).astype(f)
        col = np.zeros(128, f)
        for o in base:
            col[o:o + half] = v
            col[o + half:o + rot] = v
        put(n, col[:, None])
    return k


def tiles(w, nc=128):
    kk, n = w.shape
    return np.ascontiguousarray(
        w.reshape(kk // 128, 128, n // nc, nc).transpose(2, 1, 0, 3).reshape(n // nc, 128, -1))


def layout(i):
    def cols(v):
        v = np.asarray(v)
        return v.reshape(-1, 128).T

    mi, w2 = i["w_mix_in"][0], i["w_in_2"][0]
    mi = np.concatenate([mi[:, 0:512], mi[:, 512:576], mi[:, 512:576], mi[:, 576:640], mi[:, 576:640],
                         mi[:, 640:]], 1)
    w2r = np.concatenate([w2[:, 1792:2048], w2[:, 2048:2112], w2[:, 2048:2112], w2[:, 1536:1792],
                          w2[:, 1024:1536], w2[:, 512:1024], w2[:, 0:512], w2[:, 2116:4164]], 1)
    c2 = np.stack([cols(i["c"][0]), cols(i["c_ctx"])], 2).reshape(128, 16)
    cw = i["conv_w"][0].reshape(3, 4, 128).transpose(2, 1, 0).reshape(128, 12)
    vec = {
        "c2": c2, "b_ada": cols(i["b_ada"][0]), "g_ffn1": cols(i["norm_ffn1"][0]),
        "g_mix": cols(i["norm_mix"][0]), "g_ffn2": cols(i["norm_ffn2"][0]), "g_fin": cols(i["final_norm"]),
        "g_n1": cols(i["norm1_g_2"][0]), "g_n2": cols(i["norm2_g_2"][0]),
        "qn": np.tile(i["q_norm"][0], 2)[:, None], "kn": np.tile(i["k_norm"][0], 2)[:, None],
        "conv": cw, "aon": cols(i["attn_out_norm"][0]), "con": cols(i["conv_out_norm"][0]),
        "kvn": cols(i["kv_norm_g_2"][0]), "qn2": cols(i["q_norm_g_2"][0]), "kn2": cols(i["k_norm_g_2"][0]),
    }
    cvec = np.concatenate([vec[n] for n in CV], 1)
    xc = np.concatenate([i["x"][0], i["ctx"][0]], 0).T.reshape(8, 128, 512).transpose(1, 0, 2)
    sk = i["peer_subkeys_2"][0].reshape(16, 128, 128).transpose(2, 0, 1)
    return {
        "cvec": cvec, "kcst": constants(), "xT": xc,
        "vg": i["v_norm_g_2"][0], "vb": i["v_norm_b_2"][0], "bs": i["spatial_b_2"][0].reshape(512),
        "wsp": i["spatial_w_2"][0].transpose(2, 0, 1).reshape(128, 512),
        "pos": i["positions_2"][0],
        "w_ada": tiles(i["w_ada"][0][:, :2048]),
        "w_adaT": i["w_ada"][0].T.reshape(72, 128, 1024), "c": i["c"][0], "cctx": i["c_ctx"], "f1i": tiles(i["w_ffn1_in"][0]), "f1o": tiles(i["w_ffn1_out"][0]),
        "mi": tiles(mi), "mo": tiles(np.concatenate([i["w_mix_out"][0][512:], i["w_mix_out"][0][:512]])),
        "f2i": tiles(i["w_ffn2_in"][0]), "f2o": tiles(i["w_ffn2_out"][0]),
        "w2": tiles(w2r), "w2w": tiles(w2[:, 2112:2116], 4)[0],
        "wuk": tiles(i["w_uk_2"][0]), "wuv": tiles(i["w_uv_2"][0]),
        "wa": tiles(i["w_a_out_2"][0]), "wb": tiles(i["w_b_out_2"][0]), "wo": tiles(i["w_o_2"][0]),
        "wq": tiles(i["peer_wq_2"][0]),
        "sk": sk.reshape(128, 8, 2, 128),
        "pu": i["peer_u_2"][0], "pv": i["peer_v_2"][0],
    }


DBG = {}


def kernel(**inputs):
    import concourse.bacc as _bacc
    from concourse.bass_utils import run_bass_kernel_spmd as _run

    lay = layout({k: np.asarray(v) for k, v in inputs.items()})
    nc = _bacc.Bacc("TRN2", target_bir_lowering=False, num_devices=1)
    arrays, T = {}, {}
    for name, a in lay.items():
        a = np.ascontiguousarray(a)
        arrays[f"in_{name}"] = a
        T[name] = nc.dram_tensor(f"in_{name}", a.shape, mybir.dt.from_np(a.dtype), kind="ExternalInput").ap()
    out = nc.dram_tensor("out_0", (256, 1024), F32, kind="ExternalOutput").ap()
    dbg = {n: nc.dram_tensor("dbg_" + n, s, d, kind="ExternalOutput").ap() for n, (s, d) in DBG.items()}
    program(nc, T, out, dbg)
    r = _run(nc, [arrays], core_ids=[0])
    return r.results[0]["out_0"].reshape(1, 256, 1024)
```
